# Optimizing a Trainium2 kernel written in Bass

```python
import math
import jax, jax.numpy as jnp
from jax import lax
import numpy as np

D_MODEL = 2048
BATCH = 1
SEQ = 256
DEPTH = 2
DEC_BATCH = 8
DEC_SEQ = 4
PAST_LEN = 1024
PAGE_SIZE = 128

N_META = 16
N_A_LAYERS = DEPTH // 2
N_B_LAYERS = DEPTH - N_A_LAYERS
EPS = 1e-6

D_INNER = 2 * D_MODEL
SSM_HEAD_DIM = 64
SSM_HEADS = D_INNER // SSM_HEAD_DIM
SSM_GROUPS = 8
SSM_HPG = SSM_HEADS // SSM_GROUPS
SSM_STATE = 128
CONV_WIDTH = 4
GN = SSM_GROUPS * SSM_STATE
CONV_DIM = D_INNER + 2 * GN
A_IN_DIM = D_INNER + CONV_DIM + SSM_HEADS
SSD_CHUNK = 128

MLA_HEADS = 16
Q_LORA = 512
KV_LORA = 512
NOPE_DIM = 128
ROPE_DIM = 64
QK_DIM = NOPE_DIM + ROPE_DIM
V_DIM = 128
MLA_WIDTH = MLA_HEADS * V_DIM
B_IN_DIM = Q_LORA + MLA_WIDTH
KV_ROW = KV_LORA + ROPE_DIM
ROPE_BASE = 10000.0
Q_BLOCK = 128

kernel_name = "hybrid_ssd_yoco_mla_step"

F32 = jnp.float32

def rmsnorm(x, g):
    xf = x.astype(F32)
    y = xf * lax.rsqrt(jnp.mean(xf * xf, -1, keepdims=True) + EPS)
    return (y * g.astype(F32)).astype(x.dtype)

def rope_cos_sin(pos):
    inv = 1.0 / (ROPE_BASE ** (jnp.arange(0, ROPE_DIM, 2, dtype=F32) / ROPE_DIM))
    f = pos.astype(F32)[:, None] * inv[None, :]
    emb = jnp.concatenate([f, f], -1)
    return jnp.cos(emb), jnp.sin(emb)

def apply_rope(x, cos, sin):
    xf = x.astype(F32)
    h = ROPE_DIM // 2
    rot = jnp.concatenate([-xf[..., h:], xf[..., :h]], -1)
    return (xf * cos + rot * sin).astype(x.dtype)

def causal_conv(xbc, prev, w, b):
    L = xbc.shape[1]
    full = jnp.concatenate([prev.astype(xbc.dtype), xbc], axis=1)
    out = b + full[:, 0:L] * w[0]
    for k in range(1, CONV_WIDTH):
        out = out + full[:, k:k + L] * w[k]
    return jax.nn.silu(out), full[:, L:]

def ssd_chunk_scan(x, dt, A, Bm, Cm, s0, chunk):
    bt, L = x.shape[:2]
    nc = L // chunk
    G, E, P, N = SSM_GROUPS, SSM_HPG, SSM_HEAD_DIM, SSM_STATE

    def to_chunks(a, tail):
        return a.astype(F32).reshape((bt, nc, chunk) + tail).swapaxes(0, 1)

    xc = to_chunks(x, (G, E, P))
    dtc = to_chunks(dt, (G, E))
    Bc = to_chunks(Bm, (G, N))
    Cc = to_chunks(Cm, (G, N))
    Ag = A.reshape(G, E)
    causal = jnp.tril(jnp.ones((chunk, chunk), bool))[None, :, :, None, None]

    def step(s, inp):
        xk, dtk, Bk, Ck = inp
        cum = jnp.cumsum(dtk * Ag, axis=1)
        seg = cum[:, :, None] - cum[:, None, :]
        decay = jnp.exp(jnp.where(causal, seg, -jnp.inf))
        cb = jnp.einsum('bign,bjgn->bijg', Ck, Bk)
        xdt = xk * dtk[..., None]
        y = jnp.einsum('bijge,bjgep->bigep', decay * cb[..., None], xdt)
        y = y + jnp.einsum('bign,bgepn->bigep', Ck, s) * jnp.exp(cum)[..., None]
        last = cum[:, -1]
        w_end = jnp.exp(last[:, None] - cum)
        s_new = s * jnp.exp(last)[..., None, None] + jnp.einsum('bjge,bjgep,bjgn->bgepn', w_end, xdt, Bk)
        return s_new, y

    s_fin, ys = lax.scan(step, s0.astype(F32).reshape(bt, G, E, P, N), (xc, dtc, Bc, Cc))
    y = ys.swapaxes(0, 1).reshape(bt, L, SSM_HEADS, P)
    return y, s_fin.reshape(bt, SSM_HEADS, P, N)

def mamba_layer(x, conv_prev, s_prev, norm_g, w_in, conv_w, conv_b, dt_bias, A_log, D_skip, gate_norm, w_out, segments):
    bt, L = x.shape[:2]
    h = rmsnorm(x, norm_g)
    proj = h @ w_in
    z = proj[..., :D_INNER]
    xbc = proj[..., D_INNER:D_INNER + CONV_DIM]
    dt_raw = proj[..., D_INNER + CONV_DIM:]
    xbc, conv_new = causal_conv(xbc, conv_prev, conv_w, conv_b)
    xs = xbc[..., :D_INNER].reshape(bt, L, SSM_HEADS, SSM_HEAD_DIM)
    Bm = xbc[..., D_INNER:D_INNER + GN].reshape(bt, L, SSM_GROUPS, SSM_STATE)
    Cm = xbc[..., D_INNER + GN:].reshape(bt, L, SSM_GROUPS, SSM_STATE)
    dt = jax.nn.softplus(dt_raw.astype(F32) + dt_bias.astype(F32))
    A = -jnp.exp(A_log.astype(F32))
    s = s_prev.astype(F32)
    ys = []
    start = 0
    for length, chunk in segments:
        sl = slice(start, start + length)
        y_seg, s = ssd_chunk_scan(xs[:, sl], dt[:, sl], A, Bm[:, sl], Cm[:, sl], s, chunk)
        ys.append(y_seg)
        start += length
    y = jnp.concatenate(ys, axis=1) if len(ys) > 1 else ys[0]
    y = y + xs.astype(F32) * D_skip.astype(F32)[:, None]
    y = y.reshape(bt, L, D_INNER) * jax.nn.silu(z.astype(F32))
    yg = y.reshape(bt, L, SSM_GROUPS, D_INNER // SSM_GROUPS)
    yg = yg * lax.rsqrt(jnp.mean(yg * yg, -1, keepdims=True) + EPS)
    y = (yg.reshape(bt, L, D_INNER) * gate_norm.astype(F32)).astype(x.dtype)
    return x + y @ w_out, conv_new, s.astype(s_prev.dtype)

def mla_kv_side(x, kv_norm, w_kv_a, kv_a_norm, cos, sin):
    a = rmsnorm(x, kv_norm) @ w_kv_a
    c = rmsnorm(a[..., :KV_LORA], kv_a_norm)
    kr = apply_rope(a[..., KV_LORA:], cos, sin)
    return jnp.concatenate([c, kr], -1)

def key_inv_rms(rows, w_uk):
    rf = rows.astype(F32)
    kn = jnp.einsum('...kl,lhd->...khd', rf[..., :KV_LORA], w_uk.astype(F32))
    ss = jnp.sum(kn * kn, -1) + jnp.sum(rf[..., KV_LORA:] ** 2, -1)[..., None]
    return lax.rsqrt(ss / QK_DIM + EPS)

def past_key_inv_rms(cache_kv, page_table, w_uk):
    past = page_table.shape[1] * PAGE_SIZE
    return lax.map(lambda pages: key_inv_rms(cache_kv[pages].reshape(past, KV_ROW), w_uk), page_table)

def mla_query(x, norm_g, w_in, q_a_norm, w_q, q_norm, k_norm, cos, sin):
    proj = rmsnorm(x, norm_g) @ w_in
    qa = rmsnorm(proj[..., :Q_LORA], q_a_norm)
    gate = proj[..., Q_LORA:]
    q = (qa @ w_q).reshape(x.shape[:2] + (MLA_HEADS, QK_DIM))
    q = jnp.concatenate([q[..., :NOPE_DIM], apply_rope(q[..., NOPE_DIM:], cos[:, None], sin[:, None])], -1)
    qf = q.astype(F32)
    qf = qf * lax.rsqrt(jnp.mean(qf * qf, -1, keepdims=True) + EPS)
    qf = qf * (q_norm.astype(F32) * k_norm.astype(F32) / math.sqrt(QK_DIM))
    return qf.astype(x.dtype), gate

def mla_attend(q_eff, rows, r, mask, w_uk, w_uv):
    q_lat = jnp.einsum('...qhd,lhd->...qhl', q_eff[..., :NOPE_DIM], w_uk)
    s = (jnp.einsum('...qhl,...kl->...hqk', q_lat, rows[..., :KV_LORA])
         + jnp.einsum('...qhd,...kd->...hqk', q_eff[..., NOPE_DIM:], rows[..., KV_LORA:])).astype(F32)
    s = s * jnp.swapaxes(r, -1, -2)[..., :, None, :]
    s = jnp.where(mask, s, -jnp.inf)
    p = jax.nn.softmax(s, axis=-1).astype(rows.dtype)
    o_lat = jnp.einsum('...hqk,...kl->...qhl', p, rows[..., :KV_LORA])
    return jnp.einsum('...qhl,lhd->...qhd', o_lat, w_uv)

def mla_prompt_attention(q_eff, rows, r, w_uk, w_uv):
    bt, T = q_eff.shape[:2]
    nb = -(-T // Q_BLOCK)
    pad = nb * Q_BLOCK - T
    qp = jnp.pad(q_eff, ((0, 0), (0, pad), (0, 0), (0, 0)))
    qb = qp.reshape(bt, nb, Q_BLOCK, MLA_HEADS, QK_DIM).swapaxes(0, 1)
    starts = jnp.arange(nb) * Q_BLOCK
    kpos = jnp.arange(T)

    def block(args):
        qblk, st = args
        qpos = st + jnp.arange(Q_BLOCK)
        mask = kpos[None, :] <= qpos[:, None]
        return mla_attend(qblk, rows, r, mask, w_uk, w_uv)

    o = lax.map(block, (qb, starts))
    return o.swapaxes(0, 1).reshape(bt, nb * Q_BLOCK, MLA_HEADS, V_DIM)[:, :T]

def mla_sample_attention(q_eff, new_rows, new_r, past_r, cache_kv, page_table, w_uk, w_uv):
    S = q_eff.shape[1]
    past = page_table.shape[1] * PAGE_SIZE
    kidx = jnp.arange(past + S)
    qidx = past + jnp.arange(S)
    mask = kidx[None, :] <= qidx[:, None]

    def one(args):
        q, nrow, nr, pr, pages = args
        prow = cache_kv[pages].reshape(past, KV_ROW).astype(nrow.dtype)
        rows = jnp.concatenate([prow, nrow], 0)
        rr = jnp.concatenate([pr, nr], 0)
        return mla_attend(q, rows, rr, mask, w_uk, w_uv)

    return lax.map(one, (q_eff, new_rows, new_r, past_r, page_table))

def mla_out(x, o, gate, w_out):
    o = o.reshape(x.shape[:2] + (MLA_WIDTH,)) * jax.nn.silu(gate)
    return x + o @ w_out

def setup_inputs(seed: int = 0) -> dict:
    key = jax.random.key(seed)
    k = iter(jax.random.split(key, 40))

    def nrm(shape, scale):
        return jax.random.normal(next(k), shape, F32) * scale

    def gain(shape):
        return 1.0 + nrm(shape, 0.02)

    n_pages = PAST_LEN // PAGE_SIZE
    n_pool = (DEC_BATCH * n_pages * 5) // 4
    page_table = jax.random.permutation(next(k), n_pool)[:DEC_BATCH * n_pages].reshape(DEC_BATCH, n_pages).astype(jnp.int32)
    u = jax.random.uniform(next(k), (N_A_LAYERS, SSM_HEADS), F32)
    dt0 = jnp.exp(u * (math.log(0.1) - math.log(1e-3)) + math.log(1e-3))
    a_dt_bias = dt0 + jnp.log(-jnp.expm1(-dt0))
    a_A_log = jnp.log(jax.random.uniform(next(k), (N_A_LAYERS, SSM_HEADS), F32, 1.0, 16.0))
    return {
        "x_prompt": nrm((BATCH, SEQ, D_MODEL), 1.0),
        "x_sample": nrm((DEC_BATCH, DEC_SEQ, D_MODEL), 1.0),
        "state_ssm": nrm((N_A_LAYERS, DEC_BATCH, SSM_HEADS, SSM_HEAD_DIM, SSM_STATE), 0.1),
        "state_conv": nrm((N_A_LAYERS, DEC_BATCH, CONV_WIDTH - 1, CONV_DIM), 1.0),
        "cache_kv": nrm((n_pool, PAGE_SIZE, KV_ROW), 1.0),
        "page_table": page_table,
        "meta_tokens": nrm((N_META, D_MODEL), 1.0),
        "a_norm": gain((N_A_LAYERS, D_MODEL)),
        "a_w_in": nrm((N_A_LAYERS, D_MODEL, A_IN_DIM), D_MODEL ** -0.5),
        "a_conv_w": nrm((N_A_LAYERS, CONV_WIDTH, CONV_DIM), 0.5),
        "a_conv_b": nrm((N_A_LAYERS, CONV_DIM), 0.02),
        "a_dt_bias": a_dt_bias,
        "a_A_log": a_A_log,
        "a_D": gain((N_A_LAYERS, SSM_HEADS)),
        "a_gate_norm": gain((N_A_LAYERS, D_INNER)),
        "a_w_out": nrm((N_A_LAYERS, D_INNER, D_MODEL), D_INNER ** -0.5),
        "kv_norm": gain((D_MODEL,)),
        "w_kv_a": nrm((D_MODEL, KV_ROW), D_MODEL ** -0.5),
        "kv_a_norm": gain((KV_LORA,)),
        "w_uk": nrm((KV_LORA, MLA_HEADS, NOPE_DIM), KV_LORA ** -0.5),
        "w_uv": nrm((KV_LORA, MLA_HEADS, V_DIM), KV_LORA ** -0.5),
        "k_norm": gain((QK_DIM,)),
        "b_norm": gain((N_B_LAYERS, D_MODEL)),
        "b_w_in": nrm((N_B_LAYERS, D_MODEL, B_IN_DIM), D_MODEL ** -0.5),
        "b_q_a_norm": gain((N_B_LAYERS, Q_LORA)),
        "b_w_q": nrm((N_B_LAYERS, Q_LORA, MLA_HEADS * QK_DIM), Q_LORA ** -0.5),
        "b_q_norm": gain((N_B_LAYERS, QK_DIM)),
        "b_w_out": nrm((N_B_LAYERS, MLA_WIDTH, D_MODEL), MLA_WIDTH ** -0.5),
    }

def reference(x_prompt, x_sample, state_ssm, state_conv, cache_kv, page_table, meta_tokens,
              a_norm, a_w_in, a_conv_w, a_conv_b, a_dt_bias, a_A_log, a_D, a_gate_norm, a_w_out,
              kv_norm, w_kv_a, kv_a_norm, w_uk, w_uv, k_norm,
              b_norm, b_w_in, b_q_a_norm, b_w_q, b_q_norm, b_w_out):
    bt, L = x_prompt.shape[:2]
    T = L + N_META
    S = x_sample.shape[1]
    past = page_table.shape[1] * PAGE_SIZE
    xp = jnp.concatenate([jnp.broadcast_to(meta_tokens.astype(x_prompt.dtype)[None], (bt, N_META, D_MODEL)), x_prompt], 1)
    xs = x_sample
    segs_p = ((N_META, N_META), (L, SSD_CHUNK))
    segs_s = ((S, S),)
    conv0 = jnp.zeros((bt, CONV_WIDTH - 1, CONV_DIM), xp.dtype)
    ssm0 = jnp.zeros((bt, SSM_HEADS, SSM_HEAD_DIM, SSM_STATE), F32)
    ssm_p, conv_p, ssm_s, conv_s = [], [], [], []
    for i in range(N_A_LAYERS):
        w = (a_norm[i], a_w_in[i], a_conv_w[i], a_conv_b[i], a_dt_bias[i], a_A_log[i], a_D[i], a_gate_norm[i], a_w_out[i])
        xp, cp, sp = mamba_layer(xp, conv0, ssm0, *w, segs_p)
        xs, cs, ss = mamba_layer(xs, state_conv[i], state_ssm[i], *w, segs_s)
        ssm_p.append(sp)
        conv_p.append(cp)
        ssm_s.append(ss)
        conv_s.append(cs)

    cos_p, sin_p = rope_cos_sin(jnp.arange(T))
    cos_s, sin_s = rope_cos_sin(past + jnp.arange(S))
    kv_p = mla_kv_side(xp, kv_norm, w_kv_a, kv_a_norm, cos_p, sin_p)
    kv_s = mla_kv_side(xs, kv_norm, w_kv_a, kv_a_norm, cos_s, sin_s)
    r_p = key_inv_rms(kv_p, w_uk)
    r_s = key_inv_rms(kv_s, w_uk)
    r_past = past_key_inv_rms(cache_kv, page_table, w_uk)

    for j in range(N_B_LAYERS):
        qp, gp = mla_query(xp, b_norm[j], b_w_in[j], b_q_a_norm[j], b_w_q[j], b_q_norm[j], k_norm, cos_p, sin_p)
        op = mla_prompt_attention(qp, kv_p, r_p, w_uk, w_uv)
        xp = mla_out(xp, op, gp, b_w_out[j])
        qs, gs = mla_query(xs, b_norm[j], b_w_in[j], b_q_a_norm[j], b_w_q[j], b_q_norm[j], k_norm, cos_s, sin_s)
        osmp = mla_sample_attention(qs, kv_s, r_s, r_past, cache_kv, page_table, w_uk, w_uv)
        xs = mla_out(xs, osmp, gs, b_w_out[j])

    y_prompt = xp[:, N_META:]
    return (y_prompt, xs, jnp.stack(ssm_p), jnp.stack(conv_p), kv_p, jnp.stack(ssm_s), jnp.stack(conv_s), kv_s)


_drawn_inputs = setup_inputs


def setup_inputs(seed=0):
    import zlib

    import numpy as np

    out = dict(_drawn_inputs(seed))
    spreads = {}
    factors = {'a_D': 5.629,
     'a_gate_norm': 3.808,
     'kv_norm': 2.89,
     'kv_a_norm': 3.179,
     'k_norm': 8.0,
     'b_norm': 8.0,
     'b_q_a_norm': 8.0,
     'b_q_norm': 8.0}
    for name, (base, spread) in spreads.items():
        noise = np.random.default_rng([zlib.crc32(name.encode()), seed]).standard_normal(out[name].shape)
        drawn = base * np.exp(spread * noise) if base else spread * noise
        out[name] = __import__('jax').numpy.asarray(drawn.astype(out[name].dtype))
    for name, factor in factors.items():
        out[name] = (out[name] * factor).astype(out[name].dtype)
    return out
```

```python
import concourse.bass as bass
import numpy as np
from concourse import mybir
from concourse.alu_op_type import AluOpType as ALU

F32 = mybir.dt.float32
F32R = mybir.dt.float32r
I32 = mybir.dt.int32
ACT = mybir.ActivationFunctionType
AX = mybir.AxisListType

P = 128
D_MODEL, D_INNER = 2048, 4096
KT = D_MODEL // P
N_SAMPLE, N_META, SEQ = 32, 16, 256
DEC_BATCH, DEC_SEQ = 8, 4
TOK = N_SAMPLE + N_META + SEQ
T_PROMPT = TOK - N_SAMPLE
TILE_AT = (0, 48, 176, 304)
TILE_N = (48, 128, 128)
TILE_ORDER = (1, 2, 0)
PAIR_AT = (0, 304, 560, 688)
PAIR_N = PAIR_AT[3]
GROUPS, HEADS, HPG, HD, STATE = 8, 64, 8, 64, 128
PAIRS = HPG // 2
GW = HPG * HD
CONV_BLK = PAIRS + 2
CB = DEC_BATCH * (3 + DEC_SEQ) + 3 + T_PROMPT
CO = CB - 3
IN_UNITS, OUT_UNITS = 10, 4
UNITS = IN_UNITS + OUT_UNITS
UNIT = KT * P
EPS = 1e-6
SBUF_START, SBUF_END = 16512, 229344


class Signal:

    def __init__(self, sem, per, base=0):
        self.sem, self.per, self.base = sem, per, base

    def open(self, eng):
        eng.sem_inc(self.sem, self.per)

    def wait(self, eng, turn, k):
        eng.wait_ge(self.sem, self.per * turn + (self.base + self.per + k + 1))

    def wait_last_turn(self, eng, turn, k):
        eng.wait_ge(self.sem, self.per * turn + (self.base + k + 1))


class Shared:

    def __init__(self, nc, ctx, kind):
        self.sem_of = lambda name: ctx.enter_context(nc.semaphore(f"{kind}_{name}"))
        self.sems, self.raised = {}, {}

    def plain(self, name, total):
        if name not in self.sems:
            self.sems[name], self.raised[name] = self.sem_of(name), 0
        base = self.raised[name]
        self.raised[name] += total
        return self.sems[name], base

    def raised_by(self, name, per, raises):
        sem, base = self.plain(name, per + raises)
        return Signal(sem, per, base)


class Chain:

    def __init__(self, eng, sem):
        self.eng, self.sem, self.base, self.n = eng, sem, 0, 0

    def turn(self, turn, per):
        self.start, self.base, self.n, self.per = self.base + self.n, None, 0, per
        self.at = turn * per + self.start

    def __call__(self, ins):
        ins.then_inc(self.sem, 1)
        self.n += 1
        if self.base is None:
            self.eng.wait_ge(self.sem, self.at + self.n)
        else:
            self.eng.wait_ge(self.sem, self.base + self.n)

    def end(self, turns):
        assert self.n == self.per, (self.n, self.per)
        self.base, self.n = self.start + turns * self.per, 0


class Space:

    def __init__(self, nc, at):
        self.nc, self.at = nc, at

    def __call__(self, name, shape, dtype=F32):
        size = int(np.prod(shape[1:])) * 4
        t = self.nc.alloc_sbuf_tensor_at(name, shape, dtype, offset=self.at)
        self.at += -(-size // 32) * 32
        assert self.at <= SBUF_END, (name, self.at)
        return t


def mm3(nc, out, a, b, start, stop):
    nc.tensor.matmul(out, a[0], b[0], start=start, stop=False)
    nc.tensor.matmul(out, a[0], b[1], start=False, stop=False)
    return nc.tensor.matmul(out, a[1], b[0], start=False, stop=stop)


def memory(nc):
    m = {}
    s = Space(nc, SBUF_START)

    def put(name, shape, dtype=F32):
        m[name] = s(name, shape, dtype)

    put("x", [P, KT, TOK])
    put("h_hi", [P, KT, TOK], F32R)
    put("h_lo", [P, KT, TOK], F32R)
    for k in range(2):
        put(f"raw{k}", [P, UNIT])
        put(f"w_hi{k}", [P, UNIT], F32R)
        put(f"w_lo{k}", [P, UNIT], F32R)
    put("ident", [P, P])
    put("ones", [P, P])
    put("eps", [P, 1])
    put("norms", [P, 3, KT])
    m["common_end"] = s.at
    put("mask", [P, PAIR_N])
    put("diag", [N_SAMPLE, DEC_BATCH])
    put("conv_w", [P, GROUPS, CONV_BLK, 4])
    put("conv_b", [P, GROUPS, CONV_BLK])
    put("conv_old", [P, GROUPS, CONV_BLK, DEC_BATCH, 3])
    put("conv_new", [P, GROUPS, CONV_BLK, DEC_BATCH + 1, 3])
    put("d_skip", [P, GROUPS, PAIRS])
    put("gate_norm", [P, GROUPS, PAIRS])
    put("dt_bias", [HEADS, 1])
    put("a_log", [HEADS, 1])
    put("cumT", [HEADS, TOK])
    put("dt_n", [P, 3, HEADS])
    put("cum_n", [P, 3, HEADS])
    put("wp_n", [P, 3, HEADS])
    put("ws_n", [N_SAMPLE, HEADS])
    put("sel", [HEADS, HPG])
    put("gate", [P, PAIRS, TOK])
    put("cbuf0", [P, CB])
    put("cbuf1", [P, CB])
    put("cacc0", [P, CO])
    put("cacc1", [P, CO])
    put("xc", [P, CONV_BLK, TOK])
    put("xdt", [P, 3, GW])
    put("xwp", [P, 3, GW])
    put("xws", [N_SAMPLE, GW])
    put("b_n", [P, 3, STATE])
    put("b_diag", [N_SAMPLE, DEC_BATCH, STATE])
    put("cb", [P, PAIR_N])
    m["sel_wide"] = nc.alloc_sbuf_tensor_at("sel_wide", [HEADS, HPG, HD], F32, offset=s.at)
    put("dec0", [P, PAIR_N])
    put("dec1", [P, PAIR_N])
    put("mix0", [P, PAIR_N])
    put("mix1", [P, PAIR_N])
    put("y", [P, PAIRS, TOK])
    put("s_in0", [P, DEC_BATCH, STATE])
    put("s_in1", [P, DEC_BATCH, STATE])
    put("s_out", [P, DEC_BATCH, STATE])
    at_s_t = s.at
    put("s_t", [P, DEC_BATCH, P])
    m["narrow"] = nc.alloc_sbuf_tensor_at("narrow", [P, KT * HD], F32, offset=at_s_t)
    put("e_cum", [P, PAIRS, N_SAMPLE])
    put("tmp32", [P, N_SAMPLE])
    put("y_hi", [P, PAIRS, TOK], F32R)
    put("y_lo", [P, PAIRS, TOK], F32R)
    put("y_rstd", [P, TOK])
    put("sp_out", [P, PAIRS, STATE])
    m["mamba_end"] = s.at
    m["y_sq"] = m["gate"]
    return m


def load_stage(nc, ctx, m, d):
    sem = lambda n: ctx.enter_context(nc.semaphore(n))
    loaded, x_loaded = sem("consts_loaded"), sem("x_loaded")
    small = ["ident", "ones", "eps", "norms", "narrow", "mask", "diag", "conv_w", "conv_b", "conv_old",
             "d_skip", "gate_norm", "dt_bias", "a_log"]
    with nc.Block() as block:
        @block.sync
        def _(sp):
            sp.dma_start(m["x"][:], d["x"]).then_inc(x_loaded, 16)
            sp.wait_ge(x_loaded, 16)

        @block.scalar
        def _(act):
            for name in small:
                act.dma_start(m[name][:], d[name]).then_inc(loaded, 16)
            act.wait_ge(loaded, 16 * len(small))


def norm_stage(nc, shared, m, psum, which):
    (squared, b1), (summed, b2), (rooted, b3), (scaled, b4), (high, b5), (low, b6) = [
        shared.plain(s, n) for s, n in (("squared", KT), ("summed", KT), ("rooted", 2), ("scaled", KT), ("high", KT), ("low", KT))]
    x, hi, lo, ones = m["x"], m["h_hi"], m["h_lo"], m["ones"]
    sq = [m["raw0"], m["raw1"]]
    ln, rs = (m[f"raw{k}"][:, 2 * TOK:3 * TOK] for k in range(2))
    with nc.Block() as block:
        @block.scalar
        def _(act):
            for k in range(KT):
                if k >= 2:
                    act.wait_ge(summed, b2 + k - 1)
                nc.scalar.activation(sq[k % 2][:, 0:TOK], x[:, k, :], ACT.Square).then_inc(squared, 1)
            act.wait_ge(summed, b2 + KT)
            nc.scalar.activation(ln, psum[0][:, 0:TOK], ACT.Ln, bias=m["eps"][:, 0:1], scale=1.0 / D_MODEL).then_inc(rooted, 1)
            act.wait_ge(rooted, b3 + 1)
            nc.scalar.activation(rs, ln, ACT.Exp, scale=-0.5).then_inc(rooted, 1)
            for k in range(KT):
                act.wait_ge(scaled, b4 + k + 1)
                nc.scalar.activation(hi[:, k, :], sq[k % 2][:, TOK:2 * TOK], ACT.Copy).then_inc(high, 1)

        @block.tensor
        def _(pe):
            for k in range(KT):
                pe.wait_ge(squared, b1 + k + 1)
                nc.tensor.matmul(psum[0][:, 0:TOK], ones[:], sq[k % 2][:, 0:TOK], start=k == 0,
                                 stop=k == KT - 1).then_inc(summed, 1)

        @block.vector
        def _(dve):
            dve.wait_ge(rooted, b3 + 2)
            for k in range(KT):
                if k >= 2:
                    dve.wait_ge(low, b6 + k - 1)
                    dve.wait_ge(high, b5 + k - 1)
                nc.vector.scalar_tensor_tensor(sq[k % 2][:, TOK:2 * TOK], x[:, k, :], m["norms"][:, which, k:k + 1],
                                               rs, op0=ALU.mult, op1=ALU.mult).then_inc(scaled, 1)
                dve.wait_ge(high, b5 + k + 1)
                nc.vector.tensor_tensor(lo[:, k, :], sq[k % 2][:, TOK:2 * TOK], hi[:, k, :].bitcast(F32),
                                        ALU.subtract).then_inc(low, 1)
            dve.wait_ge(low, b6 + KT)


def dt_stage(nc, ctx, m, psum, d):
    sem = lambda n: ctx.enter_context(nc.semaphore(f"dt_{n}"))
    split, proj, a_step, v_step, t_done, t_out = [sem(n) for n in ("split", "proj", "act", "dve", "transposed", "out")]
    w_hi, w_lo = m["w_hi0"], m["w_lo0"]
    N = KT * HD
    raw = m["narrow"]
    half = lambda name, k: m[name][0:HEADS, k * TOK:(k + 1) * TOK]
    xb, ab, dt, da = half("mix0", 0), half("mix0", 1), half("mix1", 0), half("mix1", 1)
    wp, ws = half("dec0", 0), half("dec0", 1)[:, 0:N_SAMPLE]
    neg_a, seq_a = m["y_rstd"][0:HEADS, 0:1], m["y_rstd"][0:HEADS, 1:2]
    one_row = half("dec1", 0)
    cum = m["cumT"]
    by_seq = lambda ap: ap.rearrange("p (b t) -> p b t", t=DEC_SEQ)
    V_CUM = 10
    with nc.Block() as block:
        @block.scalar
        def _(act):
            c = Chain(act, a_step)
            nc.scalar.activation(w_hi[:, 0:N], raw[:, 0:N], ACT.Copy).then_inc(split, 1)
            c(nc.scalar.activation(seq_a, m["a_log"][:, 0:1], ACT.Exp))
            act.wait_ge(proj, 1)
            nc.scalar.activation(xb, psum[0][0:HEADS, 0:TOK], ACT.Identity, bias=m["dt_bias"][:, 0:1]).then_inc(a_step, 1)
            c.n += 1
            act.wait_ge(a_step, c.n)
            c(nc.scalar.activation(ab, xb, ACT.Abs))
            c(nc.scalar.activation(ab, ab, ACT.Exp, scale=-1.0))
            c(nc.scalar.activation(ab, ab, ACT.Ln, bias=1.0))
            act.wait_ge(v_step, V_CUM)
            nc.scalar.activation(wp[:, N_SAMPLE:TOK], cum[:, N_SAMPLE:TOK], ACT.Exp, scale=-1.0,
                                 bias=cum[:, TOK - 1:TOK]).then_inc(a_step, 1)
            act.wait_ge(v_step, V_CUM + 1)
            nc.scalar.activation(ws, ws, ACT.Exp).then_inc(a_step, 1)

        @block.vector
        def _(dve):
            v = Chain(dve, v_step)
            dve.wait_ge(split, 1)
            nc.vector.tensor_tensor(w_lo[:, 0:N], raw[:, 0:N], w_hi[:, 0:N].bitcast(F32), ALU.subtract).then_inc(split, 1)
            v(nc.vector.memset(one_row, 1.0))
            v(nc.vector.memset(wp, 0.0))
            dve.wait_ge(a_step, 5)
            v(nc.vector.scalar_tensor_tensor(dt, xb, 0.0, ab, op0=ALU.max, op1=ALU.add))
            v(nc.vector.tensor_scalar(neg_a, seq_a, -1.0, None, ALU.mult))
            v(nc.vector.tensor_scalar(da, dt, neg_a, None, ALU.mult))
            v(nc.vector.tensor_tensor_scan(cum[:, N_SAMPLE:TOK], one_row[:, N_SAMPLE:TOK], da[:, N_SAMPLE:TOK],
                                           0.0, ALU.mult, ALU.add))
            cs, ds = by_seq(cum[:, 0:N_SAMPLE]), by_seq(da[:, 0:N_SAMPLE])
            v(nc.vector.tensor_copy(cs[:, :, 0:1], ds[:, :, 0:1]))
            for t in range(1, DEC_SEQ):
                v(nc.vector.tensor_tensor(cs[:, :, t:t + 1], cs[:, :, t - 1:t], ds[:, :, t:t + 1], ALU.add))
            assert v.n == V_CUM
            v(nc.vector.tensor_tensor(by_seq(ws), cs[:, :, DEC_SEQ - 1:DEC_SEQ].to_broadcast([HEADS, DEC_BATCH, DEC_SEQ]), cs, ALU.subtract))
            dve.wait_ge(a_step, 7)
            v(nc.vector.tensor_tensor(wp, wp, dt, ALU.mult))
            v(nc.vector.tensor_tensor(ws, ws, dt[:, 0:N_SAMPLE], ALU.mult))
            for n, (name, where) in enumerate((("dt_n", 1), ("cum_n", 2), ("wp_n", 3))):
                dve.wait_ge(t_done, 3 * n + 3)
                for t in range(3):
                    nc.vector.tensor_copy(m[name][0:TILE_N[t], t, :],
                                          psum[where][0:TILE_N[t], t * HEADS:(t + 1) * HEADS]).then_inc(t_out, 1)
            dve.wait_ge(t_done, 10)
            nc.vector.tensor_copy(m["ws_n"][:], psum[4][0:N_SAMPLE, 0:HEADS]).then_inc(t_out, 1)
            for k in range(2):
                v(nc.vector.memset(m[f"cbuf{k}"][:], 0.0))

        @block.tensor
        def _(pe):
            pe.wait_ge(split, 2)
            for k in range(KT):
                last = mm3(nc, psum[0][0:HEADS, 0:TOK], (w_hi[:, k * HD:(k + 1) * HD], w_lo[:, k * HD:(k + 1) * HD]),
                           (m["h_hi"][:, k, :], m["h_lo"][:, k, :]), k == 0, k == KT - 1)
            last.then_inc(proj, 1)
            pe.wait_ge(v_step, 13)
            eye = m["ident"][0:HEADS, 0:HEADS]
            for src, where in ((dt, 1), (cum, 2), (wp, 3)):
                for t in range(3):
                    nc.tensor.transpose(psum[where][0:TILE_N[t], t * HEADS:(t + 1) * HEADS],
                                        src[:, TILE_AT[t]:TILE_AT[t + 1]], eye).then_inc(t_done, 1)
            nc.tensor.transpose(psum[4][0:N_SAMPLE, 0:HEADS], ws, eye).then_inc(t_done, 1)


def mamba_stage(nc, ctx, m, psum, d):
    def sig(name, per):
        return Signal(ctx.enter_context(nc.semaphore("m_" + name)), per)
    sem = lambda n: ctx.enter_context(nc.semaphore("m_" + n))
    raw_in = [sem("raw_in0"), sem("raw_in1")]
    s_loaded = [sem("s_loaded0"), sem("s_loaded1")]
    lo_done, hi_done = sig("lo_done", UNITS), sig("hi_done", UNITS)
    blk_done = sig("blk_done", IN_UNITS + 4 * OUT_UNITS)
    in_out, out_out = sig("in_evac", IN_UNITS), sig("out_evac", 16)
    conv_done, conv_saved, xc_done = sig("conv_done", CONV_BLK), sig("conv_saved", CONV_BLK), sig("xc_done", CONV_BLK)
    sel_set = sig("sel_set", 2)
    cb_done, cb_out = sig("cb_done", 2), sig("cb_evac", 2)
    bn_done, bn_out, bd_done = sig("bn_done", 1), sig("bn_evac", 2), sig("bd_done", 1)
    xn_done, xn_out = sig("xn_done", 3), sig("xn_evac", 3)
    ec_done, ec_out = sig("ec_done", 1), sig("ec_evac", 1)
    cum_done, dec_done, mix_done = sig("cum_done", HPG), sig("dec_done", HPG), sig("mix_done", HPG)
    cum_read = sig("cum_read", HPG)
    y_done, y_out, sq_done = sig("y_done", HPG), sig("y_evac", PAIRS), sig("sq_done", PAIRS)
    st_done, st_out = sig("st_done", 2 * PAIRS), sig("st_evac", 2 * PAIRS)
    ys_done, up_done, up_out = sig("ys_done", PAIRS), sig("up_done", 2 * PAIRS), sig("up_evac", 2 * PAIRS)
    sp_done, sp_evac = sig("sp_done", 1), sig("sp_evac", 1)
    s_stored = sem("s_stored")
    sp_stored, conv_stored = sem("sp_stored"), sem("conv_stored")
    norm_done, rstd_done = sig("norm_done", 1), sig("rstd_done", 1)
    yn_done, yhi_done, ylo_done = sig("yn_done", 1), sig("yhi_done", 1), sig("ylo_done", 1)
    dve_step, act_step = sem("dve_step"), sem("act_step")

    raw, w_hi, w_lo = ([m[f"{n}{k}"] for k in range(2)] for n in ("raw", "w_hi", "w_lo"))
    cbuf, cacc, s_in = ([m[f"{n}{k}"] for k in range(2)] for n in ("cbuf", "cacc", "s_in"))
    s_out = m["s_out"]
    dec, mix = ([m[f"{n}{k}"] for k in range(2)] for n in ("dec", "mix"))
    xc, x = m["xc"], m["x"]
    xB, xC = 4, 5
    DENSE = psum[0:2]
    BN, CUM, Y, SA, SB = psum[2], psum[3:5], psum[5], psum[6], psum[7]
    XN = psum[3:6]
    by_seq = lambda ap, n: ap[:, 0:DEC_BATCH * n].rearrange("p (b t) -> p b t", t=n)
    NB = IN_UNITS + 4 * OUT_UNITS

    with nc.Block() as block:
        @block.sync
        def _(sp):
            with sp.Fori(0, GROUPS) as g:
                def unit(k):
                    if k >= 2:
                        lo_done.wait(sp, g, k - 2)
                    else:
                        lo_done.wait_last_turn(sp, g, UNITS + k - 2)
                    sp.dma_start(raw[k % 2][:], d["a_units"][bass.ds(g * UNITS + k, 1)].rearrange("a p n -> (a p) n")).then_inc(raw_in[k % 2], 16)

                def state_in(p):
                    if p >= 2:
                        up_out.wait(sp, g, 2 * (p - 2) + 1)
                    else:
                        up_out.wait_last_turn(sp, g, 2 * (p + 2) + 1)
                    sp.dma_start(s_in[p % 2][:], d["state_in"][:, bass.ds(g * GW + p * P, P), :].rearrange("b p n -> p b n")).then_inc(s_loaded[p % 2], 16)

                def state_out(p):
                    up_out.wait(sp, g, 2 * p + 1)
                    sp.dma_start(d["state_out"][:, bass.ds(g * GW + p * P, P), :].rearrange("b p n -> p b n"), s_out[:]).then_inc(s_stored, 16)
                for k in range(IN_UNITS):
                    unit(k)
                    if k == 3:
                        state_in(0)
                    if k == 5:
                        state_in(1)
                unit(10)
                unit(11)
                state_in(2)
                state_out(0)
                state_in(3)
                state_out(1)
                state_out(2)
                state_out(3)
                sp_evac.wait(sp, g, 0)
                sp.dma_start(d["sp_out"][bass.ds(g, 1)].rearrange("a p j n -> (a p) j n"), m["sp_out"][:]).then_inc(sp_stored, 16)
                unit(12)
                unit(13)
            conv_saved.wait(sp, GROUPS - 1, CONV_BLK - 1)
            sp.dma_start(d["conv_out"], m["conv_new"][:]).then_inc(conv_stored, 16)
            sp.wait_ge(s_stored, 16 * (PAIRS * GROUPS + 1))
            sp.wait_ge(sp_stored, 16 * (GROUPS + 1))
            sp.wait_ge(conv_stored, 16)

        @block.gpsimd
        def _(pool):
            lo_done.open(pool)
            with pool.Fori(0, GROUPS) as g:
                for k in range(UNITS):
                    hi_done.wait(pool, g, k)
                    nc.gpsimd.tensor_tensor(w_lo[k % 2][:], raw[k % 2][:], w_hi[k % 2][:].bitcast(F32), ALU.subtract).then_inc(lo_done.sem, 1)

        @block.tensor
        def _(pe):
            for s in (blk_done, cb_done, bn_done, xn_done, ec_done, cum_done, y_done, st_done, ys_done, up_done, sp_done, norm_done):
                s.open(pe)
            with pe.Fori(0, GROUPS) as g:
                for k in range(IN_UNITS):
                    if k >= 2:
                        in_out.wait(pe, g, k - 2)
                    else:
                        out_out.wait_last_turn(pe, g, 14 + k)
                    lo_done.wait(pe, g, k)
                    for j in range(KT):
                        c = slice(j * P, (j + 1) * P)
                        last = mm3(nc, DENSE[k % 2][:, 0:TOK], (w_hi[k % 2][:, c], w_lo[k % 2][:, c]),
                                   (m["h_hi"][:, j, :], m["h_lo"][:, j, :]), j == 0, j == KT - 1)
                    last.then_inc(blk_done.sem, 1)

                xc_done.wait(pe, g, xC)
                up_out.wait_last_turn(pe, g, 7)
                sp_evac.wait_last_turn(pe, g, 0)
                nc.tensor.matmul(SA[0:48, 0:TOK], xc[:, xB, 0:48], xc[:, xC, :], start=True, stop=True).then_inc(cb_done.sem, 1)
                nc.tensor.matmul(SB[:, 0:256], xc[:, xB, 48:176], xc[:, xC, 48:TOK], start=True, stop=True)
                nc.tensor.matmul(SB[:, 256:384], xc[:, xB, 176:TOK], xc[:, xC, 176:TOK], start=True, stop=True).then_inc(cb_done.sem, 1)
                y_out.wait_last_turn(pe, g, PAIRS - 1)
                for t in TILE_ORDER:
                    last = nc.tensor.transpose(BN[0:TILE_N[t], t * STATE:(t + 1) * STATE], xc[:, xB, TILE_AT[t]:TILE_AT[t + 1]], m["ident"][:])
                last.then_inc(bn_done.sem, 1)
                rstd_done.wait_last_turn(pe, g, 0)
                for n, t in enumerate(TILE_ORDER):
                    for p in range(PAIRS):
                        last = nc.tensor.transpose(XN[n][0:TILE_N[t], p * P:(p + 1) * P], xc[:, p, TILE_AT[t]:TILE_AT[t + 1]], m["ident"][:])
                    last.then_inc(xn_done.sem, 1)
                bn_out.wait(pe, g, 1)
                sel_set.wait(pe, g, 1)
                for p in range(PAIRS):
                    last = nc.tensor.matmul(BN[:, p * N_SAMPLE:(p + 1) * N_SAMPLE], m["sel_wide"][:, 2 * p:2 * p + 2, :].rearrange("p e c -> p (e c)"),
                                            m["cumT"][:, 0:N_SAMPLE], start=True, stop=True)
                last.then_inc(ec_done.sem, 1)

                def states(p):
                    pe.wait_ge(s_loaded[p % 2], 16 * (2 * g + p // 2 + 1))
                    for half, bank in enumerate((SA, SB)):
                        if p == 0:
                            cb_out.wait(pe, g, half)
                        else:
                            up_out.wait(pe, g, 2 * (p - 1) + half)
                        for b in range(4):
                            last = nc.tensor.transpose(bank[:, b * P:(b + 1) * P], s_in[p % 2][:, 4 * half + b, :], m["ident"][:])
                        last.then_inc(st_done.sem, 1)
                    st_out.wait(pe, g, 2 * p)
                    st_out.wait(pe, g, 2 * p + 1)
                    ec_out.wait(pe, g, 0)
                    if p:
                        y_out.wait(pe, g, p - 1)
                    for b in range(DEC_BATCH):
                        last = nc.tensor.matmul(BN[:, 128 + p * N_SAMPLE + b * 4:128 + p * N_SAMPLE + b * 4 + 4], m["s_t"][:, b, :],
                                                xc[:, xC, b * 4:b * 4 + 4], start=True, stop=True)
                    last.then_inc(ys_done.sem, 1)
                    xn_out.wait(pe, g, 2)
                    bd_done.wait(pe, g, 0)
                    for half, bank in enumerate((SA, SB)):
                        nc.tensor.matmul(bank[:, :], m["xws"][:, p * P:(p + 1) * P],
                                         m["b_diag"][:, 4 * half:4 * half + 4, :].rearrange("p b n -> p (b n)"), start=True, stop=True).then_inc(up_done.sem, 1)

                def head(e):
                    if e < 2:
                        xn_out.wait(pe, g, e)
                    else:
                        cum_read.wait(pe, g, e - 2)
                    nc.tensor.matmul(CUM[e % 2][:, 0:TOK], m["sel"][:, e:e + 1].to_broadcast([HEADS, P]), m["cumT"][:, :],
                                     start=True, stop=True).then_inc(cum_done.sem, 1)

                def head_y(e):
                    p, rows = e // 2, slice(64 * (e % 2), 64 * (e % 2) + 64)
                    if e == 0:
                        xn_out.wait(pe, g, 2)
                    elif e % 2 == 0:
                        y_out.wait(pe, g, p - 1)
                    mix_done.wait(pe, g, e)
                    mx, c = mix[e % 2], slice(e * HD, (e + 1) * HD)
                    nc.tensor.matmul(Y[rows, 48:TOK], m["xdt"][:, 1, c], mx[:, 304:560], start=True, stop=False)
                    nc.tensor.matmul(Y[rows, 176:TOK], m["xdt"][:, 2, c], mx[:, 560:688], start=False, stop=False)
                    nc.tensor.matmul(Y[rows, 48:TOK], m["xdt"][0:48, 0, c], mx[0:48, 48:304], start=False, stop=False)
                    last = nc.tensor.matmul(Y[rows, 0:48], m["xdt"][0:48, 0, c], mx[0:48, 0:48], start=False, stop=True)
                    last.then_inc(y_done.sem, 1)
                head(0)
                for e in range(HPG):
                    if e % 2 == 0:
                        states(e // 2)
                    if e + 1 < HPG:
                        head(e + 1)
                    head_y(e)
                up_out.wait(pe, g, 2 * PAIRS - 2)
                for p in range(PAIRS):
                    for t in range(3):
                        last = nc.tensor.matmul(SA[:, p * STATE:(p + 1) * STATE], m["xwp"][0:TILE_N[t], t, p * P:(p + 1) * P],
                                                m["b_n"][0:TILE_N[t], t, :], start=t == 0, stop=t == 2)
                last.then_inc(sp_done.sem, 1)
                cum_read.wait(pe, g, HPG - 2)
                for p in range(PAIRS):
                    sq_done.wait(pe, g, p)
                    last = nc.tensor.matmul(CUM[0][:, 0:TOK], m["ones"][:], m["y_sq"][:, p, :], start=p == 0, stop=p == PAIRS - 1)
                last.then_inc(norm_done.sem, 1)
                ylo_done.wait(pe, g, 0)
                for k in range(OUT_UNITS):
                    lo_done.wait(pe, g, IN_UNITS + k)
                    for b in range(4):
                        c = 4 * k + b
                        if c < 2:
                            in_out.wait(pe, g, 8 + c)
                        else:
                            out_out.wait(pe, g, c - 2)
                        for j in range(PAIRS):
                            w = slice((b * 4 + j) * P, (b * 4 + j + 1) * P)
                            last = mm3(nc, DENSE[c % 2][:, 0:TOK], (w_hi[k % 2][:, w], w_lo[k % 2][:, w]),
                                       (m["y_hi"][:, j, :], m["y_lo"][:, j, :]), j == 0, j == PAIRS - 1)
                        last.then_inc(blk_done.sem, 1)

        @block.scalar
        def _(act):
            a = Chain(act, act_step)
            for s in (hi_done, in_out, xc_done, ec_out, dec_done, sq_done, rstd_done, yhi_done, cum_read):
                s.open(act)
            A_STEPS = 1
            with act.Fori(0, GROUPS) as g:
                a.turn(g, A_STEPS)

                def split(k):
                    act.wait_ge(raw_in[k % 2], 16 * ((UNITS // 2) * g + k // 2 + 1))
                    if k < 2:
                        blk_done.wait_last_turn(act, g, NB - 1 - 4 * (1 - k))
                    elif k - 2 < IN_UNITS:
                        blk_done.wait(act, g, k - 2)
                    else:
                        blk_done.wait(act, g, IN_UNITS + 4 * (k - 2 - IN_UNITS) + 3)
                    nc.scalar.activation(w_hi[k % 2][:], raw[k % 2][:], ACT.Copy).then_inc(hi_done.sem, 1)

                def evac(k):
                    blk_done.wait(act, g, k)
                    src = DENSE[k % 2]
                    if k < CONV_BLK:
                        if k >= 2:
                            conv_saved.wait(act, g, k - 2)
                        else:
                            conv_saved.wait_last_turn(act, g, CONV_BLK - 2 + k)
                        buf = cbuf[k % 2]
                        nc.scalar.activation(by_seq(buf, 7)[:, :, 0:3], m["conv_old"][:, bass.ds(g, 1), k, :, :].rearrange("p a b t -> p (a b) t"), ACT.Copy)
                        nc.scalar.activation(by_seq(buf, 7)[:, :, 3:7], by_seq(src, 4), ACT.Copy)
                        nc.scalar.activation(buf[:, 59:CB], src[:, N_SAMPLE:TOK], ACT.Copy).then_inc(in_out.sem, 1)
                    else:
                        if k == CONV_BLK:
                            y_out.wait_last_turn(act, g, PAIRS - 1)
                        nc.scalar.activation(m["gate"][:, k - CONV_BLK, :], src[:, 0:TOK], ACT.Silu).then_inc(in_out.sem, 1)

                def conv_silu(k):
                    conv_done.wait(act, g, k)
                    if k == 0:
                        ys_done.wait_last_turn(act, g, PAIRS - 1)
                        y_out.wait_last_turn(act, g, PAIRS - 1)
                    nc.scalar.activation(xc[:, k, 0:N_SAMPLE].rearrange("p (b t) -> p b t", t=4), by_seq(cacc[k % 2], 7)[:, :, 0:4], ACT.Silu)
                    nc.scalar.activation(xc[:, k, N_SAMPLE:TOK], cacc[k % 2][:, 56:CO], ACT.Silu).then_inc(xc_done.sem, 1)
                split(0)
                for k in range(IN_UNITS):
                    split(k + 1)
                    evac(k)
                    if 1 <= k <= CONV_BLK:
                        conv_silu(k - 1)
                split(11)
                ec_done.wait(act, g, 0)
                up_out.wait_last_turn(act, g, 2 * PAIRS - 1)
                y_out.wait_last_turn(act, g, PAIRS - 1)
                nc.scalar.activation(m["e_cum"][:].rearrange("p a b -> p (a b)"), BN[:, 0:P], ACT.Exp).then_inc(ec_out.sem, 1)
                for e in range(HPG):
                    cum_done.wait(act, g, e)
                    if e >= 2:
                        mix_done.wait(act, g, e - 2)
                    else:
                        mix_done.wait_last_turn(act, g, HPG - 2 + e)
                    dc = dec[e % 2]
                    for t in range(3):
                        n = TILE_N[t]
                        last = nc.scalar.activation(dc[0:n, PAIR_AT[t]:PAIR_AT[t + 1]], CUM[e % 2][0:n, TILE_AT[t]:TOK], ACT.Relu,
                                                    bias=m["cum_n"][0:n, t, bass.ds(g * HPG + e, 1)], scale=-1.0)
                    last.then_inc(cum_read.sem, 1)
                    cum_read.wait(act, g, e)
                    nc.scalar.activation(dc[0:48, 0:304], dc[0:48, 0:304], ACT.Exp, scale=-1.0)
                    nc.scalar.activation(dc[:, 304:688], dc[:, 304:688], ACT.Exp, scale=-1.0).then_inc(dec_done.sem, 1)
                for p in range(PAIRS):
                    y_out.wait(act, g, p)
                    nc.scalar.activation(m["y_sq"][:, p, :], m["y"][:, p, :], ACT.Square).then_inc(sq_done.sem, 1)
                norm_done.wait(act, g, 0)
                a(nc.scalar.activation(m["y_rstd"][:], CUM[0][:, 0:TOK], ACT.Ln, bias=m["eps"][:, 0:1], scale=1.0 / GW))
                nc.scalar.activation(m["y_rstd"][:], m["y_rstd"][:], ACT.Exp, scale=-0.5).then_inc(rstd_done.sem, 1)
                yn_done.wait(act, g, 0)
                nc.scalar.activation(m["y_hi"][:], m["y"][:], ACT.Copy).then_inc(yhi_done.sem, 1)
                split(12)
                split(13)
            a.end(GROUPS)

        @block.vector
        def _(dve):
            v = Chain(dve, dve_step)
            for s in (out_out, conv_done, conv_saved, sel_set, cb_out, bn_out, bd_done, xn_out, mix_done, y_out, st_out, up_out,
                      sp_evac, yn_done, ylo_done):
                s.open(dve)
            for s in (s_stored, sp_stored):
                dve.sem_inc(s, 16)
            V_STEPS = 3 * CONV_BLK + 3 * PAIRS
            with dve.Fori(0, GROUPS) as g:
                v.turn(g, V_STEPS)
                cum_done.wait_last_turn(dve, g, HPG - 1)
                nc.vector.tensor_copy(m["sel"][:], m["ident"][0:HEADS, bass.ds(g * HPG, HPG)]).then_inc(sel_set.sem, 1)
                sel_set.wait(dve, g, 0)
                nc.vector.tensor_copy(m["sel_wide"][:], m["sel"][:].rearrange("p (e c) -> p e c", c=1).to_broadcast([HEADS, HPG, HD])).then_inc(sel_set.sem, 1)
                for k in range(CONV_BLK):
                    in_out.wait(dve, g, k)
                    if k >= 2:
                        xc_done.wait(dve, g, k - 2)
                    else:
                        xc_done.wait_last_turn(dve, g, CONV_BLK - 2 + k)
                    buf, acc = cbuf[k % 2], cacc[k % 2]
                    cw = lambda t: m["conv_w"][:, bass.ds(g, 1), k, t:t + 1].rearrange("p a b -> p (a b)")
                    v(nc.vector.tensor_scalar(acc[:, :], buf[:, 0:CO], cw(0), m["conv_b"][:, bass.ds(g, 1), k:k + 1].rearrange("p a b -> p (a b)"), ALU.mult, ALU.add))
                    for t in range(1, 4):
                        ins = nc.vector.scalar_tensor_tensor(acc[:, :], buf[:, t:t + CO], cw(t), acc[:, :], op0=ALU.mult, op1=ALU.add)
                        if t < 3:
                            v(ins)
                    ins.then_inc(conv_done.sem, 1)
                    new = m["conv_new"][:, bass.ds(g, 1), k].rearrange("p a b t -> p (a b) t")
                    nc.vector.tensor_copy(new[:, 0:DEC_BATCH, :], by_seq(buf, 7)[:, :, 4:7])
                    nc.vector.tensor_copy(new[:, DEC_BATCH:DEC_BATCH + 1, :], buf[:, CB - 3:CB].rearrange("p (a t) -> p a t", a=1)).then_inc(conv_saved.sem, 1)
                cb_done.wait(dve, g, 0)
                y_done.wait_last_turn(dve, g, HPG - 1)
                nc.vector.tensor_tensor(m["cb"][0:48, 0:304], SA[0:48, 0:304], m["mask"][0:48, 0:304], ALU.mult).then_inc(cb_out.sem, 1)
                cb_done.wait(dve, g, 1)
                nc.vector.tensor_tensor(m["cb"][:, 304:688], SB[:, 0:384], m["mask"][:, 304:688], ALU.mult).then_inc(cb_out.sem, 1)
                bn_done.wait(dve, g, 0)
                sp_done.wait_last_turn(dve, g, 0)
                nc.vector.tensor_copy(m["b_n"][0:48, 0, :], BN[0:48, 0:STATE]).then_inc(bn_out.sem, 1)
                nc.vector.tensor_copy(m["b_n"][:, 1:3, :], BN[:, STATE:3 * STATE].rearrange("p (t n) -> p t n", t=2)).then_inc(bn_out.sem, 1)
                bn_out.wait(dve, g, 0)
                nc.vector.tensor_tensor(m["b_diag"][:], m["b_n"][0:N_SAMPLE, 0:1, :].to_broadcast([N_SAMPLE, DEC_BATCH, STATE]),
                                        m["diag"][:].rearrange("p (b a) -> p b a", a=1).to_broadcast([N_SAMPLE, DEC_BATCH, STATE]), ALU.mult).then_inc(bd_done.sem, 1)
                for bank, t in enumerate(TILE_ORDER):
                    xn_done.wait(dve, g, bank)
                    n = TILE_N[t]

                    def times(out, rows, coef):
                        return nc.vector.tensor_tensor(out.rearrange("p (e c) -> p e c", e=HPG), XN[bank][0:rows, :].rearrange("p (e c) -> p e c", e=HPG),
                                                       coef.rearrange("p (e c) -> p e c", c=1).to_broadcast([rows, HPG, HD]), ALU.mult)
                    times(m["xdt"][0:n, t, :], n, m["dt_n"][0:n, t, bass.ds(g * HPG, HPG)])
                    if t == 0:
                        times(m["xws"][:, :], N_SAMPLE, m["ws_n"][:, bass.ds(g * HPG, HPG)])
                    times(m["xwp"][0:n, t, :], n, m["wp_n"][0:n, t, bass.ds(g * HPG, HPG)]).then_inc(xn_out.sem, 1)

                def states(p):
                    for half, bank in enumerate((SA, SB)):
                        st_done.wait(dve, g, 2 * p + half)
                        if half == 0:
                            if p:
                                ys_done.wait(dve, g, p - 1)
                            else:
                                ys_done.wait_last_turn(dve, g, PAIRS - 1)
                        nc.vector.tensor_copy(m["s_t"][:, 4 * half:4 * half + 4, :].rearrange("p b n -> p (b n)"), bank[:, :]).then_inc(st_out.sem, 1)

                def update(p):
                    dve.wait_ge(s_loaded[p % 2], 16 * (2 * g + p // 2 + 1))
                    dve.wait_ge(s_stored, 16 * (PAIRS * g + p + 1))
                    for half, bank in enumerate((SA, SB)):
                        up_done.wait(dve, g, 2 * p + half)
                        for b in range(4 * half, 4 * half + 4):
                            last = nc.vector.scalar_tensor_tensor(s_out[:, b, :], s_in[p % 2][:, b, :], m["e_cum"][:, p, 4 * b + 3:4 * b + 4],
                                                                  bank[:, (b % 4) * P:(b % 4 + 1) * P], op0=ALU.mult, op1=ALU.add)
                        last.then_inc(up_out.sem, 1)

                def mixes(e):
                    dec_done.wait(dve, g, e)
                    if e >= 2:
                        mixed_used(e)
                    nc.vector.tensor_tensor(mix[e % 2][0:48, 0:304], dec[e % 2][0:48, 0:304], m["cb"][0:48, 0:304], ALU.mult)
                    nc.vector.tensor_tensor(mix[e % 2][:, 304:688], dec[e % 2][:, 304:688], m["cb"][:, 304:688], ALU.mult).then_inc(mix_done.sem, 1)

                def mixed_used(e):
                    y_done.wait(dve, g, e - 2)

                def y_pair(p):
                    y_done.wait(dve, g, 2 * p + 1)
                    ys_done.wait(dve, g, p)
                    if p == 0:
                        yhi_done.wait_last_turn(dve, g, 0)
                        ylo_done.wait_last_turn(dve, g, 0)
                    y = m["y"][:, p, :]
                    v(nc.vector.scalar_tensor_tensor(y, xc[:, p, :], m["d_skip"][:, bass.ds(g, 1), p:p + 1].rearrange("p a b -> p (a b)"), Y[:, 0:TOK], op0=ALU.mult, op1=ALU.add))
                    v(nc.vector.tensor_tensor(m["tmp32"][:], m["e_cum"][:, p, :], BN[:, 128 + p * N_SAMPLE:128 + (p + 1) * N_SAMPLE], ALU.mult))
                    v(nc.vector.tensor_tensor(y[:, 0:N_SAMPLE], y[:, 0:N_SAMPLE], m["tmp32"][:], ALU.add))
                    nc.vector.tensor_tensor(y, y, m["gate"][:, p, :], ALU.mult).then_inc(y_out.sem, 1)
                for e in range(HPG):
                    if e % 2 == 0:
                        states(e // 2)
                    mixes(e)
                    if e % 2 == 0:
                        update(e // 2)
                    else:
                        y_pair(e // 2)
                sp_done.wait(dve, g, 0)
                dve.wait_ge(sp_stored, 16 * (g + 1))
                nc.vector.tensor_copy(m["sp_out"][:].rearrange("p j n -> p (j n)"), SA[:, :]).then_inc(sp_evac.sem, 1)
                rstd_done.wait(dve, g, 0)
                for p in range(PAIRS):
                    last = nc.vector.scalar_tensor_tensor(m["y"][:, p, :], m["y"][:, p, :], m["gate_norm"][:, bass.ds(g, 1), p:p + 1].rearrange("p a b -> p (a b)"),
                                                          m["y_rstd"][:], op0=ALU.mult, op1=ALU.mult)
                last.then_inc(yn_done.sem, 1)
                yhi_done.wait(dve, g, 0)
                nc.vector.tensor_tensor(m["y_lo"][:], m["y"][:], m["y_hi"][:].bitcast(F32), ALU.subtract).then_inc(ylo_done.sem, 1)
                for c in range(16):
                    blk_done.wait(dve, g, IN_UNITS + c)
                    nc.vector.tensor_tensor(x[:, c, :], x[:, c, :], DENSE[c % 2][:, 0:TOK], ALU.add).then_inc(out_out.sem, 1)
            v.end(GROUPS)


MLA_HEADS, LATENT, ROPE, NOPE = 16, 512, 64, 128
LT = LATENT // P
QK = NOPE + ROPE
ROW = LATENT + ROPE
Q_PAIRS = MLA_HEADS // 2
PAGES = 8
QROWS = DEC_SEQ * MLA_HEADS


def memory_mla(nc, m):
    s = Space(nc, m["common_end"])

    def put(name, shape, dtype=F32):
        m[name] = s(name, shape, dtype)
    put("o", [P, MLA_HEADS, TOK])
    put("lat_s", [P, LT, N_SAMPLE])
    put("kr_s", [ROPE, N_SAMPLE])
    put("rows_s", [N_SAMPLE, LATENT])
    put("r_new", [QROWS, N_SAMPLE])
    put("table", [1, DEC_BATCH * PAGES], I32)
    m["mla_kept"] = s.at
    put("rot", [P, P])
    put("half", [P, 2, P])
    put("cos", [P, TOK])
    put("sin", [P, TOK])
    put("mla_gain", [P, 2, LT])
    put("qk_gain", [P, 4])
    put("lat", [P, LT, TOK])
    put("kr", [P, TOK])
    put("rows_n", [P, 3, ROW])
    put("r_n", [P, 3, MLA_HEADS])
    put("ss_n", [P, 3, MLA_HEADS])
    put("ssr_n", [P, 3])
    put("lat_hi", [P, LT, TOK], F32R)
    put("lat_lo", [P, LT, TOK], F32R)
    put("qn", [P, MLA_HEADS, TOK])
    put("qr", [P, Q_PAIRS, TOK])
    put("vn", [P, 3, MLA_HEADS * NOPE])
    m["qa"] = m["qr"][:, 0:LT, :]
    t = Space(nc, SBUF_START + KT * TOK * 4)
    m["kn"] = t("kn", [P, 3, MLA_HEADS * NOPE])
    m["t_work"] = t("t_work", [P, 4, TOK])
    m["sq_n"] = t("sq_n", [P, 512])
    assert t.at <= SBUF_START + 3 * KT * TOK * 4
    t = Space(nc, SBUF_START + KT * TOK * 4)
    m["qa_hi"] = t("qa_hi", [P, LT, TOK], F32R)
    m["qa_lo"] = t("qa_lo", [P, LT, TOK], F32R)
    t = Space(nc, SBUF_START + KT * TOK * 4)
    m["q_lat"] = t("q_lat", [P, LT, DEC_BATCH, QROWS])
    m["q_rs"] = t("q_rs", [ROPE, DEC_BATCH, QROWS])
    m["o_lat"] = t("o_lat", [P, LT, MLA_HEADS, N_SAMPLE])
    m["past_t"] = t("past_t", [P, LT + 1, PAGES * P])
    assert t.at <= SBUF_START + 3 * KT * TOK * 4
    ring = SBUF_START + 3 * KT * TOK * 4
    t = Space(nc, ring)
    for e in range(2):
        for name, shape in (("q_s", [P, TOK]), ("k_s", [P, 3, P]), ("v_s", [P, 3, P]), ("k_t", [P, TOK]), ("s", [P, 528]),
                            ("p_t", [P, PAIR_N]), ("mx", [P, 3]), ("sum", [P, 3])):
            m[f"{name}{e}"] = t(f"{name}{e}", shape)
    for name, shape in (("qr_s", [P, TOK]), ("kr_s2", [P, 3, P]), ("kr_t", [P, TOK]), ("att_mask", [P, 528])):
        m[name] = t(name, shape)
    assert t.at <= ring + 6 * UNIT * 4
    t = Space(nc, ring)
    m["past"] = t("past", [P, 2, PAGES, ROW])
    for k in range(2):
        m[f"pt_hi{k}"] = t(f"pt_hi{k}", [P, LATENT], F32R)
        m[f"pt_lo{k}"] = t(f"pt_lo{k}", [P, LATENT], F32R)
    m["rt"] = t("rt", [QROWS, PAGES * P])
    assert t.at <= ring + 6 * UNIT * 4, t.at
    t = Space(nc, m["mla_kept"])
    m["uk_hi"] = t("uk_hi", [P, LT, LT, 512], F32R)
    m["uk_lo"] = t("uk_lo", [P, LT, LT, 512], F32R)
    for name, shape in (("sc", [QROWS, PAGES * P + N_SAMPLE]), ("sq0", [P, 512]), ("pst", [P, PAGES + 1, QROWS]),
                        ("r4", [P, PAGES, DEC_SEQ, MLA_HEADS]), ("ss", [P, PAGES, MLA_HEADS]), ("ssr", [P, PAGES]), ("smx", [QROWS, 2]),
                        ("new_mask", [QROWS, DEC_BATCH, N_SAMPLE]), ("q_ls", [P, LT, QROWS]), ("q_rss", [ROPE, QROWS])):
        m[name] = t(name, shape)


def dense_stage(nc, shared, m, psum, units, n, per, rhs, evac):
    kt = KT // per
    raw_in = [shared.plain(f"raw_in{k}", 16 * ((n + 1 - k) // 2)) for k in range(2)]
    hi_done, lo_done = shared.raised_by("hi_done", 2, n), shared.raised_by("lo_done", 2, n)
    blk_done, blk_out = shared.raised_by("blk_done", 2 * per, n * per), shared.raised_by("blk_evac", 2 * per, n * per)
    raw, w_hi, w_lo = ([m[f"{x}{k}"] for k in range(2)] for x in ("raw", "w_hi", "w_lo"))

    def turns(eng, body):
        if n > 1:
            with eng.Fori(0, n // 2) as i:
                body(i, 0)
                body(i, 1)
        if n % 2:
            body(n // 2, 0)
    with nc.Block() as block:
        @block.sync
        def _(sp):
            def load(i, k):
                lo_done.wait_last_turn(sp, i, k)
                sp.dma_start(raw[k][:], units[bass.ds(2 * i + k, 1)].rearrange("a p n -> (a p) n")).then_inc(raw_in[k][0], 16)
            turns(sp, load)

        @block.scalar
        def _(act):
            hi_done.open(act)

            def high(i, k):
                act.wait_ge(raw_in[k][0], 16 * i + (raw_in[k][1] + 16))
                blk_done.wait_last_turn(act, i, k * per + per - 1)
                nc.scalar.activation(w_hi[k][:], raw[k][:], ACT.Copy).then_inc(hi_done.sem, 1)
            turns(act, high)

        @block.gpsimd
        def _(pool):
            lo_done.open(pool)

            def low(i, k):
                hi_done.wait(pool, i, k)
                nc.gpsimd.tensor_tensor(w_lo[k][:], raw[k][:], w_hi[k][:].bitcast(F32), ALU.subtract).then_inc(lo_done.sem, 1)
            turns(pool, low)

        @block.tensor
        def _(pe):
            blk_done.open(pe)

            def products(i, k):
                lo_done.wait(pe, i, k)
                for b in range(per):
                    c = k * per + b
                    if c >= 2:
                        blk_out.wait(pe, i, c - 2)
                    else:
                        blk_out.wait_last_turn(pe, i, 2 * per + c - 2)
                    for j in range(kt):
                        w = slice((b * kt + j) * P, (b * kt + j + 1) * P)
                        last = mm3(nc, psum[c % 2][:, 0:TOK], (w_hi[k][:, w], w_lo[k][:, w]), rhs(j), j == 0, j == kt - 1)
                    last.then_inc(blk_done.sem, 1)
            turns(pe, products)

        @block.vector
        def _(dve):
            blk_out.open(dve)

            def out(i, k):
                for b in range(per):
                    c = k * per + b
                    blk_done.wait(dve, i, c)
                    evac(i * (2 * per) + c, psum[c % 2]).then_inc(blk_out.sem, 1)
            turns(dve, out)


def latent_norm(nc, shared, m, psum, src, gain, hi, lo):
    (squared, b1), (summed, b2), (rooted, b3), (scaled, b4), (high, b5), (low, b6) = [
        shared.plain(s, n) for s, n in (("squared", 1), ("summed", 1), ("rooted", 2), ("scaled", 1), ("high", 1), ("low", 1))]
    sq, rs = m["raw0"][:, 0:LT * TOK].rearrange("p (k t) -> p k t", k=LT), m["raw1"][:, 0:TOK]
    with nc.Block() as block:
        @block.scalar
        def _(act):
            nc.scalar.activation(sq, src[:], ACT.Square).then_inc(squared, 1)
            act.wait_ge(summed, b2 + 1)
            nc.scalar.activation(rs, psum[0][:, 0:TOK], ACT.Ln, bias=m["eps"][:, 0:1], scale=1.0 / LATENT).then_inc(rooted, 1)
            act.wait_ge(rooted, b3 + 1)
            nc.scalar.activation(rs, rs, ACT.Exp, scale=-0.5).then_inc(rooted, 1)
            act.wait_ge(scaled, b4 + 1)
            nc.scalar.activation(hi[:], src[:], ACT.Copy).then_inc(high, 1)

        @block.tensor
        def _(pe):
            pe.wait_ge(squared, b1 + 1)
            for k in range(LT):
                last = nc.tensor.matmul(psum[0][:, 0:TOK], m["ones"][:], sq[:, k, :], start=k == 0, stop=k == LT - 1)
            last.then_inc(summed, 1)

        @block.vector
        def _(dve):
            dve.wait_ge(rooted, b3 + 2)
            for k in range(LT):
                last = nc.vector.scalar_tensor_tensor(src[:, k, :], src[:, k, :], gain[:, k:k + 1], rs, op0=ALU.mult, op1=ALU.mult)
            last.then_inc(scaled, 1)
            dve.wait_ge(high, b5 + 1)
            nc.vector.tensor_tensor(lo[:], src[:], hi[:].bitcast(F32), ALU.subtract).then_inc(low, 1)
            dve.wait_ge(low, b6 + 1)


def rows_stage(nc, ctx, m, psum, d):
    sem = lambda s: ctx.enter_context(nc.semaphore(f"rows_{s}"))
    turned, v_step, t_done, t_out, stored, sq_done = [sem(s) for s in ("turned", "dve", "transposed", "evac", "stored", "squared")]
    kr, t1, t2 = m["kr"], m["t_work"][:, 0, :], m["t_work"][:, 1, :]
    rows = m["rows_n"]
    with nc.Block() as block:
        @block.tensor
        def _(pe):
            nc.tensor.matmul(psum[6][:, 0:TOK], m["rot"][:], kr[:], start=True, stop=True).then_inc(turned, 1)
            for n, t in enumerate(TILE_ORDER):
                for k in range(LT):
                    nc.tensor.transpose(psum[n][0:TILE_N[t], k * P:(k + 1) * P], m["lat"][:, k, TILE_AT[t]:TILE_AT[t + 1]], m["ident"][:])
                if n == 0:
                    pe.wait_ge(v_step, 3)
                last = nc.tensor.transpose(psum[3 + n][0:TILE_N[t], 0:ROPE], kr[0:ROPE, TILE_AT[t]:TILE_AT[t + 1]], m["ident"][0:ROPE, 0:ROPE])
                last.then_inc(t_done, 1)

        @block.vector
        def _(dve):
            v = Chain(dve, v_step)
            dve.wait_ge(turned, 1)
            v(nc.vector.tensor_tensor(t1, psum[6][:, 0:TOK], m["sin"][:], ALU.mult))
            v(nc.vector.tensor_tensor(t2, kr[:], m["cos"][:], ALU.mult))
            v(nc.vector.tensor_tensor(kr[:], t1, t2, ALU.add))
            for n, t in enumerate(TILE_ORDER):
                r = slice(0, TILE_N[t])
                dve.wait_ge(t_done, n + 1)
                nc.vector.tensor_copy(rows[r, t, 0:LATENT], psum[n][r, :]).then_inc(t_out, 1)
                nc.vector.tensor_copy(rows[r, t, LATENT:ROW], psum[3 + n][r, 0:ROPE]).then_inc(t_out, 1)
            dve.wait_ge(t_out, 6)
            for t in range(3):
                r = slice(0, TILE_N[t])
                v(nc.vector.tensor_tensor(m["t_work"][r, t, 0:ROPE], rows[r, t, LATENT:ROW], rows[r, t, LATENT:ROW], ALU.mult))
                v(nc.vector.tensor_reduce(m["ssr_n"][r, t:t + 1], m["t_work"][r, t, 0:ROPE], AX.X, ALU.add))

        @block.sync
        def _(sp):
            for n, t in enumerate(TILE_ORDER):
                sp.wait_ge(t_out, 2 * n + 2)
                sp.dma_start(d["kv_out"][TILE_AT[t]:TILE_AT[t + 1], :], rows[0:TILE_N[t], t, :]).then_inc(stored, 16)
            sp.wait_ge(stored, 48)


def query_stage(nc, ctx, m, psum):
    sem = lambda s: ctx.enter_context(nc.semaphore(f"query_{s}"))
    turned, roped, squared, summed, rstd_done = [Signal(sem(s), n) for s, n in
                                                 (("turned", 1), ("roped", 1), ("squared", 3), ("summed", 2), ("rstd", 2))]
    normed, v_step, a_step, gains = Signal(sem("normed"), 1), sem("dve"), sem("act"), sem("gains")
    qn, qr, w = m["qn"], m["qr"], m["t_work"]
    qs = m["raw0"][:, 0:TOK]
    t1, t2 = m["raw0"][:, TOK:2 * TOK], m["raw0"][:, 2 * TOK:3 * TOK]
    sq = [m["raw1"][:, k * TOK:(k + 1) * TOK] for k in range(3)]
    rstd = [m["raw1"][:, (3 + k) * TOK:(4 + k) * TOK] for k in range(2)]
    pair = lambda i, e: bass.ds(2 * i + e, 1)
    flat = lambda ap: ap.rearrange("p a t -> p (a t)")
    with nc.Block() as block:
        @block.tensor
        def _(pe):
            turned.open(pe)
            summed.open(pe)
            with pe.Fori(0, Q_PAIRS) as i:
                normed.wait_last_turn(pe, i, 0)
                nc.tensor.matmul(psum[0][:, 0:TOK], m["rot"][:], flat(qr[:, bass.ds(i, 1), :]), start=True, stop=True).then_inc(turned.sem, 1)
                for e in range(2):
                    squared.wait(pe, i, 2)
                    nc.tensor.matmul(psum[1 + e][:, 0:TOK], m["ones"][:], sq[e], start=True, stop=False)
                    nc.tensor.matmul(psum[1 + e][:, 0:TOK], m["half"][:, e, :], sq[2], start=False, stop=True).then_inc(summed.sem, 1)

        @block.scalar
        def _(act):
            squared.open(act)
            rstd_done.open(act)
            c = Chain(act, a_step)
            with act.Fori(0, Q_PAIRS) as i:
                c.turn(i, 2)
                summed.wait_last_turn(act, i, 1)
                for e in range(2):
                    nc.scalar.activation(sq[e], flat(qn[:, pair(i, e), :]), ACT.Square).then_inc(squared.sem, 1)
                roped.wait(act, i, 0)
                nc.scalar.activation(sq[2], qs, ACT.Square).then_inc(squared.sem, 1)
                normed.wait_last_turn(act, i, 0)
                for e in range(2):
                    summed.wait(act, i, e)
                    c(nc.scalar.activation(rstd[e], psum[1 + e][:, 0:TOK], ACT.Ln, bias=m["eps"][:, 0:1], scale=1.0 / QK))
                    nc.scalar.activation(rstd[e], rstd[e], ACT.Exp, scale=-0.5).then_inc(rstd_done.sem, 1)
            c.end(Q_PAIRS)
            for h in range(MLA_HEADS):
                nc.scalar.activation(m["o"][:, h, :], m["o"][:, h, :], ACT.Silu)

        @block.vector
        def _(dve):
            roped.open(dve)
            normed.open(dve)
            v = Chain(dve, v_step)
            g = m["qk_gain"]
            v(nc.vector.tensor_tensor(g[:, 0:1], g[:, 0:1], g[:, 1:2], ALU.mult))
            v(nc.vector.tensor_tensor(g[:, 2:3], g[:, 2:3], g[:, 3:4], ALU.mult))
            v(nc.vector.tensor_scalar(g[:, 0:1], g[:, 0:1], float(QK) ** -0.5, None, ALU.mult))
            v(nc.vector.tensor_scalar(g[:, 2:3], g[:, 2:3], float(QK) ** -0.5, None, ALU.mult))
            with dve.Fori(0, Q_PAIRS) as i:
                v.turn(i, 2)
                turned.wait(dve, i, 0)
                v(nc.vector.tensor_tensor(t1, psum[0][:, 0:TOK], m["sin"][:], ALU.mult))
                v(nc.vector.tensor_tensor(t2, flat(qr[:, bass.ds(i, 1), :]), m["cos"][:], ALU.mult))
                nc.vector.tensor_tensor(qs, t1, t2, ALU.add).then_inc(roped.sem, 1)
                for e in range(2):
                    rstd_done.wait(dve, i, e)
                    q = flat(qn[:, pair(i, e), :])
                    nc.vector.scalar_tensor_tensor(q, q, g[:, 0:1], rstd[e], op0=ALU.mult, op1=ALU.mult)
                    r = slice(64 * e, 64 * e + 64)
                    last = nc.vector.scalar_tensor_tensor(flat(qr[r, bass.ds(i, 1), :]), qs[r, :], g[r, 2:3], rstd[e][r, :], op0=ALU.mult, op1=ALU.mult)
                last.then_inc(normed.sem, 1)
            v.end(Q_PAIRS)


def key_stage(nc, shared, m, psum, d):
    raw_in = [shared.plain(f"raw_in{k}", 16 * 4) for k in range(2)]
    hi_done, lo_done = shared.raised_by("hi_done", 2, 8), shared.raised_by("lo_done", 2, 8)
    blk_done, blk_out = shared.raised_by("blk_done", 6, 24), shared.raised_by("blk_evac", 6, 24)
    raw, w_hi, w_lo = ([m[f"{x}{k}"] for k in range(2)] for x in ("raw", "w_hi", "w_lo"))
    hi, lo = m["lat_hi"], m["lat_lo"]
    with nc.Block() as block:
        @block.sync
        def _(sp):
            with sp.Fori(0, 4) as i:
                for k in range(2):
                    lo_done.wait_last_turn(sp, i, k)
                    sp.dma_start(raw[k][:], d["kv_units"][bass.ds(2 * i + k, 1)].rearrange("a p n -> (a p) n")).then_inc(raw_in[k][0], 16)

        @block.gpsimd
        def _(pool):
            lo_done.open(pool)
            with pool.Fori(0, 4) as i:
                for k in range(2):
                    hi_done.wait(pool, i, k)
                    nc.gpsimd.tensor_tensor(w_lo[k][:], raw[k][:], w_hi[k][:].bitcast(F32), ALU.subtract).then_inc(lo_done.sem, 1)

        @block.scalar
        def _(act):
            hi_done.open(act)
            with act.Fori(0, 4) as i:
                for k in range(2):
                    act.wait_ge(raw_in[k][0], 16 * i + (raw_in[k][1] + 16))
                    blk_done.wait_last_turn(act, i, 3 * k + 2)
                    nc.scalar.activation(w_hi[k][:], raw[k][:], ACT.Copy).then_inc(hi_done.sem, 1)

        @block.tensor
        def _(pe):
            blk_done.open(pe)
            with pe.Fori(0, 4) as i:
                for k in range(2):
                    lo_done.wait(pe, i, k)
                    for n, t in enumerate(TILE_ORDER):
                        c = 3 * k + n
                        blk_out.wait_last_turn(pe, i, c)
                        tok = slice(TILE_AT[t], TILE_AT[t + 1])
                        for j in range(LT):
                            w = slice(j * 512, (j + 1) * 512)
                            last = mm3(nc, psum[c][0:TILE_N[t], :], (hi[:, j, tok], lo[:, j, tok]), (w_hi[k][:, w], w_lo[k][:, w]), j == 0, j == LT - 1)
                        last.then_inc(blk_done.sem, 1)

        @block.vector
        def _(dve):
            blk_out.open(dve)

            def heads(i, k, dst):
                for n, t in enumerate(TILE_ORDER):
                    c, r = 3 * k + n, slice(0, TILE_N[t])
                    blk_done.wait(dve, 2 * which + i, c)
                    nc.vector.tensor_copy(dst[r, t, bass.ds((2 * i + k) * 512, 512)], psum[c][r, :]).then_inc(blk_out.sem, 1)
            for which, dst in enumerate((m["kn"], m["vn"])):
                with dve.Fori(0, 2) as i:
                    heads(i, 0, dst)
                    heads(i, 1, dst)


def key_rms_stage(nc, ctx, m, psum):
    sem = lambda s: ctx.enter_context(nc.semaphore(f"krms_{s}"))
    v_step, squared, reduced, a_step, rep_done, t_done = [sem(s) for s in ("dve", "squared", "reduced", "act", "rep", "transposed")]
    sq = m["sq_n"]
    rep = m["t_work"][0:N_SAMPLE, 0, 0:QROWS]
    with nc.Block() as block:
        @block.scalar
        def _(act):
            n = 0
            for t in range(3):
                r = slice(0, TILE_N[t])
                for u in range(4):
                    if n:
                        act.wait_ge(reduced, n)
                    nc.scalar.activation(sq[r, :], m["kn"][r, t, u * 512:(u + 1) * 512], ACT.Square).then_inc(squared, 1)
                    n += 1
            act.wait_ge(v_step, 3)
            for t in range(3):
                r = slice(0, TILE_N[t])
                nc.scalar.activation(m["r_n"][r, t, :], m["ss_n"][r, t, :], ACT.Ln, bias=m["eps"][r, 0:1], scale=1.0 / QK).then_inc(a_step, 1)
            act.wait_ge(a_step, 3)
            for t in range(3):
                r = slice(0, TILE_N[t])
                nc.scalar.activation(m["r_n"][r, t, :], m["r_n"][r, t, :], ACT.Exp, scale=-0.5).then_inc(a_step, 1)

        @block.vector
        def _(dve):
            v = Chain(dve, v_step)
            n = 0
            for t in range(3):
                r = slice(0, TILE_N[t])
                for u in range(4):
                    dve.wait_ge(squared, n + 1)
                    nc.vector.tensor_reduce(m["ss_n"][r, t, 4 * u:4 * u + 4], sq[r, :].rearrange("p (h d) -> p h d", h=4), AX.X, ALU.add).then_inc(reduced, 1)
                    n += 1
            dve.wait_ge(reduced, n)
            for t in range(3):
                r = slice(0, TILE_N[t])
                v(nc.vector.tensor_scalar(m["ss_n"][r, t, :], m["ss_n"][r, t, :], m["ssr_n"][r, t:t + 1], None, ALU.add))
            dve.wait_ge(a_step, 6)
            nc.vector.tensor_copy(rep.rearrange("p (t h) -> p t h", h=MLA_HEADS),
                                  m["r_n"][0:N_SAMPLE, 0:1, :].to_broadcast([N_SAMPLE, DEC_SEQ, MLA_HEADS])).then_inc(rep_done, 1)
            dve.wait_ge(t_done, 1)
            v(nc.vector.tensor_copy(m["r_new"][:], psum[0][0:QROWS, 0:N_SAMPLE]))

        @block.tensor
        def _(pe):
            pe.wait_ge(rep_done, 1)
            nc.tensor.transpose(psum[0][0:QROWS, 0:N_SAMPLE], rep, m["ident"][0:N_SAMPLE, 0:N_SAMPLE]).then_inc(t_done, 1)


def q_lat_stage(nc, shared, m, psum, d):
    raw_in = [shared.plain(f"raw_in{k}", 16 * 2) for k in range(2)]
    ql_done, ql_out = shared.raised_by("blk_done", 2, 4), shared.raised_by("blk_evac", 2, 4)
    ropes, ropes_base = shared.plain("copied", 1)
    raw = [m["raw0"], m["raw1"]]
    with nc.Block() as block:
        @block.sync
        def _(sp):
            with sp.Fori(0, 2) as i:
                for k in range(2):
                    ql_done.wait_last_turn(sp, i, k)
                    sp.dma_start(raw[k][:], d["ukt_units"][bass.ds(2 * i + k, 1)].rearrange("a p n -> (a p) n")).then_inc(raw_in[k][0], 16)

        @block.tensor
        def _(pe):
            ql_done.open(pe)
            with pe.Fori(0, 2) as i:
                for k in range(2):
                    pe.wait_ge(raw_in[k][0], 16 * i + (raw_in[k][1] + 16))
                    ql_out.wait_last_turn(pe, i, k)
                    for hh in range(4):
                        for lb in range(LT):
                            last = nc.tensor.matmul(psum[6 + k][:, (hh * LT + lb) * N_SAMPLE:(hh * LT + lb + 1) * N_SAMPLE],
                                                    raw[k][:, hh * 512 + lb * P:hh * 512 + (lb + 1) * P],
                                                    m["qn"][:, bass.ds(8 * i + 4 * k + hh, 1), 0:N_SAMPLE].rearrange("p a t -> p (a t)"), start=True, stop=True)
                    last.then_inc(ql_done.sem, 1)

        @block.vector
        def _(dve):
            ql_out.open(dve)
            with dve.Fori(0, 2) as i:
                for k in range(2):
                    ql_done.wait(dve, i, k)
                    for hh in range(4):
                        src = psum[6 + k][:, hh * P:(hh + 1) * P].rearrange("p (l t) -> p l t", l=LT)
                        dst = m["q_lat"][:].rearrange("p l b (t h) -> p l (b t) h", h=MLA_HEADS)[:, :, :, bass.ds(8 * i + 4 * k + hh, 1)].rearrange("p l t a -> p l (t a)")
                        last = nc.vector.tensor_copy(dst, src)
                    last.then_inc(ql_out.sem, 1)
            for e in range(2):
                src = m["qr"][64 * e:64 * e + 64, :, 0:N_SAMPLE].rearrange("p h t -> p t h")
                dst = m["q_rs"][:].rearrange("p b (t h) -> p (b t) h", h=MLA_HEADS)[:, :, e:MLA_HEADS:2]
                last = nc.vector.tensor_copy(dst, src)
            nc.vector.tensor_copy(m["lat_s"][:], m["lat"][:, :, 0:N_SAMPLE])
            nc.vector.tensor_copy(m["kr_s"][:], m["kr"][0:ROPE, 0:N_SAMPLE])
            nc.vector.tensor_copy(m["rows_s"][:], m["rows_n"][0:N_SAMPLE, 0, 0:LATENT]).then_inc(ropes, 1)
            dve.wait_ge(ropes, ropes_base + 1)


def prompt_attention_stage(nc, ctx, m, psum, d):
    sem = lambda s: ctx.enter_context(nc.semaphore(f"pa_{s}"))
    sig = lambda s, per: Signal(sem(s), per)
    mask_in = sem("mask_in")
    kr_staged, q_staged, v_staged, k_staged = sig("kr_staged", 1), sig("q_staged", 2), sig("v_staged", 2), sig("k_staged", 2)
    k_turned, kr_turned, kt_out, krt_out = sig("k_turned", 2), sig("kr_turned", 1), sig("kt_out", 2), sig("krt_out", 1)
    s_done, s_out, mx_done, exp_done, p_done = sig("s_done", 4), sig("s_out", 4), sig("mx_done", 2), sig("exp_done", 2), sig("p_done", 2)
    pt_done, pt_out, o_done, o_out = sig("pt_done", 4), sig("pt_out", 4), sig("o_done", 2), sig("o_out", 2)
    v_step, passed = sem("dve"), sem("passed")
    two = lambda n: [m[f"{n}{e}"] for e in range(2)]
    q_s, k_s, v_s, k_t, s_, p_t, mx, sm = (two(n) for n in ("q_s", "k_s", "v_s", "k_t", "s", "p_t", "mx", "sum"))
    qr_s, kr_s, kr_t = m["qr_s"], m["kr_s2"], m["kr_t"]
    S_AT, S_N = (0, 48, 224), (48, 176, 304)
    KT_, KRT, SL, SH, PL, PH, O = psum[0], psum[1], psum[2], psum[3], psum[4], psum[5], psum[6]
    rows = lambda t: slice(0, TILE_N[t])
    toks = lambda t: slice(TILE_AT[t], TILE_AT[t + 1])
    flat = lambda ap: ap.rearrange("p a t -> p (a t)")
    with nc.Block() as block:
        @block.sync
        def _(sp):
            sp.dma_start(m["att_mask"][:], d["att_mask"]).then_inc(mask_in, 16)
            sp.wait_ge(mask_in, 16)

        @block.gpsimd
        def _(pool):
            for s in (v_staged, q_staged):
                s.open(pool)
            with pool.Fori(0, Q_PAIRS) as i:
                for e in range(2):
                    h = 2 * i + e
                    s_done.wait_last_turn(pool, i, 2 * e + 1)
                    if e == 0:
                        s_done.wait_last_turn(pool, i, 3)
                        nc.gpsimd.tensor_copy(qr_s[:], flat(m["qr"][:, bass.ds(i, 1), :]))
                    nc.gpsimd.tensor_copy(q_s[e][:], flat(m["qn"][:, bass.ds(h, 1), :])).then_inc(q_staged.sem, 1)
                    o_done.wait_last_turn(pool, i, e)
                    nc.gpsimd.tensor_copy(v_s[e][rows(0), 0, :], m["vn"][rows(0), 0, bass.ds(h * P, P)])
                    nc.gpsimd.tensor_copy(v_s[e][:, 1:3, :], m["vn"][:, 1:3, bass.ds(h * P, P)]).then_inc(v_staged.sem, 1)

        @block.tensor
        def _(pe):
            for s in (k_turned, kr_turned, s_done, pt_done, o_done):
                s.open(pe)
            with pe.Fori(0, Q_PAIRS) as i:
                def keys(e):
                    if e == 0:
                        kr_staged.wait(pe, i, 0)
                        krt_out.wait_last_turn(pe, i, 0)
                        for t in TILE_ORDER:
                            last = nc.tensor.transpose(KRT[:, toks(t)], kr_s[rows(t), t, :], m["ident"][rows(t), rows(t)])
                        last.then_inc(kr_turned.sem, 1)
                        kt_out.wait_last_turn(pe, i, 1)
                    else:
                        kt_out.wait(pe, i, 0)
                    k_staged.wait(pe, i, e)
                    for t in TILE_ORDER:
                        last = nc.tensor.transpose(KT_[:, toks(t)], k_s[e][rows(t), t, :], m["ident"][rows(t), rows(t)])
                    last.then_inc(k_turned.sem, 1)

                def scores(e):
                    if e == 0:
                        krt_out.wait(pe, i, 0)
                    kt_out.wait(pe, i, e)
                    q_staged.wait(pe, i, e)
                    half = slice(64 * e, 64 * e + 64)
                    for bank, tiles, at in ((SL, (1, 0), S_AT), (SH, (2,), (0, 0, 0))):
                        n = 2 * e + (bank is SH)
                        if n >= 2:
                            s_out.wait(pe, i, n - 2)
                        else:
                            s_out.wait_last_turn(pe, i, n + 2)
                        for t in tiles:
                            dst = bank[rows(t), at[t]:at[t] + S_N[t]]
                            nc.tensor.matmul(dst, q_s[e][:, toks(t)], k_t[e][:, 0:S_N[t]], start=True, stop=False)
                            last = nc.tensor.matmul(dst, qr_s[half, toks(t)], kr_t[half, 0:S_N[t]], start=False, stop=True)
                        last.then_inc(s_done.sem, 1)

                def turns(e):
                    p_done.wait(pe, i, e)
                    for bank, pairs, n in ((PH, ((1, 1, 0), (1, 2, 128), (2, 2, 256)), 2 * e), (PL, ((0, 1, 48), (0, 2, 176), (0, 0, 0)), 2 * e + 1)):
                        if n >= 2:
                            pt_out.wait(pe, i, n - 2)
                        else:
                            pt_out.wait_last_turn(pe, i, n + 2)
                        pe.sem_inc(passed, 1)
                        for kt, qt, at in pairs:
                            last = nc.tensor.transpose(bank[rows(kt), at:at + TILE_N[qt]],
                                                       s_[e][rows(qt), S_AT[qt] + TILE_AT[kt]:S_AT[qt] + TILE_AT[kt + 1]],
                                                       m["ident"][rows(qt), rows(qt)])
                        last.then_inc(pt_done.sem, 1)
                    v_staged.wait(pe, i, e)
                    pt_out.wait(pe, i, 2 * e)
                    pt_out.wait(pe, i, 2 * e + 1)
                    if e:
                        o_out.wait(pe, i, 0)
                    else:
                        o_out.wait_last_turn(pe, i, 1)
                    pt = p_t[e]
                    nc.tensor.matmul(O[:, 48:TOK], v_s[e][:, 1, :], pt[:, 304:560], start=True, stop=False)
                    nc.tensor.matmul(O[:, 176:TOK], v_s[e][:, 2, :], pt[:, 560:688], start=False, stop=False)
                    nc.tensor.matmul(O[:, 48:TOK], v_s[e][rows(0), 0, :], pt[rows(0), 48:304], start=False, stop=False)
                    nc.tensor.matmul(O[:, 0:48], v_s[e][rows(0), 0, :], pt[rows(0), 0:48], start=False, stop=True).then_inc(o_done.sem, 1)
                keys(0)
                scores(0)
                keys(1)
                scores(1)
                turns(0)
                turns(1)

        @block.scalar
        def _(act):
            for s in (kt_out, krt_out, exp_done, pt_out):
                s.open(act)
            with act.Fori(0, Q_PAIRS) as i:
                def keys(e):
                    if e == 0:
                        kr_turned.wait(act, i, 0)
                        s_done.wait_last_turn(act, i, 3)
                        nc.scalar.activation(kr_t[:], KRT[:, 0:TOK], ACT.Copy).then_inc(krt_out.sem, 1)
                    k_turned.wait(act, i, e)
                    s_done.wait_last_turn(act, i, 2 * e + 1)
                    nc.scalar.activation(k_t[e][:], KT_[:, 0:TOK], ACT.Copy).then_inc(kt_out.sem, 1)

                def exps(e):
                    mx_done.wait(act, i, e)
                    for t in range(3):
                        at = s_[e][rows(t), S_AT[t]:S_AT[t] + S_N[t]]
                        last = nc.scalar.activation(at, at, ACT.Exp, bias=mx[e][rows(t), t:t + 1], accum_out=sm[e][rows(t), t:t + 1])
                    last.then_inc(exp_done.sem, 1)

                def turned(e):
                    o_done.wait_last_turn(act, i, e)
                    pt_done.wait(act, i, 2 * e)
                    nc.scalar.activation(p_t[e][:, 304:688], PH[:, 0:384], ACT.Copy).then_inc(pt_out.sem, 1)
                    pt_done.wait(act, i, 2 * e + 1)
                    nc.scalar.activation(p_t[e][rows(0), 0:304], PL[rows(0), 0:304], ACT.Copy).then_inc(pt_out.sem, 1)
                keys(0)
                keys(1)
                exps(0)
                exps(1)
                turned(0)
                turned(1)

        @block.vector
        def _(dve):
            for s in (kr_staged, k_staged, s_out, mx_done, p_done, o_out):
                s.open(dve)
            v = Chain(dve, v_step)
            dve.wait_ge(mask_in, 16)
            with dve.Fori(0, Q_PAIRS) as i:
                v.turn(i, 4)

                def stage(e):
                    if e == 0:
                        kr_turned.wait_last_turn(dve, i, 0)
                        for t in range(3):
                            for ee in range(2):
                                last = nc.vector.tensor_scalar(kr_s[rows(t), t, 64 * ee:64 * ee + 64], m["rows_n"][rows(t), t, LATENT:ROW],
                                                               m["r_n"][rows(t), t, bass.ds(2 * i + ee, 1)], None, ALU.mult)
                        last.then_inc(kr_staged.sem, 1)
                    k_turned.wait_last_turn(dve, i, e)
                    for t in range(3):
                        last = nc.vector.tensor_scalar(k_s[e][rows(t), t, :], m["kn"][rows(t), t, bass.ds((2 * i + e) * P, P)],
                                                       m["r_n"][rows(t), t, bass.ds(2 * i + e, 1)], None, ALU.mult)
                    last.then_inc(k_staged.sem, 1)

                def masked(e):
                    pt_done.wait_last_turn(dve, i, 2 * e + 1)
                    for n, (bank, tiles, at) in enumerate(((SL, (1, 0), S_AT), (SH, (2,), (0, 0, 0)))):
                        s_done.wait(dve, i, 2 * e + n)
                        for t in tiles:
                            c = slice(S_AT[t], S_AT[t] + S_N[t])
                            last = nc.vector.tensor_tensor(s_[e][rows(t), c], bank[rows(t), at[t]:at[t] + S_N[t]], m["att_mask"][rows(t), c], ALU.add)
                        last.then_inc(s_out.sem, 1)
                    s_out.wait(dve, i, 2 * e + 1)
                    for t in range(3):
                        last = nc.vector.tensor_reduce(mx[e][rows(t), t:t + 1], s_[e][rows(t), S_AT[t]:S_AT[t] + S_N[t]], AX.X, ALU.max, negate=True)
                    last.then_inc(mx_done.sem, 1)

                def normed(e):
                    exp_done.wait(dve, i, e)
                    v(nc.vector.reciprocal(sm[e][rows(0), 0:1], sm[e][rows(0), 0:1]))
                    v(nc.vector.reciprocal(sm[e][:, 1:3], sm[e][:, 1:3]))
                    for t in range(3):
                        at = s_[e][rows(t), S_AT[t]:S_AT[t] + S_N[t]]
                        last = nc.vector.tensor_scalar(at, at, sm[e][rows(t), t:t + 1], None, ALU.mult)
                    last.then_inc(p_done.sem, 1)

                def gated(e):
                    o_done.wait(dve, i, e)
                    o = flat(m["o"][:, bass.ds(2 * i + e, 1), N_SAMPLE:TOK])
                    nc.vector.tensor_tensor(o, o, O[:, N_SAMPLE:TOK], ALU.mult).then_inc(o_out.sem, 1)
                stage(0)
                stage(1)
                masked(0)
                masked(1)
                normed(0)
                normed(1)
                gated(0)
                gated(1)
            v.end(Q_PAIRS)


def sample_attention_stage(nc, ctx, m, psum, d):
    sem = lambda s: ctx.enter_context(nc.semaphore(f"sa_{s}"))
    sig = lambda s, per: Signal(sem(s), per)
    BODY = 2
    uk_in, tab_in, uk_hi_done, uk_lo_done = [sem(s) for s in ("uk_in", "tab_in", "uk_hi", "uk_lo")]
    seq_in = [sem(f"seq_in{u}") for u in range(BODY)]
    N = BODY * PAGES
    t_done, t_hi, t_f32, kr_out, t_lo = sig("t_done", N), sig("t_hi", N), sig("t_f32", N), sig("kr_out", N), sig("t_lo", N)
    k_done, sq_out = sig("k_done", 4 * N), sig("sq_out", 4 * N)
    red = sig("red", 4 * N)
    r_done, r_turned, r_out = sig("r_done", BODY), sig("r_turned", BODY), sig("r_out", 2 * BODY)
    q_staged, s_done, s_out, s_max, s_exp = sig("q_staged", BODY), sig("s_done", 3 * BODY), sig("s_out", 2 * BODY), sig("s_max", BODY), sig("s_exp", BODY)
    p_turned, p_out, o_done, o_scaled, o_turned, o_out = (sig(s, BODY) for s in ("p_turned", "p_out", "o_done", "o_scaled", "o_turned", "o_out"))
    v_step, a_step, passed = sem("dve"), sem("act"), sem("passed")
    past, past_t = m["past"], m["past_t"]
    pt_hi, pt_lo = ([m[f"{n}{k}"] for k in range(2)] for n in ("pt_hi", "pt_lo"))
    uk_hi, uk_lo, sc, rt, sq = m["uk_hi"], m["uk_lo"], m["sc"], m["rt"], m["sq0"]
    PT, PK, KN, SA, SB = psum[0], psum[1], psum[2:6], psum[6], psum[7]
    NEW = PAGES * P
    seq = lambda i, u: BODY * i + u
    stage = m["past"][:].rearrange("p a b c -> p (a b c)")[:, 0:LT * UNIT].rearrange("p (u n) -> p u n", u=LT)
    with nc.Block() as block:
        @block.sync
        def _(sp):
            sp.dma_start(stage, d["kv_units"][0:LT].rearrange("u p n -> p u n")).then_inc(uk_in, 16)
            sp.dma_start(m["table"][:], d["table"]).then_inc(tab_in, 16)
            sp.dma_start(m["new_mask"][:], d["new_mask"]).then_inc(tab_in, 16)
            sp.wait_ge(tab_in, 32)
            sp.wait_ge(uk_lo_done, LT)
            with sp.Fori(0, DEC_BATCH // BODY) as i:
                for u in range(BODY):
                    o_done.wait_last_turn(sp, i, u)
                    for k in range(PAGES):
                        page = sp.value_load(m["table"][0:1, bass.ds(seq(i, u) * PAGES + k, 1)], min_val=0, max_val=d["cache"].shape[0] - 1)
                        sp.dma_start(past[:, u, k, :], d["cache"][bass.ds(page, 1)].rearrange("a p n -> (a p) n")).then_inc(seq_in[u], 16)

        @block.gpsimd
        def _(pool):
            t_lo.open(pool)
            with pool.Fori(0, DEC_BATCH // BODY) as i:
                for u in range(BODY):
                    for k in range(PAGES):
                        n = u * PAGES + k
                        t_hi.wait(pool, i, n)
                        t_f32.wait(pool, i, n)
                        nc.gpsimd.tensor_tensor(pt_lo[k % 2][:].rearrange("p (l t) -> p l t", l=LT), past_t[:, 0:LT, k * P:(k + 1) * P],
                                                pt_hi[k % 2][:].bitcast(F32).rearrange("p (l t) -> p l t", l=LT), ALU.subtract).then_inc(t_lo.sem, 1)

        @block.scalar
        def _(act):
            act.wait_ge(uk_in, 16)
            for u in range(LT):
                nc.scalar.activation(uk_hi[:, u].rearrange("p l n -> p (l n)"), stage[:, u, :], ACT.Copy).then_inc(uk_hi_done, 1)
            for s in (t_hi, kr_out, sq_out, r_done, s_exp, p_out):
                s.open(act)
            c = Chain(act, a_step)
            with act.Fori(0, DEC_BATCH // BODY) as i:
                c.turn(i, BODY * 1)
                for u in range(BODY):
                    def split(k):
                        n = u * PAGES + k
                        t_done.wait(act, i, n)
                        if n >= 2:
                            k_done.wait(act, i, 4 * (n - 2) + 3)
                        else:
                            k_done.wait_last_turn(act, i, 4 * (N + n - 2) + 3)
                        nc.scalar.activation(pt_hi[k % 2][:], PT[:, :], ACT.Copy).then_inc(t_hi.sem, 1)
                        if k == 0:
                            if u:
                                s_done.wait(act, i, 3 * u - 1)
                            else:
                                s_done.wait_last_turn(act, i, 3 * BODY - 1)
                        nc.scalar.activation(past_t[0:ROPE, LT, k * P:(k + 1) * P], PK[0:ROPE, 0:P], ACT.Copy).then_inc(kr_out.sem, 1)

                    def squares(k):
                        n = u * PAGES + k
                        for c4 in range(4):
                            k_done.wait(act, i, 4 * n + c4)
                            if 4 * n + c4 >= 1:
                                red.wait(act, i, 4 * n + c4 - 1)
                            else:
                                red.wait_last_turn(act, i, 4 * N - 1)
                            nc.scalar.activation(sq[:], KN[c4][:, :], ACT.Square).then_inc(sq_out.sem, 1)
                    split(0)
                    for k in range(PAGES):
                        if k + 1 < PAGES:
                            split(k + 1)
                        squares(k)
                    q_staged.wait(act, i, u)
                    c(nc.scalar.activation(m["ss"][:], m["ss"][:], ACT.Ln, bias=m["eps"][:, 0:1], scale=1.0 / QK))
                    if u:
                        r_turned.wait(act, i, u - 1)
                    else:
                        r_turned.wait_last_turn(act, i, BODY - 1)
                    for t in range(DEC_SEQ):
                        last = nc.scalar.activation(m["r4"][:, :, t, :], m["ss"][:], ACT.Exp, scale=-0.5)
                    last.then_inc(r_done.sem, 1)
                    s_max.wait(act, i, u)
                    nc.scalar.activation(sc[:], sc[:], ACT.Exp, bias=m["smx"][:, 0:1], accum_out=m["smx"][:, 1:2]).then_inc(s_exp.sem, 1)
                    p_turned.wait(act, i, u)
                    if u:
                        o_done.wait(act, i, u - 1)
                    else:
                        o_done.wait_last_turn(act, i, BODY - 1)
                    nc.scalar.activation(m["pst"][:, 0:PAGES, :].rearrange("p k q -> p (k q)"), SA[:, :], ACT.Copy)
                    nc.scalar.activation(m["pst"][0:N_SAMPLE, PAGES, :], SB[0:N_SAMPLE, 0:QROWS], ACT.Copy).then_inc(p_out.sem, 1)
            c.end(DEC_BATCH // BODY)

        @block.tensor
        def _(pe):
            for s in (t_done, k_done, r_turned, s_done, p_turned, o_done, o_turned):
                s.open(pe)
            pe.wait_ge(uk_lo_done, LT)
            with pe.Fori(0, DEC_BATCH // BODY) as i:
                def turn_page(u, k):
                    n = u * PAGES + k
                    if k == 0:
                        pe.wait_ge(seq_in[u], 16 * PAGES * (i + 1))
                    if n:
                        t_f32.wait(pe, i, n - 1)
                        t_hi.wait(pe, i, n - 1)
                        kr_out.wait(pe, i, n - 1)
                    else:
                        t_f32.wait_last_turn(pe, i, N - 1)
                        t_hi.wait_last_turn(pe, i, N - 1)
                        kr_out.wait_last_turn(pe, i, N - 1)
                    if k == 0:
                        if u:
                            s_out.wait(pe, i, 2 * u - 1)
                        else:
                            s_out.wait_last_turn(pe, i, 2 * BODY - 1)
                    for l in range(LT):
                        nc.tensor.transpose(PT[:, l * P:(l + 1) * P], past[:, u, k, l * P:(l + 1) * P], m["ident"][:])
                    nc.tensor.transpose(PK[0:ROPE, 0:P], past[:, u, k, LATENT:ROW], m["ident"][:]).then_inc(t_done.sem, 1)

                def keys(u, k):
                    n = u * PAGES + k
                    t_lo.wait(pe, i, n)
                    for c4 in range(4):
                        if n:
                            sq_out.wait(pe, i, 4 * (n - 1) + c4)
                        else:
                            sq_out.wait_last_turn(pe, i, 4 * (N - 1) + c4)
                        for l in range(LT):
                            a = slice(l * P, (l + 1) * P)
                            last = mm3(nc, KN[c4][:, :], (pt_hi[k % 2][:, a], pt_lo[k % 2][:, a]), (uk_hi[:, c4, l, :], uk_lo[:, c4, l, :]), l == 0, l == LT - 1)
                        last.then_inc(k_done.sem, 1)

                def attend(u):
                    r_done.wait(pe, i, u)
                    if u:
                        o_out.wait(pe, i, u - 1)
                    else:
                        o_out.wait_last_turn(pe, i, BODY - 1)
                    pe.sem_inc(passed, 1)
                    for k in range(PAGES):
                        last = nc.tensor.transpose((SA, SB)[k // 4][0:QROWS, (k % 4) * P:(k % 4 + 1) * P], m["r4"][:, k].rearrange("p t h -> p (t h)"), m["ident"][:])
                    last.then_inc(r_turned.sem, 1)
                    q_staged.wait(pe, i, u)
                    for half, bank in enumerate((SA, SB)):
                        r_out.wait(pe, i, 2 * u + half)
                        cols = slice(half * 512, half * 512 + 512)
                        for l in range(LT):
                            nc.tensor.matmul(bank[0:QROWS, :], m["q_ls"][:, l, :], past_t[:, l, cols], start=l == 0, stop=False)
                        nc.tensor.matmul(bank[0:QROWS, :], m["q_rss"][:], past_t[0:ROPE, LT, cols], start=False, stop=True).then_inc(s_done.sem, 1)
                    kr_out.wait(pe, i, u * PAGES + PAGES - 1)
                    for l in range(LT):
                        nc.tensor.matmul(PK[0:QROWS, 0:N_SAMPLE], m["q_ls"][:, l, :], m["lat_s"][:, l, :], start=l == 0, stop=False)
                    nc.tensor.matmul(PK[0:QROWS, 0:N_SAMPLE], m["q_rss"][:], m["kr_s"][:], start=False, stop=True).then_inc(s_done.sem, 1)
                    s_exp.wait(pe, i, u)
                    pe.sem_inc(passed, 1)
                    for k in range(PAGES):
                        nc.tensor.transpose(SA[:, k * QROWS:(k + 1) * QROWS], sc[:, k * P:(k + 1) * P], m["ident"][0:QROWS, 0:QROWS])
                    nc.tensor.transpose(SB[0:N_SAMPLE, 0:QROWS], sc[:, NEW:NEW + N_SAMPLE], m["ident"][0:QROWS, 0:QROWS]).then_inc(p_turned.sem, 1)
                    p_out.wait(pe, i, u)
                    for k in range(PAGES):
                        nc.tensor.matmul(SB[0:QROWS, :], m["pst"][:, k, :], past[:, u, k, 0:LATENT], start=k == 0, stop=False)
                    nc.tensor.matmul(SB[0:QROWS, :], m["pst"][0:N_SAMPLE, PAGES, :], m["rows_s"][:], start=False, stop=True).then_inc(o_done.sem, 1)
                    o_scaled.wait(pe, i, u)
                    pe.sem_inc(passed, 1)
                    for l in range(LT):
                        last = nc.tensor.transpose(SA[:, l * QROWS:(l + 1) * QROWS], sc[:, l * P:(l + 1) * P], m["ident"][0:QROWS, 0:QROWS])
                    last.then_inc(o_turned.sem, 1)
                for u in range(BODY):
                    turn_page(u, 0)
                    for k in range(PAGES):
                        if k + 1 < PAGES:
                            turn_page(u, k + 1)
                        keys(u, k)
                    attend(u)

        @block.vector
        def _(dve):
            for u in range(LT):
                dve.wait_ge(uk_hi_done, u + 1)
                nc.vector.tensor_tensor(uk_lo[:, u].rearrange("p l n -> p (l n)"), stage[:, u, :], uk_hi[:, u].bitcast(F32).rearrange("p l n -> p (l n)"), ALU.subtract).then_inc(uk_lo_done, 1)
            for s in (t_f32, red, q_staged, r_out, s_out, s_max, o_scaled, o_out):
                s.open(dve)
            v = Chain(dve, v_step)
            dve.wait_ge(tab_in, 32)
            with dve.Fori(0, DEC_BATCH // BODY) as i:
                v.turn(i, BODY * 5)
                for u in range(BODY):
                    def reduces(k):
                        n = u * PAGES + k
                        for c4 in range(4):
                            sq_out.wait(dve, i, 4 * n + c4)
                            nc.vector.tensor_reduce(m["ss"][:, k, 4 * c4:4 * c4 + 4], sq[:].rearrange("p (h d) -> p h d", h=4), AX.X, ALU.add).then_inc(red.sem, 1)
                    if u:
                        r_turned.wait(dve, i, u - 1)
                    else:
                        r_turned.wait_last_turn(dve, i, BODY - 1)

                    def turned(k):
                        n = u * PAGES + k
                        t_done.wait(dve, i, n)
                        t_hi.wait(dve, i, n)
                        nc.vector.tensor_copy(past_t[:, 0:LT, k * P:(k + 1) * P], PT[:, :].rearrange("p (l t) -> p l t", l=LT)).then_inc(t_f32.sem, 1)
                    turned(0)
                    for k in range(PAGES):
                        if k + 1 < PAGES:
                            turned(k + 1)
                        reduces(k)
                    dve.wait_ge(seq_in[u], 16 * PAGES * (i + 1))
                    red.wait(dve, i, 4 * (u + 1) * PAGES - 1)
                    kr = past[:, u, :, LATENT:ROW]
                    tmp = m["sq0"][:].rearrange("p (k c) -> p k c", k=PAGES)
                    v(nc.vector.tensor_tensor(tmp, kr, kr, ALU.mult))
                    v(nc.vector.tensor_reduce(m["ssr"][:], tmp, AX.X, ALU.add))
                    v(nc.vector.tensor_tensor(m["ss"][:], m["ss"][:], m["ssr"][:].rearrange("p (k a) -> p k a", a=1).to_broadcast([P, PAGES, MLA_HEADS]), ALU.add))
                    nc.vector.tensor_copy(m["q_ls"][:], m["q_lat"][:, :, bass.ds(seq(i, u), 1), :].rearrange("p l a q -> p l (a q)"))
                    nc.vector.tensor_copy(m["q_rss"][:], m["q_rs"][:, bass.ds(seq(i, u), 1), :].rearrange("p a q -> p (a q)")).then_inc(q_staged.sem, 1)
                    r_turned.wait(dve, i, u)
                    for half, bank in enumerate((SA, SB)):
                        nc.vector.tensor_copy(rt[:, half * 512:half * 512 + 512], bank[0:QROWS, :]).then_inc(r_out.sem, 1)
                    for half, bank in enumerate((SA, SB)):
                        s_done.wait(dve, i, 3 * u + half)
                        cols = slice(half * 512, half * 512 + 512)
                        nc.vector.tensor_tensor(sc[:, cols], bank[0:QROWS, :], rt[:, cols], ALU.mult)
                    s_done.wait(dve, i, 3 * u + 2)
                    v(nc.vector.tensor_tensor(sc[:, NEW:NEW + N_SAMPLE], PK[0:QROWS, 0:N_SAMPLE], m["r_new"][:], ALU.mult))
                    nc.vector.tensor_tensor(sc[:, NEW:NEW + N_SAMPLE], sc[:, NEW:NEW + N_SAMPLE],
                                            m["new_mask"][:, bass.ds(seq(i, u), 1), :].rearrange("p a t -> p (a t)"), ALU.add).then_inc(s_out.sem, 2)
                    s_out.wait(dve, i, 2 * u + 1)
                    nc.vector.tensor_reduce(m["smx"][:, 0:1], sc[:], AX.X, ALU.max, negate=True).then_inc(s_max.sem, 1)
                    s_exp.wait(dve, i, u)
                    v(nc.vector.reciprocal(m["smx"][:, 1:2], m["smx"][:, 1:2]))
                    o_done.wait(dve, i, u)
                    nc.vector.tensor_scalar(sc[:, 0:LATENT], SB[0:QROWS, :], m["smx"][:, 1:2], None, ALU.mult).then_inc(o_scaled.sem, 1)
                    o_turned.wait(dve, i, u)
                    for l in range(LT):
                        dst = m["o_lat"][:, l].rearrange("p h (b t) -> p b t h", t=DEC_SEQ)[:, bass.ds(seq(i, u), 1)].rearrange("p a t h -> p (a t) h")
                        last = nc.vector.tensor_copy(dst, SA[:, l * QROWS:(l + 1) * QROWS].rearrange("p (t h) -> p t h", h=MLA_HEADS))
                    last.then_inc(o_out.sem, 1)
            v.end(DEC_BATCH // BODY)


def sample_value_stage(nc, shared, m, psum, d):
    raw_in = [shared.plain(f"raw_in{k}", 16 * 2) for k in range(2)]
    v_done, v_out = shared.raised_by("blk_done", 2, 4), shared.raised_by("blk_evac", 2, 4)
    (high, high_base), (low, low_base) = shared.plain("hi_done", 4), shared.plain("lo_done", 4)
    raw = [m["raw0"], m["raw1"]]
    with nc.Block() as block:
        @block.sync
        def _(sp):
            with sp.Fori(0, 2) as i:
                for k in range(2):
                    v_done.wait_last_turn(sp, i, k)
                    sp.dma_start(raw[k][:], d["kv_units"][bass.ds(2 * i + k + 4, 1)].rearrange("a p n -> (a p) n")).then_inc(raw_in[k][0], 16)

        @block.tensor
        def _(pe):
            v_done.open(pe)
            with pe.Fori(0, 2) as i:
                for k in range(2):
                    pe.wait_ge(raw_in[k][0], 16 * i + (raw_in[k][1] + 16))
                    v_out.wait_last_turn(pe, i, k)
                    for hh in range(4):
                        for l in range(LT):
                            last = nc.tensor.matmul(psum[k][:, hh * N_SAMPLE:(hh + 1) * N_SAMPLE], raw[k][:, l * 512 + hh * P:l * 512 + (hh + 1) * P],
                                                    m["o_lat"][:, l, bass.ds(8 * i + 4 * k + hh, 1), :].rearrange("p a t -> p (a t)"), start=l == 0, stop=l == LT - 1)
                    last.then_inc(v_done.sem, 1)

        @block.vector
        def _(dve):
            v_out.open(dve)
            with dve.Fori(0, 2) as i:
                for k in range(2):
                    v_done.wait(dve, i, k)
                    o = m["o"][:, bass.ds(8 * i + 4 * k, 4), 0:N_SAMPLE]
                    nc.vector.tensor_tensor(o, o, psum[k][:, 0:4 * N_SAMPLE].rearrange("p (h t) -> p h t", h=4), ALU.mult).then_inc(v_out.sem, 1)
            for h in range(4):
                c = slice(4 * h, 4 * h + 4)
                dve.wait_ge(high, high_base + h + 1)
                nc.vector.tensor_tensor(m["h_lo"][:, c, :], m["o"][:, c, :], m["h_hi"][:, c, :].bitcast(F32), ALU.subtract).then_inc(low, 1)
            dve.wait_ge(low, low_base + 4)

        @block.scalar
        def _(act):
            v_out.wait(act, 1, 1)
            for h in range(4):
                c = slice(4 * h, 4 * h + 4)
                nc.scalar.activation(m["h_hi"][:, c, :], m["o"][:, c, :], ACT.Copy).then_inc(high, 1)


def store_stage(nc, ctx, m, d):
    stored = ctx.enter_context(nc.semaphore("y_stored"))
    with nc.Block() as block:
        @block.sync
        def _(sp):
            sp.dma_start(d["y_out"], m["x"][:]).then_inc(stored, 16)
            sp.wait_ge(stored, 16)


def load_mla_consts(nc, ctx, m, d):
    loaded = ctx.enter_context(nc.semaphore("mla_loaded"))
    names = ("rot", "half", "cos", "sin", "mla_gain", "qk_gain")
    with nc.Block() as block:
        @block.sync
        def _(sp):
            for name in names:
                sp.dma_start(m[name][:], d[name]).then_inc(loaded, 16)
            sp.wait_ge(loaded, 16 * len(names))


def build(nc, d):
    from contextlib import ExitStack
    with ExitStack() as ctx:
        m = memory(nc)
        psum = [ctx.enter_context(nc.psum_tensor(f"bank{i}", [P, 512], F32)) for i in range(8)]
        norms, latents, dense = (Shared(nc, ctx, kind) for kind in ("norm", "latent", "dense"))
        load_stage(nc, ctx, m, d)
        norm_stage(nc, norms, m, psum, 0)
        dt_stage(nc, ctx, m, psum, d)
        mamba_stage(nc, ctx, m, psum, d)
        memory_mla(nc, m)
        load_mla_consts(nc, ctx, m, d)
        flat = lambda ap: ap.rearrange("p a t -> p (a t)")
        h = lambda j: (m["h_hi"][:, j, :], m["h_lo"][:, j, :])
        norm_stage(nc, norms, m, psum, 1)
        dense_stage(nc, dense, m, psum, d["kva_units"], LT, 1, h,
                    lambda c, bank: nc.vector.tensor_copy(flat(m["lat"][:, bass.ds(c, 1), :]), bank[:, 0:TOK]))
        dense_stage(nc, dense, m, psum, d["kvr_unit"], 1, 1, h,
                    lambda c, bank: nc.vector.tensor_copy(m["kr"][:], bank[:, 0:TOK]))
        latent_norm(nc, latents, m, psum, m["lat"], m["mla_gain"][:, 0, :], m["lat_hi"], m["lat_lo"])
        rows_stage(nc, ctx, m, psum, d)
        norm_stage(nc, norms, m, psum, 2)
        dense_stage(nc, dense, m, psum, d["qa_units"], LT, 1, h,
                    lambda c, bank: nc.vector.tensor_copy(flat(m["qa"][:, bass.ds(c, 1), :]), bank[:, 0:TOK]))
        dense_stage(nc, dense, m, psum, d["gate_units"], MLA_HEADS, 1, h,
                    lambda c, bank: nc.vector.tensor_copy(flat(m["o"][:, bass.ds(c, 1), :]), bank[:, 0:TOK]))
        latent_norm(nc, latents, m, psum, m["qa"], m["mla_gain"][:, 1, :], m["qa_hi"], m["qa_lo"])
        qa = lambda j: (m["qa_hi"][:, j, :], m["qa_lo"][:, j, :])
        dense_stage(nc, dense, m, psum, d["qn_units"], 4, 4, qa,
                    lambda c, bank: nc.vector.tensor_copy(flat(m["qn"][:, bass.ds(c, 1), :]), bank[:, 0:TOK]))
        dense_stage(nc, dense, m, psum, d["qr_units"], 2, 4, qa,
                    lambda c, bank: nc.vector.tensor_copy(flat(m["qr"][:, bass.ds(c, 1), :]), bank[:, 0:TOK]))
        query_stage(nc, ctx, m, psum)
        key_stage(nc, dense, m, psum, d)
        key_rms_stage(nc, ctx, m, psum)
        prompt_attention_stage(nc, ctx, m, psum, d)
        q_lat_stage(nc, dense, m, psum, d)
        sample_attention_stage(nc, ctx, m, psum, d)
        sample_value_stage(nc, dense, m, psum, d)
        dense_stage(nc, dense, m, psum, d["o_units"], KT, 1, h,
                    lambda c, bank: nc.vector.tensor_tensor(flat(m["x"][:, bass.ds(c, 1), :]), flat(m["x"][:, bass.ds(c, 1), :]), bank[:, 0:TOK], ALU.add))
        store_stage(nc, ctx, m, d)


def tables():
    mask = np.zeros((P, PAIR_N), np.float32)
    col = np.arange(TOK)
    for t in range(3):
        j = TILE_AT[t] + np.arange(TILE_N[t])[:, None]
        i = col[None, TILE_AT[t]:]
        sample = (j < N_SAMPLE) & (i < N_SAMPLE) & (i // DEC_SEQ == j // DEC_SEQ) & (j <= i)
        prompt = (j >= N_SAMPLE) & (i >= N_SAMPLE) & (j <= i)
        mask[:TILE_N[t], PAIR_AT[t]:PAIR_AT[t + 1]] = sample | prompt
    diag = (np.arange(N_SAMPLE)[:, None] // DEC_SEQ == np.arange(DEC_BATCH)[None]).astype(np.float32)
    rot = np.zeros((P, P), np.float32)
    for at in (0, ROPE):
        for c in range(ROPE // 2):
            rot[at + ROPE // 2 + c, at + c] = -1.0
            rot[at + c, at + ROPE // 2 + c] = 1.0
    half = np.zeros((P, 2, P), np.float32)
    half[:ROPE, 0] = 1.0
    half[ROPE:, 1] = 1.0
    pos = np.concatenate([np.tile(PAGES * P + np.arange(DEC_SEQ), DEC_BATCH), np.arange(T_PROMPT)]).astype(np.float32)
    inv = (1.0 / (np.float32(10000.0) ** (np.arange(0, ROPE, 2, dtype=np.float32) / ROPE))).astype(np.float32)
    angle = np.tile((pos[:, None] * inv[None, :]).T, (4, 1))
    none = np.float32(-1e30)
    att = np.full((P, 528), none, np.float32)
    for t, at, n in ((0, 0, 48), (1, 48, 176), (2, 224, 304)):
        q, k = TILE_AT[t] + np.arange(TILE_N[t])[:, None], np.arange(n)[None]
        att[:TILE_N[t], at:at + n] = np.where((k >= N_SAMPLE) & (k <= q), np.float32(0), none)
    q, b, k = np.arange(QROWS)[:, None, None] // MLA_HEADS, np.arange(DEC_BATCH)[None, :, None], np.arange(N_SAMPLE)[None, None]
    new = np.where((k // DEC_SEQ == b) & (k % DEC_SEQ <= q), np.float32(0), none).astype(np.float32)
    return {"rot": rot, "half": half, "cos": np.cos(angle).astype(np.float32), "sin": np.sin(angle).astype(np.float32), "att_mask": att, "new_mask": new, "ident": np.eye(P, dtype=np.float32), "ones": np.ones((P, P), np.float32), "eps": np.full((P, 1), EPS, np.float32),
            "mask": mask, "diag": diag}


def lay_out(inp):
    a = {k: np.asarray(v) for k, v in inp.items()}
    blocks = lambda v: v.reshape(-1, P).T
    d = dict(tables())
    x = np.concatenate([a["x_sample"].reshape(N_SAMPLE, D_MODEL), a["meta_tokens"], a["x_prompt"][0]], 0)
    d["x"] = x.T.reshape(KT, P, TOK).transpose(1, 0, 2)
    d["norms"] = np.stack([blocks(a["a_norm"][0]), blocks(a["kv_norm"]), blocks(a["b_norm"][0])], 1)
    w = a["a_w_in"][0]
    d["narrow"] = w[:, D_INNER + 6144:].reshape(KT, P, HD).transpose(1, 0, 2).reshape(P, KT * HD)
    tile = lambda cols: cols.reshape(KT, P, P).transpose(1, 0, 2).reshape(P, UNIT)
    units = []
    for g in range(GROUPS):
        at = [D_INNER + g * GW + p * P for p in range(PAIRS)] + [2 * D_INNER + g * P, 2 * D_INNER + 1024 + g * P] + [g * GW + p * P for p in range(PAIRS)]
        units += [tile(w[:, c:c + P]) for c in at]
        rows = a["a_w_out"][0][g * GW:(g + 1) * GW].reshape(PAIRS, P, OUT_UNITS, 4, P)
        units += [rows[:, :, k].transpose(1, 2, 0, 3).reshape(P, UNIT) for k in range(OUT_UNITS)]
    d["a_units"] = np.stack(units)

    def conv_order(v):
        v = v.reshape(v.shape[:-1] + (48, P))
        order = [[4 * g + p for p in range(PAIRS)] + [32 + g, 40 + g] for g in range(GROUPS)]
        v = v[..., np.array(order), :]
        return np.moveaxis(np.moveaxis(v, -1, 0), (-2, -1), (1, 2))
    d["conv_w"] = conv_order(a["a_conv_w"][0])
    d["conv_b"] = conv_order(a["a_conv_b"][0])
    d["conv_old"] = conv_order(a["state_conv"][0])
    d["d_skip"] = blocks(np.repeat(a["a_D"][0], HD)).reshape(P, GROUPS, PAIRS)
    d["gate_norm"] = blocks(a["a_gate_norm"][0]).reshape(P, GROUPS, PAIRS)
    d["dt_bias"] = a["a_dt_bias"][0][:, None]
    d["a_log"] = a["a_A_log"][0][:, None]
    two = lambda v: np.concatenate([v, v])
    d["mla_gain"] = np.stack([blocks(a["kv_a_norm"]), blocks(a["b_q_a_norm"][0])], 1)
    qg, kg = a["b_q_norm"][0], a["k_norm"]
    d["qk_gain"] = np.stack([qg[:NOPE], kg[:NOPE], two(qg[NOPE:]), two(kg[NOPE:])], 1)
    kva = a["w_kv_a"]
    d["kva_units"] = np.stack([tile(kva[:, k * P:(k + 1) * P]) for k in range(LT)])
    d["kvr_unit"] = tile(np.concatenate([kva[:, LATENT:]] * 2, 1))[None]
    w = a["b_w_in"][0]
    d["qa_units"] = np.stack([tile(w[:, k * P:(k + 1) * P]) for k in range(LT)])
    d["gate_units"] = np.stack([tile(w[:, LATENT + k * P:LATENT + (k + 1) * P]) for k in range(MLA_HEADS)])
    wq = a["b_w_q"][0].reshape(LT, P, MLA_HEADS, QK)

    def quads(blk):
        return blk.transpose(2, 1, 0, 3).reshape(-1, 4, P, LT * P).transpose(0, 2, 1, 3).reshape(-1, P, UNIT)
    d["qn_units"] = quads(wq[..., :NOPE])
    d["qr_units"] = quads(wq[..., NOPE:].reshape(LT, P, Q_PAIRS, P))
    kv = [a[n].reshape(LT, P, 4, 512).transpose(2, 1, 0, 3).reshape(4, P, UNIT) for n in ("w_uk", "w_uv")]
    d["kv_units"] = np.concatenate(kv)
    d["ukt_units"] = a["w_uk"].transpose(1, 2, 0).reshape(4, 4, P, LATENT).transpose(0, 2, 1, 3).reshape(4, P, UNIT)
    d["o_units"] = np.stack([tile(a["b_w_out"][0][:, k * P:(k + 1) * P]) for k in range(KT)])
    d["cache"] = a["cache_kv"]
    d["table"] = a["page_table"].reshape(1, -1)
    d["state_in"] = a["state_ssm"][0].reshape(DEC_BATCH, D_INNER, STATE)
    return {k: np.ascontiguousarray(v) for k, v in d.items()}


OUTS = {"state_out": (DEC_BATCH, D_INNER, STATE), "sp_out": (GROUPS, P, PAIRS, STATE),
        "conv_out": (P, GROUPS, CONV_BLK, DEC_BATCH + 1, 3), "y_out": (P, KT, TOK), "kv_out": (TOK, 576)}


def kernel(**inputs):
    import concourse.bacc as bacc
    from concourse.bass_utils import run_bass_kernel_spmd as run

    nc = bacc.Bacc("TRN2", target_bir_lowering=False, num_devices=1)
    arrays = {f"in_{k}": v for k, v in lay_out(inputs).items()}
    d = {k[3:]: nc.dram_tensor(k, v.shape, mybir.dt.from_np(v.dtype), kind="ExternalInput").ap() for k, v in arrays.items()}
    for k, shape in OUTS.items():
        d[k] = nc.dram_tensor(f"out_{k}", shape, F32, kind="ExternalOutput").ap()
    build(nc, d)
    r = run(nc, [arrays], core_ids=[0]).results[0]
    got = {k: r[f"out_{k}"] for k in OUTS}
    y = got["y_out"].transpose(1, 0, 2).reshape(D_MODEL, TOK).T
    conv = got["conv_out"]
    back = np.empty((9, 3, 48, P), np.float32)
    for g in range(GROUPS):
        for k, blk in enumerate([4 * g + p for p in range(PAIRS)] + [32 + g, 40 + g]):
            back[:, :, blk] = conv[:, g, k].transpose(1, 2, 0)
    back = back.reshape(9, 3, 6144)
    sp = got["sp_out"].transpose(0, 2, 1, 3).reshape(1, 1, HEADS, HD, STATE)
    kv = got["kv_out"]
    return (y[N_SAMPLE + N_META:][None], y[:N_SAMPLE].reshape(DEC_BATCH, DEC_SEQ, D_MODEL), sp, back[8][None, None],
            kv[N_SAMPLE:][None], got["state_out"].reshape(1, DEC_BATCH, HEADS, HD, STATE), back[:8][None],
            kv[:N_SAMPLE].reshape(DEC_BATCH, DEC_SEQ, 576))
```

```python
import concourse.bass as bass
import numpy as np
from concourse import mybir
from concourse.alu_op_type import AluOpType as ALU

F32 = mybir.dt.float32
F32R = mybir.dt.float32r
I32 = mybir.dt.int32
ACT = mybir.ActivationFunctionType
AX = mybir.AxisListType

P = 128
D_MODEL, D_INNER = 2048, 4096
KT = D_MODEL // P
N_SAMPLE, N_META, SEQ = 32, 16, 256
DEC_BATCH, DEC_SEQ = 8, 4
TOK = N_SAMPLE + N_META + SEQ
T_PROMPT = TOK - N_SAMPLE
TILE_AT = (0, 48, 176, 304)
TILE_N = (48, 128, 128)
TILE_ORDER = (1, 2, 0)
PAIR_AT = (0, 304, 560, 688)
PAIR_N = PAIR_AT[3]
GROUPS, HEADS, HPG, HD, STATE = 8, 64, 8, 64, 128
PAIRS = HPG // 2
GW = HPG * HD
CONV_BLK = PAIRS + 2
CB = DEC_BATCH * (3 + DEC_SEQ) + 3 + T_PROMPT
CO = CB - 3
IN_UNITS, OUT_UNITS = 10, 4
UNITS = IN_UNITS + OUT_UNITS
UNIT = KT * P
HALVES = (slice(0, UNIT // 2), slice(UNIT // 2, UNIT))
EPS = 1e-6
SBUF_START, SBUF_END = 16512, 229344


class Signal:

    def __init__(self, sem, per, base=0):
        self.sem, self.per, self.base = sem, per, base

    def open(self, eng):
        eng.sem_inc(self.sem, self.per)

    def wait(self, eng, turn, k):
        eng.wait_ge(self.sem, self.per * turn + (self.base + self.per + k + 1))

    def wait_last_turn(self, eng, turn, k):
        eng.wait_ge(self.sem, self.per * turn + (self.base + k + 1))


class Shared:

    def __init__(self, nc, ctx, kind):
        self.sem_of = lambda name: ctx.enter_context(nc.semaphore(f"{kind}_{name}"))
        self.sems, self.raised = {}, {}

    def plain(self, name, total):
        if name not in self.sems:
            self.sems[name], self.raised[name] = self.sem_of(name), 0
        base = self.raised[name]
        self.raised[name] += total
        return self.sems[name], base

    def raised_by(self, name, per, raises):
        sem, base = self.plain(name, per + raises)
        return Signal(sem, per, base)


class Chain:

    def __init__(self, eng, sem):
        self.eng, self.sem, self.base, self.n = eng, sem, 0, 0

    def turn(self, turn, per):
        self.start, self.base, self.n, self.per = self.base + self.n, None, 0, per
        self.at = turn * per + self.start

    def __call__(self, ins):
        ins.then_inc(self.sem, 1)
        self.n += 1
        if self.base is None:
            self.eng.wait_ge(self.sem, self.at + self.n)
        else:
            self.eng.wait_ge(self.sem, self.base + self.n)

    def end(self, turns):
        assert self.n == self.per, (self.n, self.per)
        self.base, self.n = self.start + turns * self.per, 0


class Space:

    def __init__(self, nc, at):
        self.nc, self.at = nc, at

    def __call__(self, name, shape, dtype=F32):
        size = int(np.prod(shape[1:])) * 4
        t = self.nc.alloc_sbuf_tensor_at(name, shape, dtype, offset=self.at)
        self.at += -(-size // 32) * 32
        assert self.at <= SBUF_END, (name, self.at)
        return t


def mm3(nc, out, a, b, start, stop):
    nc.tensor.matmul(out, a[0], b[0], start=start, stop=False)
    nc.tensor.matmul(out, a[0], b[1], start=False, stop=False)
    return nc.tensor.matmul(out, a[1], b[0], start=False, stop=stop)


def memory(nc):
    m = {}
    s = Space(nc, SBUF_START)

    def put(name, shape, dtype=F32):
        m[name] = s(name, shape, dtype)

    put("x", [P, KT, TOK])
    put("h_hi", [P, KT, TOK], F32R)
    put("h_lo", [P, KT, TOK], F32R)
    for k in range(2):
        put(f"raw{k}", [P, UNIT])
        put(f"w_hi{k}", [P, UNIT], F32R)
        put(f"w_lo{k}", [P, UNIT], F32R)
    put("ident", [P, P])
    put("ones", [P, P])
    put("eps", [P, 1])
    put("norms", [P, 3, KT])
    m["common_end"] = s.at
    put("mask", [P, PAIR_N])
    put("diag", [N_SAMPLE, DEC_BATCH])
    put("conv_w", [P, GROUPS, CONV_BLK, 4])
    put("conv_b", [P, GROUPS, CONV_BLK])
    put("conv_old", [P, GROUPS, CONV_BLK, DEC_BATCH, 3])
    put("conv_new", [P, GROUPS, CONV_BLK, DEC_BATCH + 1, 3])
    put("d_skip", [P, GROUPS, PAIRS])
    put("gate_norm", [P, GROUPS, PAIRS])
    put("dt_bias", [HEADS, 1])
    put("a_log", [HEADS, 1])
    put("cumT", [HEADS, TOK])
    put("dt_n", [P, 3, HEADS])
    put("cum_n", [P, 3, HEADS])
    put("wp_n", [P, 3, HEADS])
    put("ws_n", [N_SAMPLE, HEADS])
    put("sel", [HEADS, HPG])
    put("gate", [P, PAIRS, TOK])
    put("cbuf0", [P, CB])
    put("cbuf1", [P, CB])
    put("cacc0", [P, CO])
    put("cacc1", [P, CO])
    put("xc", [P, CONV_BLK, TOK])
    put("xdt", [P, 3, GW])
    put("xwp", [P, 3, GW])
    put("xws", [N_SAMPLE, GW])
    put("b_n", [P, 3, STATE])
    put("b_diag", [N_SAMPLE, DEC_BATCH, STATE])
    put("cb", [P, PAIR_N])
    m["sel_wide"] = nc.alloc_sbuf_tensor_at("sel_wide", [HEADS, HPG, HD], F32, offset=s.at)
    put("dec0", [P, PAIR_N])
    put("dec1", [P, PAIR_N])
    put("mix0", [P, PAIR_N])
    put("mix1", [P, PAIR_N])
    put("y", [P, PAIRS, TOK])
    put("s_in0", [P, DEC_BATCH, STATE])
    put("s_in1", [P, DEC_BATCH, STATE])
    put("s_out", [P, DEC_BATCH, STATE])
    at_s_t = s.at
    put("s_t", [P, DEC_BATCH, P])
    m["narrow"] = nc.alloc_sbuf_tensor_at("narrow", [P, KT * HD], F32, offset=at_s_t)
    put("e_cum", [P, PAIRS, N_SAMPLE])
    put("tmp32", [P, N_SAMPLE])
    put("y_hi", [P, PAIRS, TOK], F32R)
    put("y_lo", [P, PAIRS, TOK], F32R)
    put("y_rstd", [P, TOK])
    put("sp_out", [P, PAIRS, STATE])
    m["mamba_end"] = s.at
    m["y_sq"] = m["gate"]
    return m


def load_stage(nc, ctx, m, d):
    sem = lambda n: ctx.enter_context(nc.semaphore(n))
    loaded, x_loaded = sem("consts_loaded"), sem("x_loaded")
    small = ["ident", "ones", "eps", "norms", "narrow", "mask", "diag", "conv_w", "conv_b", "conv_old",
             "d_skip", "gate_norm", "dt_bias", "a_log"]
    with nc.Block() as block:
        @block.sync
        def _(sp):
            sp.dma_start(m["x"][:], d["x"]).then_inc(x_loaded, 16)
            sp.wait_ge(x_loaded, 16)

        @block.scalar
        def _(act):
            for name in small:
                act.dma_start(m[name][:], d[name]).then_inc(loaded, 16)
            act.wait_ge(loaded, 16 * len(small))


def norm_stage(nc, shared, m, psum, which):
    (squared, b1), (summed, b2), (rooted, b3), (scaled, b4), (high, b5), (low, b6) = [
        shared.plain(s, n) for s, n in (("squared", KT), ("summed", KT), ("rooted", 2), ("scaled", KT), ("high", KT), ("low", KT))]
    x, hi, lo, ones = m["x"], m["h_hi"], m["h_lo"], m["ones"]
    sq = [m["raw0"], m["raw1"]]
    ln, rs = (m[f"raw{k}"][:, 2 * TOK:3 * TOK] for k in range(2))
    with nc.Block() as block:
        @block.scalar
        def _(act):
            for k in range(KT):
                if k >= 2:
                    act.wait_ge(summed, b2 + k - 1)
                nc.scalar.activation(sq[k % 2][:, 0:TOK], x[:, k, :], ACT.Square).then_inc(squared, 1)
            act.wait_ge(summed, b2 + KT)
            nc.scalar.activation(ln, psum[0][:, 0:TOK], ACT.Ln, bias=m["eps"][:, 0:1], scale=1.0 / D_MODEL).then_inc(rooted, 1)
            act.wait_ge(rooted, b3 + 1)
            nc.scalar.activation(rs, ln, ACT.Exp, scale=-0.5).then_inc(rooted, 1)
            for k in range(KT):
                act.wait_ge(scaled, b4 + k + 1)
                nc.scalar.activation(hi[:, k, :], sq[k % 2][:, TOK:2 * TOK], ACT.Copy).then_inc(high, 1)

        @block.tensor
        def _(pe):
            for k in range(KT):
                pe.wait_ge(squared, b1 + k + 1)
                nc.tensor.matmul(psum[0][:, 0:TOK], ones[:], sq[k % 2][:, 0:TOK], start=k == 0,
                                 stop=k == KT - 1).then_inc(summed, 1)

        @block.vector
        def _(dve):
            dve.wait_ge(rooted, b3 + 2)
            for k in range(KT):
                if k >= 2:
                    dve.wait_ge(low, b6 + k - 1)
                    dve.wait_ge(high, b5 + k - 1)
                nc.vector.scalar_tensor_tensor(sq[k % 2][:, TOK:2 * TOK], x[:, k, :], m["norms"][:, which, k:k + 1],
                                               rs, op0=ALU.mult, op1=ALU.mult).then_inc(scaled, 1)
                dve.wait_ge(high, b5 + k + 1)
                nc.vector.tensor_tensor(lo[:, k, :], sq[k % 2][:, TOK:2 * TOK], hi[:, k, :].bitcast(F32),
                                        ALU.subtract).then_inc(low, 1)
            dve.wait_ge(low, b6 + KT)


def dt_stage(nc, ctx, m, psum, d):
    sem = lambda n: ctx.enter_context(nc.semaphore(f"dt_{n}"))
    split, proj, a_step, v_step, t_done, t_out = [sem(n) for n in ("split", "proj", "act", "dve", "transposed", "out")]
    w_hi, w_lo = m["w_hi0"], m["w_lo0"]
    N = KT * HD
    raw = m["narrow"]
    half = lambda name, k: m[name][0:HEADS, k * TOK:(k + 1) * TOK]
    xb, ab, dt, da = half("mix0", 0), half("mix0", 1), half("mix1", 0), half("mix1", 1)
    wp, ws = half("dec0", 0), half("dec0", 1)[:, 0:N_SAMPLE]
    neg_a, seq_a = m["y_rstd"][0:HEADS, 0:1], m["y_rstd"][0:HEADS, 1:2]
    one_row = half("dec1", 0)
    cum = m["cumT"]
    by_seq = lambda ap: ap.rearrange("p (b t) -> p b t", t=DEC_SEQ)
    V_CUM = 10
    with nc.Block() as block:
        @block.scalar
        def _(act):
            c = Chain(act, a_step)
            nc.scalar.activation(w_hi[:, 0:N], raw[:, 0:N], ACT.Copy).then_inc(split, 1)
            c(nc.scalar.activation(seq_a, m["a_log"][:, 0:1], ACT.Exp))
            act.wait_ge(proj, 1)
            nc.scalar.activation(xb, psum[0][0:HEADS, 0:TOK], ACT.Identity, bias=m["dt_bias"][:, 0:1]).then_inc(a_step, 1)
            c.n += 1
            act.wait_ge(a_step, c.n)
            c(nc.scalar.activation(ab, xb, ACT.Abs))
            c(nc.scalar.activation(ab, ab, ACT.Exp, scale=-1.0))
            c(nc.scalar.activation(ab, ab, ACT.Ln, bias=1.0))
            act.wait_ge(v_step, V_CUM)
            nc.scalar.activation(wp[:, N_SAMPLE:TOK], cum[:, N_SAMPLE:TOK], ACT.Exp, scale=-1.0,
                                 bias=cum[:, TOK - 1:TOK]).then_inc(a_step, 1)
            act.wait_ge(v_step, V_CUM + 1)
            nc.scalar.activation(ws, ws, ACT.Exp).then_inc(a_step, 1)

        @block.vector
        def _(dve):
            v = Chain(dve, v_step)
            dve.wait_ge(split, 1)
            nc.vector.tensor_tensor(w_lo[:, 0:N], raw[:, 0:N], w_hi[:, 0:N].bitcast(F32), ALU.subtract).then_inc(split, 1)
            v(nc.vector.memset(one_row, 1.0))
            v(nc.vector.memset(wp, 0.0))
            dve.wait_ge(a_step, 5)
            v(nc.vector.scalar_tensor_tensor(dt, xb, 0.0, ab, op0=ALU.max, op1=ALU.add))
            v(nc.vector.tensor_scalar(neg_a, seq_a, -1.0, None, ALU.mult))
            v(nc.vector.tensor_scalar(da, dt, neg_a, None, ALU.mult))
            v(nc.vector.tensor_tensor_scan(cum[:, N_SAMPLE:TOK], one_row[:, N_SAMPLE:TOK], da[:, N_SAMPLE:TOK],
                                           0.0, ALU.mult, ALU.add))
            cs, ds = by_seq(cum[:, 0:N_SAMPLE]), by_seq(da[:, 0:N_SAMPLE])
            v(nc.vector.tensor_copy(cs[:, :, 0:1], ds[:, :, 0:1]))
            for t in range(1, DEC_SEQ):
                v(nc.vector.tensor_tensor(cs[:, :, t:t + 1], cs[:, :, t - 1:t], ds[:, :, t:t + 1], ALU.add))
            assert v.n == V_CUM
            v(nc.vector.tensor_tensor(by_seq(ws), cs[:, :, DEC_SEQ - 1:DEC_SEQ].to_broadcast([HEADS, DEC_BATCH, DEC_SEQ]), cs, ALU.subtract))
            dve.wait_ge(a_step, 7)
            v(nc.vector.tensor_tensor(wp, wp, dt, ALU.mult))
            v(nc.vector.tensor_tensor(ws, ws, dt[:, 0:N_SAMPLE], ALU.mult))
            for n, (name, where) in enumerate((("dt_n", 1), ("cum_n", 2), ("wp_n", 3))):
                dve.wait_ge(t_done, 3 * n + 3)
                for t in range(3):
                    nc.vector.tensor_copy(m[name][0:TILE_N[t], t, :],
                                          psum[where][0:TILE_N[t], t * HEADS:(t + 1) * HEADS]).then_inc(t_out, 1)
            dve.wait_ge(t_done, 10)
            nc.vector.tensor_copy(m["ws_n"][:], psum[4][0:N_SAMPLE, 0:HEADS]).then_inc(t_out, 1)
            v(nc.vector.tensor_scalar(m["y_hi"][:], m["h_hi"][:, 0:PAIRS, :].bitcast(F32), 0.0, None, ALU.mult))
            v(nc.vector.tensor_scalar(m["y_lo"][:], m["h_hi"][:, 0:PAIRS, :].bitcast(F32), 0.0, None, ALU.mult))
            for k in range(2):
                v(nc.vector.memset(m[f"cbuf{k}"][:], 0.0))

        @block.tensor
        def _(pe):
            pe.wait_ge(split, 2)
            for k in range(KT):
                last = mm3(nc, psum[0][0:HEADS, 0:TOK], (w_hi[:, k * HD:(k + 1) * HD], w_lo[:, k * HD:(k + 1) * HD]),
                           (m["h_hi"][:, k, :], m["h_lo"][:, k, :]), k == 0, k == KT - 1)
            last.then_inc(proj, 1)
            pe.wait_ge(v_step, 13)
            eye = m["ident"][0:HEADS, 0:HEADS]
            for src, where in ((dt, 1), (cum, 2), (wp, 3)):
                for t in range(3):
                    nc.tensor.transpose(psum[where][0:TILE_N[t], t * HEADS:(t + 1) * HEADS],
                                        src[:, TILE_AT[t]:TILE_AT[t + 1]], eye).then_inc(t_done, 1)
            nc.tensor.transpose(psum[4][0:N_SAMPLE, 0:HEADS], ws, eye).then_inc(t_done, 1)


def mamba_stage(nc, ctx, m, psum, d):
    def sig(name, per):
        return Signal(ctx.enter_context(nc.semaphore("m_" + name)), per)
    sem = lambda n: ctx.enter_context(nc.semaphore("m_" + n))
    raw_in = [sem("raw_in0"), sem("raw_in1")]
    s_loaded = [sem("s_loaded0"), sem("s_loaded1")]
    lo_done, hi_done = sig("lo_done", 2 * UNITS), sig("hi_done", 2 * UNITS)
    blk_done = sig("blk_done", IN_UNITS + 4 * OUT_UNITS)
    in_out, out_out = sig("in_evac", IN_UNITS), sig("out_evac", 16)
    conv_done, conv_saved, xc_done = sig("conv_done", CONV_BLK), sig("conv_saved", CONV_BLK), sig("xc_done", CONV_BLK)
    sel_set = sig("sel_set", 2)
    cb_done, cb_out = sig("cb_done", 2), sig("cb_evac", 2)
    bn_done, bn_out, bd_done = sig("bn_done", 1), sig("bn_evac", 2), sig("bd_done", 1)
    xn_done, xn_out = sig("xn_done", 3), sig("xn_evac", 3)
    ec_done, ec_out = sig("ec_done", 1), sig("ec_evac", 1)
    cum_done, dec_done, mix_done = sig("cum_done", HPG), sig("dec_done", HPG), sig("mix_done", HPG)
    cum_read = sig("cum_read", HPG)
    y_done, y_out, sq_done = sig("y_done", HPG), sig("y_evac", PAIRS), sig("sq_done", PAIRS)
    st_done, st_out = sig("st_done", 2 * PAIRS), sig("st_evac", 2 * PAIRS)
    ys_done, up_done, up_out = sig("ys_done", PAIRS), sig("up_done", 2 * PAIRS), sig("up_evac", 2 * PAIRS)
    sp_done, sp_evac = sig("sp_done", 1), sig("sp_evac", 1)
    s_stored = sem("s_stored")
    sp_stored, conv_stored = sem("sp_stored"), sem("conv_stored")
    norm_done, rstd_done = sig("norm_done", 1), sig("rstd_done", 1)
    yn_done, yhi_done, ylo_done = sig("yn_done", 1), sig("yhi_done", 1), sig("ylo_done", 1)
    dve_step, act_step = sem("dve_step"), sem("act_step")

    raw, w_hi, w_lo = ([m[f"{n}{k}"] for k in range(2)] for n in ("raw", "w_hi", "w_lo"))
    cbuf, cacc, s_in = ([m[f"{n}{k}"] for k in range(2)] for n in ("cbuf", "cacc", "s_in"))
    s_out = m["s_out"]
    dec, mix = ([m[f"{n}{k}"] for k in range(2)] for n in ("dec", "mix"))
    xc, x = m["xc"], m["x"]
    xB, xC = 4, 5
    DENSE = psum[0:2]
    BN, CUM, Y, SA, SB = psum[2], psum[3:5], psum[5], psum[6], psum[7]
    XN = psum[3:6]
    by_seq = lambda ap, n: ap[:, 0:DEC_BATCH * n].rearrange("p (b t) -> p b t", t=n)

    with nc.Block() as block:
        @block.sync
        def _(sp):
            def unit(g, k):
                if k >= 2:
                    lo_done.wait(sp, g, 2 * (k - 2) + 1)
                sp.dma_start(raw[k % 2][:], d["a_units"][bass.ds(g * UNITS + k, 1)].rearrange("a p n -> (a p) n")).then_inc(raw_in[k % 2], 16)
            unit(0, 0)
            unit(0, 1)
            with sp.Fori(0, GROUPS) as g:
                def state_in(p):
                    if p >= 2:
                        up_out.wait(sp, g, 2 * (p - 2) + 1)
                    else:
                        up_out.wait_last_turn(sp, g, 2 * (p + 2) + 1)
                    sp.dma_start(s_in[p % 2][:], d["state_in"][:, bass.ds(g * GW + p * P, P), :].rearrange("b p n -> p b n")).then_inc(s_loaded[p % 2], 16)

                def state_out(p):
                    up_out.wait(sp, g, 2 * p + 1)
                    sp.dma_start(d["state_out"][:, bass.ds(g * GW + p * P, P), :].rearrange("b p n -> p b n"), s_out[:]).then_inc(s_stored, 16)
                for k in range(2, UNITS):
                    unit(g, k)
                    if k == 3:
                        state_in(0)
                    if k == 5:
                        state_in(1)
                state_in(2)
                state_out(0)
                unit(g, UNITS)
                state_out(1)
                state_in(3)
                unit(g, UNITS + 1)
                state_out(2)
                state_out(3)
                sp_evac.wait(sp, g, 0)
                sp.dma_start(d["sp_out"][bass.ds(g, 1)].rearrange("a p j n -> (a p) j n"), m["sp_out"][:]).then_inc(sp_stored, 16)
            unit(GROUPS, 2)
            unit(GROUPS, 3)
            conv_saved.wait(sp, GROUPS - 1, CONV_BLK - 1)
            sp.dma_start(d["conv_out"], m["conv_new"][:]).then_inc(conv_stored, 16)
            sp.wait_ge(s_stored, 16 * (PAIRS * GROUPS + 1))
            sp.wait_ge(sp_stored, 16 * (GROUPS + 1))
            sp.wait_ge(conv_stored, 16)

        @block.gpsimd
        def _(pool):
            lo_done.open(pool)
            def low(g, k):
                for n, c in enumerate(HALVES):
                    hi_done.wait(pool, g, 2 * k + n)
                    nc.gpsimd.tensor_tensor(w_lo[k % 2][:, c], raw[k % 2][:, c], w_hi[k % 2][:, c].bitcast(F32), ALU.subtract).then_inc(lo_done.sem, 1)
            with pool.Fori(0, GROUPS) as g:
                for k in range(UNITS):
                    low(g, k)
            for k in range(OUT_UNITS):
                low(GROUPS, k)

        @block.tensor
        def _(pe):
            for s in (blk_done, cb_done, bn_done, xn_done, ec_done, cum_done, y_done, st_done, ys_done, up_done, sp_done, norm_done):
                s.open(pe)
            def out_block(g, first, c):
                if c >= 2:
                    out_out.wait(pe, g, c - 2)
                elif first:
                    in_out.wait(pe, g, 8 + c)
                else:
                    out_out.wait_last_turn(pe, g, 14 + c)
                k = c // 4
                if c == 0 and first:
                    ylo_done.wait_last_turn(pe, g, 0)
                elif c == 0:
                    ylo_done.wait(pe, g - 1, 0)
                if c % 2 == 0:
                    lo_done.wait(pe, g, 2 * (first + k) + c // 2 % 2)
                for j in range(PAIRS):
                    w = slice((c % 4 * 4 + j) * P, (c % 4 * 4 + j + 1) * P)
                    last = mm3(nc, DENSE[c % 2][:, 0:TOK], (w_hi[k % 2][:, w], w_lo[k % 2][:, w]),
                               (m["y_hi"][:, j, :], m["y_lo"][:, j, :]), j == 0, j == PAIRS - 1)
                last.then_inc(blk_done.sem, 1)
            with pe.Fori(0, GROUPS) as g:
                def in_block(k):
                    if k >= 2:
                        in_out.wait(pe, g, k - 2)
                    else:
                        out_out.wait_last_turn(pe, g, 14 + k)
                    for j in range(KT):
                        if j % (KT // 2) == 0:
                            lo_done.wait(pe, g, 2 * k + j // (KT // 2))
                        c = slice(j * P, (j + 1) * P)
                        last = mm3(nc, DENSE[k % 2][:, 0:TOK], (w_hi[k % 2][:, c], w_lo[k % 2][:, c]),
                                   (m["h_hi"][:, j, :], m["h_lo"][:, j, :]), j == 0, j == KT - 1)
                    last.then_inc(blk_done.sem, 1)
                for k in range(CONV_BLK + 1):
                    in_block(k)

                xc_done.wait(pe, g, xC)
                up_out.wait_last_turn(pe, g, 7)
                sp_evac.wait_last_turn(pe, g, 0)
                nc.tensor.matmul(SA[0:48, 0:TOK], xc[:, xB, 0:48], xc[:, xC, :], start=True, stop=True).then_inc(cb_done.sem, 1)
                nc.tensor.matmul(SB[:, 0:256], xc[:, xB, 48:176], xc[:, xC, 48:TOK], start=True, stop=True)
                nc.tensor.matmul(SB[:, 256:384], xc[:, xB, 176:TOK], xc[:, xC, 176:TOK], start=True, stop=True).then_inc(cb_done.sem, 1)
                y_out.wait_last_turn(pe, g, PAIRS - 1)
                for t in TILE_ORDER:
                    last = nc.tensor.transpose(BN[0:TILE_N[t], t * STATE:(t + 1) * STATE], xc[:, xB, TILE_AT[t]:TILE_AT[t + 1]], m["ident"][:])
                last.then_inc(bn_done.sem, 1)
                rstd_done.wait_last_turn(pe, g, 0)
                for n, t in enumerate(TILE_ORDER):
                    for p in range(PAIRS):
                        last = nc.tensor.transpose(XN[n][0:TILE_N[t], p * P:(p + 1) * P], xc[:, p, TILE_AT[t]:TILE_AT[t + 1]], m["ident"][:])
                    last.then_inc(xn_done.sem, 1)
                in_block(CONV_BLK + 1)
                in_block(CONV_BLK + 2)
                bn_out.wait(pe, g, 1)
                sel_set.wait(pe, g, 1)
                for p in range(PAIRS):
                    last = nc.tensor.matmul(BN[:, p * N_SAMPLE:(p + 1) * N_SAMPLE], m["sel_wide"][:, 2 * p:2 * p + 2, :].rearrange("p e c -> p (e c)"),
                                            m["cumT"][:, 0:N_SAMPLE], start=True, stop=True)
                last.then_inc(ec_done.sem, 1)

                def states_in(p):
                    pe.wait_ge(s_loaded[p % 2], 16 * (2 * g + p // 2 + 1))
                    for half, bank in enumerate((SA, SB)):
                        if p == 0:
                            cb_out.wait(pe, g, half)
                        else:
                            up_out.wait(pe, g, 2 * (p - 1) + half)
                        for b in range(4):
                            last = nc.tensor.transpose(bank[:, b * P:(b + 1) * P], s_in[p % 2][:, 4 * half + b, :], m["ident"][:])
                        last.then_inc(st_done.sem, 1)

                def states(p):
                    st_out.wait(pe, g, 2 * p)
                    st_out.wait(pe, g, 2 * p + 1)
                    ec_out.wait(pe, g, 0)
                    if p:
                        y_out.wait(pe, g, p - 1)
                    for b in range(DEC_BATCH):
                        last = nc.tensor.matmul(BN[:, 128 + p * N_SAMPLE + b * 4:128 + p * N_SAMPLE + b * 4 + 4], m["s_t"][:, b, :],
                                                xc[:, xC, b * 4:b * 4 + 4], start=True, stop=True)
                    last.then_inc(ys_done.sem, 1)
                    xn_out.wait(pe, g, 2)
                    bd_done.wait(pe, g, 0)
                    for half, bank in enumerate((SA, SB)):
                        nc.tensor.matmul(bank[:, :], m["xws"][:, p * P:(p + 1) * P],
                                         m["b_diag"][:, 4 * half:4 * half + 4, :].rearrange("p b n -> p (b n)"), start=True, stop=True).then_inc(up_done.sem, 1)

                def head(e):
                    if e < 2:
                        xn_out.wait(pe, g, e)
                    else:
                        cum_read.wait(pe, g, e - 2)
                    nc.tensor.matmul(CUM[e % 2][:, 0:TOK], m["sel"][:, e:e + 1].to_broadcast([HEADS, P]), m["cumT"][:, :],
                                     start=True, stop=True).then_inc(cum_done.sem, 1)

                def head_y(e):
                    p, rows = e // 2, slice(64 * (e % 2), 64 * (e % 2) + 64)
                    if e == 0:
                        xn_out.wait(pe, g, 2)
                    elif e % 2 == 0:
                        y_out.wait(pe, g, p - 1)
                    mix_done.wait(pe, g, e)
                    mx, c = mix[e % 2], slice(e * HD, (e + 1) * HD)
                    nc.tensor.matmul(Y[rows, 48:TOK], m["xdt"][:, 1, c], mx[:, 304:560], start=True, stop=False)
                    nc.tensor.matmul(Y[rows, 176:TOK], m["xdt"][:, 2, c], mx[:, 560:688], start=False, stop=False)
                    nc.tensor.matmul(Y[rows, 48:TOK], m["xdt"][0:48, 0, c], mx[0:48, 48:304], start=False, stop=False)
                    last = nc.tensor.matmul(Y[rows, 0:48], m["xdt"][0:48, 0, c], mx[0:48, 0:48], start=False, stop=True)
                    last.then_inc(y_done.sem, 1)
                states_in(0)
                head(0)
                in_block(CONV_BLK + 3)
                for e in range(HPG - 1):
                    head(e + 1)
                    if e % 2:
                        states_in(e // 2 + 1)
                    out_block(g, IN_UNITS, 2 * e)
                    if e % 2 == 0:
                        states(e // 2)
                    out_block(g, IN_UNITS, 2 * e + 1)
                    head_y(e)
                head_y(HPG - 1)
                out_block(g, IN_UNITS, 14)
                out_block(g, IN_UNITS, 15)
                up_out.wait(pe, g, 2 * PAIRS - 2)
                for p in range(PAIRS):
                    for t in range(3):
                        last = nc.tensor.matmul(SA[:, p * STATE:(p + 1) * STATE], m["xwp"][0:TILE_N[t], t, p * P:(p + 1) * P],
                                                m["b_n"][0:TILE_N[t], t, :], start=t == 0, stop=t == 2)
                last.then_inc(sp_done.sem, 1)
                cum_read.wait(pe, g, HPG - 2)
                for p in range(PAIRS):
                    sq_done.wait(pe, g, p)
                    last = nc.tensor.matmul(CUM[0][:, 0:TOK], m["ones"][:], m["y_sq"][:, p, :], start=p == 0, stop=p == PAIRS - 1)
                last.then_inc(norm_done.sem, 1)
            for c in range(4 * OUT_UNITS):
                out_block(GROUPS, 0, c)

        @block.scalar
        def _(act):
            a = Chain(act, act_step)
            for s in (hi_done, in_out, xc_done, ec_out, dec_done, sq_done, rstd_done, yhi_done, cum_read):
                s.open(act)
            A_STEPS = 1
            def split(g, k, done=None):
                act.wait_ge(raw_in[k % 2], 16 * ((UNITS // 2) * g + k // 2 + 1))
                if done is not None:
                    blk_done.wait(act, g, done)
                for c in HALVES:
                    nc.scalar.activation(w_hi[k % 2][:, c], raw[k % 2][:, c], ACT.Copy).then_inc(hi_done.sem, 1)
            split(0, 0)
            split(0, 1)
            with act.Fori(0, GROUPS) as g:
                a.turn(g, A_STEPS)

                def out_split(k):
                    split(g, k, IN_UNITS + 4 * (k - 2 - IN_UNITS) + 3)

                def evac(k):
                    blk_done.wait(act, g, k)
                    src = DENSE[k % 2]
                    if k < CONV_BLK:
                        if k >= 2:
                            conv_saved.wait(act, g, k - 2)
                        else:
                            conv_saved.wait_last_turn(act, g, CONV_BLK - 2 + k)
                        buf = cbuf[k % 2]
                        nc.scalar.activation(by_seq(buf, 7)[:, :, 0:3], m["conv_old"][:, bass.ds(g, 1), k, :, :].rearrange("p a b t -> p (a b) t"), ACT.Copy)
                        nc.scalar.activation(by_seq(buf, 7)[:, :, 3:7], by_seq(src, 4), ACT.Copy)
                        nc.scalar.activation(buf[:, 59:CB], src[:, N_SAMPLE:TOK], ACT.Copy).then_inc(in_out.sem, 1)
                    else:
                        if k == CONV_BLK:
                            y_out.wait_last_turn(act, g, PAIRS - 1)
                        nc.scalar.activation(m["gate"][:, k - CONV_BLK, :], src[:, 0:TOK], ACT.Silu).then_inc(in_out.sem, 1)

                def conv_silu(k):
                    conv_done.wait(act, g, k)
                    if k == 0:
                        ys_done.wait_last_turn(act, g, PAIRS - 1)
                        y_out.wait_last_turn(act, g, PAIRS - 1)
                    nc.scalar.activation(xc[:, k, 0:N_SAMPLE].rearrange("p (b t) -> p b t", t=4), by_seq(cacc[k % 2], 7)[:, :, 0:4], ACT.Silu)
                    nc.scalar.activation(xc[:, k, N_SAMPLE:TOK], cacc[k % 2][:, 56:CO], ACT.Silu).then_inc(xc_done.sem, 1)
                for k in range(IN_UNITS):
                    split(g, k + 2, k)
                    evac(k)
                    if 1 <= k < CONV_BLK:
                        conv_silu(k - 1)
                    if k == CONV_BLK - 1:
                        conv_silu(k)
                ec_done.wait(act, g, 0)
                up_out.wait_last_turn(act, g, 2 * PAIRS - 1)
                y_out.wait_last_turn(act, g, PAIRS - 1)
                nc.scalar.activation(m["e_cum"][:].rearrange("p a b -> p (a b)"), BN[:, 0:P], ACT.Exp).then_inc(ec_out.sem, 1)
                for e in range(HPG):
                    cum_done.wait(act, g, e)
                    if e >= 2:
                        mix_done.wait(act, g, e - 2)
                    else:
                        mix_done.wait_last_turn(act, g, HPG - 2 + e)
                    dc = dec[e % 2]
                    for t in range(3):
                        n = TILE_N[t]
                        last = nc.scalar.activation(dc[0:n, PAIR_AT[t]:PAIR_AT[t + 1]], CUM[e % 2][0:n, TILE_AT[t]:TOK], ACT.Relu,
                                                    bias=m["cum_n"][0:n, t, bass.ds(g * HPG + e, 1)], scale=-1.0)
                    last.then_inc(cum_read.sem, 1)
                    cum_read.wait(act, g, e)
                    nc.scalar.activation(dc[0:48, 0:304], dc[0:48, 0:304], ACT.Exp, scale=-1.0)
                    nc.scalar.activation(dc[:, 304:688], dc[:, 304:688], ACT.Exp, scale=-1.0).then_inc(dec_done.sem, 1)
                    if e in (2, 4, 6):
                        out_split(IN_UNITS + 1 + e // 2)
                for p in range(PAIRS):
                    y_out.wait(act, g, p)
                    nc.scalar.activation(m["y_sq"][:, p, :], m["y"][:, p, :], ACT.Square).then_inc(sq_done.sem, 1)
                out_split(UNITS + 1)
                norm_done.wait(act, g, 0)
                a(nc.scalar.activation(m["y_rstd"][:], CUM[0][:, 0:TOK], ACT.Ln, bias=m["eps"][:, 0:1], scale=1.0 / GW))
                nc.scalar.activation(m["y_rstd"][:], m["y_rstd"][:], ACT.Exp, scale=-0.5).then_inc(rstd_done.sem, 1)
                yn_done.wait(act, g, 0)
                nc.scalar.activation(m["y_hi"][:], m["y"][:], ACT.Copy).then_inc(yhi_done.sem, 1)
            for k in (2, 3):
                split(GROUPS, k, 4 * (k - 2) + 3)
            a.end(GROUPS)

        @block.vector
        def _(dve):
            v = Chain(dve, dve_step)
            for s in (out_out, conv_done, conv_saved, sel_set, cb_out, bn_out, bd_done, xn_out, mix_done, y_out, st_out, up_out,
                      sp_evac, yn_done, ylo_done):
                s.open(dve)
            for s in (s_stored, sp_stored):
                dve.sem_inc(s, 16)
            V_STEPS = 3 * CONV_BLK + 3 * PAIRS

            def add_out(g, first, c):
                blk_done.wait(dve, g, first + c)
                nc.vector.tensor_tensor(x[:, c, :], x[:, c, :], DENSE[c % 2][:, 0:TOK], ALU.add).then_inc(out_out.sem, 1)
            with dve.Fori(0, GROUPS) as g:
                v.turn(g, V_STEPS)
                cum_done.wait_last_turn(dve, g, HPG - 1)
                nc.vector.tensor_copy(m["sel"][:], m["ident"][0:HEADS, bass.ds(g * HPG, HPG)]).then_inc(sel_set.sem, 1)
                sel_set.wait(dve, g, 0)
                nc.vector.tensor_copy(m["sel_wide"][:], m["sel"][:].rearrange("p (e c) -> p e c", c=1).to_broadcast([HEADS, HPG, HD])).then_inc(sel_set.sem, 1)
                for k in range(CONV_BLK):
                    in_out.wait(dve, g, k)
                    if k >= 2:
                        xc_done.wait(dve, g, k - 2)
                    else:
                        xc_done.wait_last_turn(dve, g, CONV_BLK - 2 + k)
                    buf, acc = cbuf[k % 2], cacc[k % 2]
                    cw = lambda t: m["conv_w"][:, bass.ds(g, 1), k, t:t + 1].rearrange("p a b -> p (a b)")
                    v(nc.vector.tensor_scalar(acc[:, :], buf[:, 0:CO], cw(0), m["conv_b"][:, bass.ds(g, 1), k:k + 1].rearrange("p a b -> p (a b)"), ALU.mult, ALU.add))
                    for t in range(1, 4):
                        ins = nc.vector.scalar_tensor_tensor(acc[:, :], buf[:, t:t + CO], cw(t), acc[:, :], op0=ALU.mult, op1=ALU.add)
                        if t < 3:
                            v(ins)
                    ins.then_inc(conv_done.sem, 1)
                    new = m["conv_new"][:, bass.ds(g, 1), k].rearrange("p a b t -> p (a b) t")
                    nc.vector.tensor_copy(new[:, 0:DEC_BATCH, :], by_seq(buf, 7)[:, :, 4:7])
                    nc.vector.tensor_copy(new[:, DEC_BATCH:DEC_BATCH + 1, :], buf[:, CB - 3:CB].rearrange("p (a t) -> p a t", a=1)).then_inc(conv_saved.sem, 1)
                cb_done.wait(dve, g, 0)
                y_done.wait_last_turn(dve, g, HPG - 1)
                nc.vector.tensor_tensor(m["cb"][0:48, 0:304], SA[0:48, 0:304], m["mask"][0:48, 0:304], ALU.mult).then_inc(cb_out.sem, 1)
                cb_done.wait(dve, g, 1)
                nc.vector.tensor_tensor(m["cb"][:, 304:688], SB[:, 0:384], m["mask"][:, 304:688], ALU.mult).then_inc(cb_out.sem, 1)
                bn_done.wait(dve, g, 0)
                sp_done.wait_last_turn(dve, g, 0)
                nc.vector.tensor_copy(m["b_n"][0:48, 0, :], BN[0:48, 0:STATE]).then_inc(bn_out.sem, 1)
                nc.vector.tensor_copy(m["b_n"][:, 1:3, :], BN[:, STATE:3 * STATE].rearrange("p (t n) -> p t n", t=2)).then_inc(bn_out.sem, 1)
                bn_out.wait(dve, g, 0)
                nc.vector.tensor_tensor(m["b_diag"][:], m["b_n"][0:N_SAMPLE, 0:1, :].to_broadcast([N_SAMPLE, DEC_BATCH, STATE]),
                                        m["diag"][:].rearrange("p (b a) -> p b a", a=1).to_broadcast([N_SAMPLE, DEC_BATCH, STATE]), ALU.mult).then_inc(bd_done.sem, 1)
                for bank, t in enumerate(TILE_ORDER):
                    xn_done.wait(dve, g, bank)
                    n = TILE_N[t]

                    def times(out, rows, coef):
                        return nc.vector.tensor_tensor(out.rearrange("p (e c) -> p e c", e=HPG), XN[bank][0:rows, :].rearrange("p (e c) -> p e c", e=HPG),
                                                       coef.rearrange("p (e c) -> p e c", c=1).to_broadcast([rows, HPG, HD]), ALU.mult)
                    times(m["xdt"][0:n, t, :], n, m["dt_n"][0:n, t, bass.ds(g * HPG, HPG)])
                    if t == 0:
                        times(m["xws"][:, :], N_SAMPLE, m["ws_n"][:, bass.ds(g * HPG, HPG)])
                    times(m["xwp"][0:n, t, :], n, m["wp_n"][0:n, t, bass.ds(g * HPG, HPG)]).then_inc(xn_out.sem, 1)

                def states(p):
                    for half, bank in enumerate((SA, SB)):
                        st_done.wait(dve, g, 2 * p + half)
                        if half == 0:
                            if p:
                                ys_done.wait(dve, g, p - 1)
                            else:
                                ys_done.wait_last_turn(dve, g, PAIRS - 1)
                        nc.vector.tensor_copy(m["s_t"][:, 4 * half:4 * half + 4, :].rearrange("p b n -> p (b n)"), bank[:, :]).then_inc(st_out.sem, 1)

                def update(p):
                    dve.wait_ge(s_loaded[p % 2], 16 * (2 * g + p // 2 + 1))
                    dve.wait_ge(s_stored, 16 * (PAIRS * g + p + 1))
                    for half, bank in enumerate((SA, SB)):
                        up_done.wait(dve, g, 2 * p + half)
                        for b in range(4 * half, 4 * half + 4):
                            last = nc.vector.scalar_tensor_tensor(s_out[:, b, :], s_in[p % 2][:, b, :], m["e_cum"][:, p, 4 * b + 3:4 * b + 4],
                                                                  bank[:, (b % 4) * P:(b % 4 + 1) * P], op0=ALU.mult, op1=ALU.add)
                        last.then_inc(up_out.sem, 1)

                def mixes(e):
                    dec_done.wait(dve, g, e)
                    if e >= 2:
                        mixed_used(e)
                    nc.vector.tensor_tensor(mix[e % 2][0:48, 0:304], dec[e % 2][0:48, 0:304], m["cb"][0:48, 0:304], ALU.mult)
                    nc.vector.tensor_tensor(mix[e % 2][:, 304:688], dec[e % 2][:, 304:688], m["cb"][:, 304:688], ALU.mult).then_inc(mix_done.sem, 1)

                def mixed_used(e):
                    y_done.wait(dve, g, e - 2)

                def y_pair(p):
                    y_done.wait(dve, g, 2 * p + 1)
                    ys_done.wait(dve, g, p)
                    if p == 0:
                        yhi_done.wait_last_turn(dve, g, 0)
                        ylo_done.wait_last_turn(dve, g, 0)
                    y = m["y"][:, p, :]
                    v(nc.vector.scalar_tensor_tensor(y, xc[:, p, :], m["d_skip"][:, bass.ds(g, 1), p:p + 1].rearrange("p a b -> p (a b)"), Y[:, 0:TOK], op0=ALU.mult, op1=ALU.add))
                    v(nc.vector.tensor_tensor(m["tmp32"][:], m["e_cum"][:, p, :], BN[:, 128 + p * N_SAMPLE:128 + (p + 1) * N_SAMPLE], ALU.mult))
                    v(nc.vector.tensor_tensor(y[:, 0:N_SAMPLE], y[:, 0:N_SAMPLE], m["tmp32"][:], ALU.add))
                    nc.vector.tensor_tensor(y, y, m["gate"][:, p, :], ALU.mult).then_inc(y_out.sem, 1)
                states(0)
                for e in range(HPG - 1):
                    mixes(e)
                    add_out(g, IN_UNITS, 2 * e)
                    if e % 2 == 0:
                        update(e // 2)
                    else:
                        states(e // 2 + 1)
                    add_out(g, IN_UNITS, 2 * e + 1)
                    if e % 2:
                        y_pair(e // 2)
                mixes(HPG - 1)
                y_pair(PAIRS - 1)
                add_out(g, IN_UNITS, 14)
                add_out(g, IN_UNITS, 15)
                sp_done.wait(dve, g, 0)
                dve.wait_ge(sp_stored, 16 * (g + 1))
                nc.vector.tensor_copy(m["sp_out"][:].rearrange("p j n -> p (j n)"), SA[:, :]).then_inc(sp_evac.sem, 1)
                rstd_done.wait(dve, g, 0)
                for p in range(PAIRS):
                    last = nc.vector.scalar_tensor_tensor(m["y"][:, p, :], m["y"][:, p, :], m["gate_norm"][:, bass.ds(g, 1), p:p + 1].rearrange("p a b -> p (a b)"),
                                                          m["y_rstd"][:], op0=ALU.mult, op1=ALU.mult)
                last.then_inc(yn_done.sem, 1)
                yhi_done.wait(dve, g, 0)
                nc.vector.tensor_tensor(m["y_lo"][:], m["y"][:], m["y_hi"][:].bitcast(F32), ALU.subtract).then_inc(ylo_done.sem, 1)
            for c in range(4 * OUT_UNITS):
                add_out(GROUPS, 0, c)
            v.end(GROUPS)


MLA_HEADS, LATENT, ROPE, NOPE = 16, 512, 64, 128
LT = LATENT // P
QK = NOPE + ROPE
ROW = LATENT + ROPE
Q_PAIRS = MLA_HEADS // 2
PAGES = 8
QROWS = DEC_SEQ * MLA_HEADS


def memory_mla(nc, m):
    s = Space(nc, m["common_end"])

    def put(name, shape, dtype=F32):
        m[name] = s(name, shape, dtype)
    put("o", [P, MLA_HEADS, TOK])
    put("lat_s", [P, LT, N_SAMPLE])
    put("kr_s", [ROPE, N_SAMPLE])
    put("rows_s", [N_SAMPLE, LATENT])
    put("r_new", [QROWS, N_SAMPLE])
    put("table", [1, DEC_BATCH * PAGES], I32)
    m["mla_kept"] = s.at
    put("rot", [P, P])
    put("half", [P, 2, P])
    put("cos", [P, TOK])
    put("sin", [P, TOK])
    put("mla_gain", [P, 2, LT])
    put("qk_gain", [P, 4])
    put("lat", [P, LT, TOK])
    put("kr", [P, TOK])
    put("rows_n", [P, 3, ROW])
    put("r_n", [P, 3, MLA_HEADS])
    put("ss_n", [P, 3, MLA_HEADS])
    put("ssr_n", [P, 3])
    put("lat_hi", [P, LT, TOK], F32R)
    put("lat_lo", [P, LT, TOK], F32R)
    put("qn", [P, MLA_HEADS, TOK])
    put("qr", [P, Q_PAIRS, TOK])
    put("vn", [P, 3, MLA_HEADS * NOPE])
    m["qa"] = m["qr"][:, 0:LT, :]
    t = Space(nc, SBUF_START + KT * TOK * 4)
    m["kn"] = t("kn", [P, 3, MLA_HEADS * NOPE])
    m["t_work"] = t("t_work", [P, 4, TOK])
    m["sq_n"] = t("sq_n", [P, 512])
    assert t.at <= SBUF_START + 3 * KT * TOK * 4
    t = Space(nc, SBUF_START + KT * TOK * 4)
    m["qa_hi"] = t("qa_hi", [P, LT, TOK], F32R)
    m["qa_lo"] = t("qa_lo", [P, LT, TOK], F32R)
    t = Space(nc, SBUF_START + KT * TOK * 4)
    m["q_lat"] = t("q_lat", [P, LT, DEC_BATCH, QROWS])
    m["q_rs"] = t("q_rs", [ROPE, DEC_BATCH, QROWS])
    m["o_lat"] = t("o_lat", [P, LT, MLA_HEADS, N_SAMPLE])
    for k in range(2):
        m[f"pt{k}"] = t(f"pt{k}", [P, LATENT])
        m[f"pk{k}"] = t(f"pk{k}", [ROPE, P])
    m["sq1"] = t("sq1", [P, 512])
    m["kr_sq"] = t("kr_sq", [P, PAGES, ROPE])
    m["r4"] = t("r4", [P, PAGES, DEC_SEQ, MLA_HEADS])
    assert t.at <= SBUF_START + 3 * KT * TOK * 4
    ring = SBUF_START + 3 * KT * TOK * 4
    t = Space(nc, ring)
    for e in range(2):
        for name, shape in (("q_s", [P, TOK]), ("k_s", [P, 3, P]), ("v_s", [P, 3, P]), ("k_t", [P, TOK]), ("s", [P, 528]),
                            ("p_t", [P, PAIR_N]), ("mx", [P, 3]), ("sum", [P, 3])):
            m[f"{name}{e}"] = t(f"{name}{e}", shape)
    for name, shape in (("qr_s", [P, TOK]), ("kr_s2", [P, 3, P]), ("kr_t", [P, TOK]), ("att_mask", [P, 528])):
        m[name] = t(name, shape)
    assert t.at <= ring + 6 * UNIT * 4
    t = Space(nc, ring)
    m["past"] = t("past", [P, 2, PAGES, ROW])
    for k in range(2):
        m[f"pt_hi{k}"] = t(f"pt_hi{k}", [P, LATENT], F32R)
        m[f"pt_lo{k}"] = t(f"pt_lo{k}", [P, LATENT], F32R)
    m["o_s"] = t("o_s", [QROWS, LATENT])
    assert t.at <= ring + 6 * UNIT * 4, t.at
    t = Space(nc, m["mla_kept"])
    m["uk_hi"] = t("uk_hi", [P, LT, LT, 512], F32R)
    m["uk_lo"] = t("uk_lo", [P, LT, LT, 512], F32R)
    for name, shape in (("sc0", [QROWS, PAGES * P + N_SAMPLE]), ("sc1", [QROWS, PAGES * P + N_SAMPLE]), ("sq0", [P, 512]), ("pst", [P, PAGES + 1, QROWS]),
                        ("ss", [P, PAGES, MLA_HEADS]), ("ssr", [P, PAGES]), ("smx", [QROWS, 2]),
                        ("new_mask", [QROWS, DEC_BATCH, N_SAMPLE]), ("q_ls", [P, LT, QROWS]), ("q_rss", [ROPE, QROWS])):
        m[name] = t(name, shape)


def dense_stage(nc, shared, m, psum, units, n, per, rhs, evac):
    kt = KT // per
    raw_in = [shared.plain(f"raw_in{k}", 16 * ((n + 1 - k) // 2)) for k in range(2)]
    hi_done, lo_done = shared.raised_by("hi_done", 2, n), shared.raised_by("lo_done", 2, n)
    blk_done, blk_out = shared.raised_by("blk_done", 2 * per, n * per), shared.raised_by("blk_evac", 2 * per, n * per)
    raw, w_hi, w_lo = ([m[f"{x}{k}"] for k in range(2)] for x in ("raw", "w_hi", "w_lo"))

    def turns(eng, body):
        if n > 1:
            with eng.Fori(0, n // 2) as i:
                body(i, 0)
                body(i, 1)
        if n % 2:
            body(n // 2, 0)
    with nc.Block() as block:
        @block.sync
        def _(sp):
            def load(i, k):
                lo_done.wait_last_turn(sp, i, k)
                sp.dma_start(raw[k][:], units[bass.ds(2 * i + k, 1)].rearrange("a p n -> (a p) n")).then_inc(raw_in[k][0], 16)
            turns(sp, load)

        @block.scalar
        def _(act):
            hi_done.open(act)

            def high(i, k):
                act.wait_ge(raw_in[k][0], 16 * i + (raw_in[k][1] + 16))
                blk_done.wait_last_turn(act, i, k * per + per - 1)
                nc.scalar.activation(w_hi[k][:], raw[k][:], ACT.Copy).then_inc(hi_done.sem, 1)
            turns(act, high)

        @block.gpsimd
        def _(pool):
            lo_done.open(pool)

            def low(i, k):
                hi_done.wait(pool, i, k)
                nc.gpsimd.tensor_tensor(w_lo[k][:], raw[k][:], w_hi[k][:].bitcast(F32), ALU.subtract).then_inc(lo_done.sem, 1)
            turns(pool, low)

        @block.tensor
        def _(pe):
            blk_done.open(pe)

            def products(i, k):
                lo_done.wait(pe, i, k)
                for b in range(per):
                    c = k * per + b
                    if c >= 2:
                        blk_out.wait(pe, i, c - 2)
                    else:
                        blk_out.wait_last_turn(pe, i, 2 * per + c - 2)
                    for j in range(kt):
                        w = slice((b * kt + j) * P, (b * kt + j + 1) * P)
                        last = mm3(nc, psum[c % 2][:, 0:TOK], (w_hi[k][:, w], w_lo[k][:, w]), rhs(j), j == 0, j == kt - 1)
                    last.then_inc(blk_done.sem, 1)
            turns(pe, products)

        @block.vector
        def _(dve):
            blk_out.open(dve)

            def out(i, k):
                for b in range(per):
                    c = k * per + b
                    blk_done.wait(dve, i, c)
                    evac(i * (2 * per) + c, psum[c % 2]).then_inc(blk_out.sem, 1)
            turns(dve, out)


def latent_norm(nc, shared, m, psum, src, gain, hi, lo):
    (squared, b1), (summed, b2), (rooted, b3), (scaled, b4), (high, b5), (low, b6) = [
        shared.plain(s, n) for s, n in (("squared", 1), ("summed", 1), ("rooted", 2), ("scaled", 1), ("high", 1), ("low", 1))]
    sq, rs = m["raw0"][:, 0:LT * TOK].rearrange("p (k t) -> p k t", k=LT), m["raw1"][:, 0:TOK]
    with nc.Block() as block:
        @block.scalar
        def _(act):
            nc.scalar.activation(sq, src[:], ACT.Square).then_inc(squared, 1)
            act.wait_ge(summed, b2 + 1)
            nc.scalar.activation(rs, psum[0][:, 0:TOK], ACT.Ln, bias=m["eps"][:, 0:1], scale=1.0 / LATENT).then_inc(rooted, 1)
            act.wait_ge(rooted, b3 + 1)
            nc.scalar.activation(rs, rs, ACT.Exp, scale=-0.5).then_inc(rooted, 1)
            act.wait_ge(scaled, b4 + 1)
            nc.scalar.activation(hi[:], src[:], ACT.Copy).then_inc(high, 1)

        @block.tensor
        def _(pe):
            pe.wait_ge(squared, b1 + 1)
            for k in range(LT):
                last = nc.tensor.matmul(psum[0][:, 0:TOK], m["ones"][:], sq[:, k, :], start=k == 0, stop=k == LT - 1)
            last.then_inc(summed, 1)

        @block.vector
        def _(dve):
            dve.wait_ge(rooted, b3 + 2)
            for k in range(LT):
                last = nc.vector.scalar_tensor_tensor(src[:, k, :], src[:, k, :], gain[:, k:k + 1], rs, op0=ALU.mult, op1=ALU.mult)
            last.then_inc(scaled, 1)
            dve.wait_ge(high, b5 + 1)
            nc.vector.tensor_tensor(lo[:], src[:], hi[:].bitcast(F32), ALU.subtract).then_inc(low, 1)
            dve.wait_ge(low, b6 + 1)


def rows_stage(nc, ctx, m, psum, d):
    sem = lambda s: ctx.enter_context(nc.semaphore(f"rows_{s}"))
    turned, v_step, t_done, t_out, stored = [sem(s) for s in ("turned", "dve", "transposed", "evac", "stored")]
    kr, t1, t2 = m["kr"], m["t_work"][:, 0, :], m["t_work"][:, 1, :]
    rows = m["rows_n"]
    with nc.Block() as block:
        @block.tensor
        def _(pe):
            nc.tensor.matmul(psum[6][:, 0:TOK], m["rot"][:], kr[:], start=True, stop=True).then_inc(turned, 1)
            for n, t in enumerate(TILE_ORDER):
                for k in range(LT):
                    nc.tensor.transpose(psum[n][0:TILE_N[t], k * P:(k + 1) * P], m["lat"][:, k, TILE_AT[t]:TILE_AT[t + 1]], m["ident"][:])
                if n == 0:
                    pe.wait_ge(v_step, 3)
                last = nc.tensor.transpose(psum[3 + n][0:TILE_N[t], 0:ROPE], kr[0:ROPE, TILE_AT[t]:TILE_AT[t + 1]], m["ident"][0:ROPE, 0:ROPE])
                last.then_inc(t_done, 1)

        @block.vector
        def _(dve):
            v = Chain(dve, v_step)
            dve.wait_ge(turned, 1)
            v(nc.vector.tensor_tensor(t1, psum[6][:, 0:TOK], m["sin"][:], ALU.mult))
            v(nc.vector.tensor_tensor(t2, kr[:], m["cos"][:], ALU.mult))
            v(nc.vector.tensor_tensor(kr[:], t1, t2, ALU.add))
            for n, t in enumerate(TILE_ORDER):
                r = slice(0, TILE_N[t])
                dve.wait_ge(t_done, n + 1)
                nc.vector.tensor_copy(rows[r, t, 0:LATENT], psum[n][r, :]).then_inc(t_out, 1)
                nc.vector.tensor_copy(rows[r, t, LATENT:ROW], psum[3 + n][r, 0:ROPE]).then_inc(t_out, 1)
            dve.wait_ge(t_out, 6)
            for t in range(3):
                r = slice(0, TILE_N[t])
                v(nc.vector.tensor_tensor(m["t_work"][r, t, 0:ROPE], rows[r, t, LATENT:ROW], rows[r, t, LATENT:ROW], ALU.mult))
                v(nc.vector.tensor_reduce(m["ssr_n"][r, t:t + 1], m["t_work"][r, t, 0:ROPE], AX.X, ALU.add))

        @block.sync
        def _(sp):
            for n, t in enumerate(TILE_ORDER):
                sp.wait_ge(t_out, 2 * n + 2)
                sp.dma_start(d["kv_out"][TILE_AT[t]:TILE_AT[t + 1], :], rows[0:TILE_N[t], t, :]).then_inc(stored, 16)
            sp.wait_ge(stored, 48)


def query_stage(nc, ctx, m, psum):
    sem = lambda s: ctx.enter_context(nc.semaphore(f"query_{s}"))
    turned, roped, squared, summed, rstd_done = [Signal(sem(s), n) for s, n in
                                                 (("turned", 1), ("roped", 1), ("squared", 3), ("summed", 2), ("rstd", 2))]
    normed, v_step, a_step = Signal(sem("normed"), 1), sem("dve"), sem("act")
    qn, qr, w = m["qn"], m["qr"], m["t_work"]
    qs = m["raw0"][:, 0:TOK]
    t1, t2 = m["raw0"][:, TOK:2 * TOK], m["raw0"][:, 2 * TOK:3 * TOK]
    sq = [m["raw1"][:, k * TOK:(k + 1) * TOK] for k in range(3)]
    rstd = [m["raw1"][:, (3 + k) * TOK:(4 + k) * TOK] for k in range(2)]
    pair = lambda i, e: bass.ds(2 * i + e, 1)
    flat = lambda ap: ap.rearrange("p a t -> p (a t)")
    with nc.Block() as block:
        @block.tensor
        def _(pe):
            turned.open(pe)
            summed.open(pe)
            with pe.Fori(0, Q_PAIRS) as i:
                normed.wait_last_turn(pe, i, 0)
                nc.tensor.matmul(psum[0][:, 0:TOK], m["rot"][:], flat(qr[:, bass.ds(i, 1), :]), start=True, stop=True).then_inc(turned.sem, 1)
                for e in range(2):
                    squared.wait(pe, i, 2)
                    nc.tensor.matmul(psum[1 + e][:, 0:TOK], m["ones"][:], sq[e], start=True, stop=False)
                    nc.tensor.matmul(psum[1 + e][:, 0:TOK], m["half"][:, e, :], sq[2], start=False, stop=True).then_inc(summed.sem, 1)

        @block.scalar
        def _(act):
            squared.open(act)
            rstd_done.open(act)
            c = Chain(act, a_step)
            with act.Fori(0, Q_PAIRS) as i:
                c.turn(i, 2)
                summed.wait_last_turn(act, i, 1)
                for e in range(2):
                    nc.scalar.activation(sq[e], flat(qn[:, pair(i, e), :]), ACT.Square).then_inc(squared.sem, 1)
                roped.wait(act, i, 0)
                nc.scalar.activation(sq[2], qs, ACT.Square).then_inc(squared.sem, 1)
                normed.wait_last_turn(act, i, 0)
                for e in range(2):
                    summed.wait(act, i, e)
                    c(nc.scalar.activation(rstd[e], psum[1 + e][:, 0:TOK], ACT.Ln, bias=m["eps"][:, 0:1], scale=1.0 / QK))
                    nc.scalar.activation(rstd[e], rstd[e], ACT.Exp, scale=-0.5).then_inc(rstd_done.sem, 1)
            c.end(Q_PAIRS)
            for h in range(MLA_HEADS):
                nc.scalar.activation(m["o"][:, h, :], m["o"][:, h, :], ACT.Silu)

        @block.vector
        def _(dve):
            roped.open(dve)
            normed.open(dve)
            v = Chain(dve, v_step)
            g = m["qk_gain"]
            v(nc.vector.tensor_tensor(g[:, 0:1], g[:, 0:1], g[:, 1:2], ALU.mult))
            v(nc.vector.tensor_tensor(g[:, 2:3], g[:, 2:3], g[:, 3:4], ALU.mult))
            v(nc.vector.tensor_scalar(g[:, 0:1], g[:, 0:1], float(QK) ** -0.5, None, ALU.mult))
            v(nc.vector.tensor_scalar(g[:, 2:3], g[:, 2:3], float(QK) ** -0.5, None, ALU.mult))
            with dve.Fori(0, Q_PAIRS) as i:
                v.turn(i, 2)
                turned.wait(dve, i, 0)
                v(nc.vector.tensor_tensor(t1, psum[0][:, 0:TOK], m["sin"][:], ALU.mult))
                v(nc.vector.tensor_tensor(t2, flat(qr[:, bass.ds(i, 1), :]), m["cos"][:], ALU.mult))
                nc.vector.tensor_tensor(qs, t1, t2, ALU.add).then_inc(roped.sem, 1)
                for e in range(2):
                    rstd_done.wait(dve, i, e)
                    q = flat(qn[:, pair(i, e), :])
                    nc.vector.scalar_tensor_tensor(q, q, g[:, 0:1], rstd[e], op0=ALU.mult, op1=ALU.mult)
                    r = slice(64 * e, 64 * e + 64)
                    last = nc.vector.scalar_tensor_tensor(flat(qr[r, bass.ds(i, 1), :]), qs[r, :], g[r, 2:3], rstd[e][r, :], op0=ALU.mult, op1=ALU.mult)
                last.then_inc(normed.sem, 1)
            v.end(Q_PAIRS)


def key_stage(nc, shared, m, psum, d):
    raw_in = [shared.plain(f"raw_in{k}", 16 * 4) for k in range(2)]
    hi_done, lo_done = shared.raised_by("hi_done", 2, 8), shared.raised_by("lo_done", 2, 8)
    blk_done, blk_out = shared.raised_by("blk_done", 6, 24), shared.raised_by("blk_evac", 6, 24)
    raw, w_hi, w_lo = ([m[f"{x}{k}"] for k in range(2)] for x in ("raw", "w_hi", "w_lo"))
    hi, lo = m["lat_hi"], m["lat_lo"]
    with nc.Block() as block:
        @block.sync
        def _(sp):
            with sp.Fori(0, 4) as i:
                for k in range(2):
                    lo_done.wait_last_turn(sp, i, k)
                    sp.dma_start(raw[k][:], d["kv_units"][bass.ds(2 * i + k, 1)].rearrange("a p n -> (a p) n")).then_inc(raw_in[k][0], 16)

        @block.gpsimd
        def _(pool):
            lo_done.open(pool)
            with pool.Fori(0, 4) as i:
                for k in range(2):
                    hi_done.wait(pool, i, k)
                    nc.gpsimd.tensor_tensor(w_lo[k][:], raw[k][:], w_hi[k][:].bitcast(F32), ALU.subtract).then_inc(lo_done.sem, 1)

        @block.scalar
        def _(act):
            hi_done.open(act)
            with act.Fori(0, 4) as i:
                for k in range(2):
                    act.wait_ge(raw_in[k][0], 16 * i + (raw_in[k][1] + 16))
                    blk_done.wait_last_turn(act, i, 3 * k + 2)
                    nc.scalar.activation(w_hi[k][:], raw[k][:], ACT.Copy).then_inc(hi_done.sem, 1)

        @block.tensor
        def _(pe):
            blk_done.open(pe)
            with pe.Fori(0, 4) as i:
                for k in range(2):
                    lo_done.wait(pe, i, k)
                    for n, t in enumerate(TILE_ORDER):
                        c = 3 * k + n
                        blk_out.wait_last_turn(pe, i, c)
                        tok = slice(TILE_AT[t], TILE_AT[t + 1])
                        for j in range(LT):
                            w = slice(j * 512, (j + 1) * 512)
                            last = mm3(nc, psum[c][0:TILE_N[t], :], (hi[:, j, tok], lo[:, j, tok]), (w_hi[k][:, w], w_lo[k][:, w]), j == 0, j == LT - 1)
                        last.then_inc(blk_done.sem, 1)

        @block.vector
        def _(dve):
            blk_out.open(dve)

            def heads(i, k, dst):
                for n, t in enumerate(TILE_ORDER):
                    c, r = 3 * k + n, slice(0, TILE_N[t])
                    blk_done.wait(dve, 2 * which + i, c)
                    nc.vector.tensor_copy(dst[r, t, bass.ds((2 * i + k) * 512, 512)], psum[c][r, :]).then_inc(blk_out.sem, 1)
            for which, dst in enumerate((m["kn"], m["vn"])):
                with dve.Fori(0, 2) as i:
                    heads(i, 0, dst)
                    heads(i, 1, dst)


def key_rms_stage(nc, ctx, m, psum):
    sem = lambda s: ctx.enter_context(nc.semaphore(f"krms_{s}"))
    v_step, squared, reduced, a_step, rep_done, t_done = [sem(s) for s in ("dve", "squared", "reduced", "act", "rep", "transposed")]
    sq = m["sq_n"]
    rep = m["t_work"][0:N_SAMPLE, 0, 0:QROWS]
    with nc.Block() as block:
        @block.scalar
        def _(act):
            n = 0
            for t in range(3):
                r = slice(0, TILE_N[t])
                for u in range(4):
                    if n:
                        act.wait_ge(reduced, n)
                    nc.scalar.activation(sq[r, :], m["kn"][r, t, u * 512:(u + 1) * 512], ACT.Square).then_inc(squared, 1)
                    n += 1
            act.wait_ge(v_step, 3)
            for t in range(3):
                r = slice(0, TILE_N[t])
                nc.scalar.activation(m["r_n"][r, t, :], m["ss_n"][r, t, :], ACT.Ln, bias=m["eps"][r, 0:1], scale=1.0 / QK).then_inc(a_step, 1)
            act.wait_ge(a_step, 3)
            for t in range(3):
                r = slice(0, TILE_N[t])
                nc.scalar.activation(m["r_n"][r, t, :], m["r_n"][r, t, :], ACT.Exp, scale=-0.5).then_inc(a_step, 1)

        @block.vector
        def _(dve):
            v = Chain(dve, v_step)
            n = 0
            for t in range(3):
                r = slice(0, TILE_N[t])
                for u in range(4):
                    dve.wait_ge(squared, n + 1)
                    nc.vector.tensor_reduce(m["ss_n"][r, t, 4 * u:4 * u + 4], sq[r, :].rearrange("p (h d) -> p h d", h=4), AX.X, ALU.add).then_inc(reduced, 1)
                    n += 1
            dve.wait_ge(reduced, n)
            for t in range(3):
                r = slice(0, TILE_N[t])
                v(nc.vector.tensor_scalar(m["ss_n"][r, t, :], m["ss_n"][r, t, :], m["ssr_n"][r, t:t + 1], None, ALU.add))
            dve.wait_ge(a_step, 6)
            nc.vector.tensor_copy(rep.rearrange("p (t h) -> p t h", h=MLA_HEADS),
                                  m["r_n"][0:N_SAMPLE, 0:1, :].to_broadcast([N_SAMPLE, DEC_SEQ, MLA_HEADS])).then_inc(rep_done, 1)
            dve.wait_ge(t_done, 1)
            v(nc.vector.tensor_copy(m["r_new"][:], psum[0][0:QROWS, 0:N_SAMPLE]))

        @block.tensor
        def _(pe):
            pe.wait_ge(rep_done, 1)
            nc.tensor.transpose(psum[0][0:QROWS, 0:N_SAMPLE], rep, m["ident"][0:N_SAMPLE, 0:N_SAMPLE]).then_inc(t_done, 1)


def q_lat_stage(nc, shared, m, psum, d):
    raw_in = [shared.plain(f"raw_in{k}", 16 * 2) for k in range(2)]
    ql_done, ql_out = shared.raised_by("blk_done", 2, 4), shared.raised_by("blk_evac", 2, 4)
    ropes, ropes_base = shared.plain("copied", 1)
    raw = [m["raw0"], m["raw1"]]
    with nc.Block() as block:
        @block.sync
        def _(sp):
            with sp.Fori(0, 2) as i:
                for k in range(2):
                    ql_done.wait_last_turn(sp, i, k)
                    sp.dma_start(raw[k][:], d["ukt_units"][bass.ds(2 * i + k, 1)].rearrange("a p n -> (a p) n")).then_inc(raw_in[k][0], 16)

        @block.tensor
        def _(pe):
            ql_done.open(pe)
            with pe.Fori(0, 2) as i:
                for k in range(2):
                    pe.wait_ge(raw_in[k][0], 16 * i + (raw_in[k][1] + 16))
                    ql_out.wait_last_turn(pe, i, k)
                    for hh in range(4):
                        for lb in range(LT):
                            last = nc.tensor.matmul(psum[6 + k][:, (hh * LT + lb) * N_SAMPLE:(hh * LT + lb + 1) * N_SAMPLE],
                                                    raw[k][:, hh * 512 + lb * P:hh * 512 + (lb + 1) * P],
                                                    m["qn"][:, bass.ds(8 * i + 4 * k + hh, 1), 0:N_SAMPLE].rearrange("p a t -> p (a t)"), start=True, stop=True)
                    last.then_inc(ql_done.sem, 1)

        @block.vector
        def _(dve):
            ql_out.open(dve)
            with dve.Fori(0, 2) as i:
                for k in range(2):
                    ql_done.wait(dve, i, k)
                    for hh in range(4):
                        src = psum[6 + k][:, hh * P:(hh + 1) * P].rearrange("p (l t) -> p l t", l=LT)
                        dst = m["q_lat"][:].rearrange("p l b (t h) -> p l (b t) h", h=MLA_HEADS)[:, :, :, bass.ds(8 * i + 4 * k + hh, 1)].rearrange("p l t a -> p l (t a)")
                        last = nc.vector.tensor_copy(dst, src)
                    last.then_inc(ql_out.sem, 1)
            for e in range(2):
                src = m["qr"][64 * e:64 * e + 64, :, 0:N_SAMPLE].rearrange("p h t -> p t h")
                dst = m["q_rs"][:].rearrange("p b (t h) -> p (b t) h", h=MLA_HEADS)[:, :, e:MLA_HEADS:2]
                last = nc.vector.tensor_copy(dst, src)
            nc.vector.tensor_copy(m["lat_s"][:], m["lat"][:, :, 0:N_SAMPLE])
            nc.vector.tensor_copy(m["kr_s"][:], m["kr"][0:ROPE, 0:N_SAMPLE])
            nc.vector.tensor_copy(m["rows_s"][:], m["rows_n"][0:N_SAMPLE, 0, 0:LATENT]).then_inc(ropes, 1)
            dve.wait_ge(ropes, ropes_base + 1)


def prompt_attention_stage(nc, ctx, m, psum, d):
    sem = lambda s: ctx.enter_context(nc.semaphore(f"pa_{s}"))
    sig = lambda s, per: Signal(sem(s), per)
    mask_in = sem("mask_in")
    kr_staged, q_staged, v_staged, k_staged = sig("kr_staged", 1), sig("q_staged", 2), sig("v_staged", 2), sig("k_staged", 2)
    k_turned, kr_turned, kt_out, krt_out = sig("k_turned", 2), sig("kr_turned", 1), sig("kt_out", 2), sig("krt_out", 1)
    s_done, s_out, mx_done, exp_done, p_done = sig("s_done", 4), sig("s_out", 4), sig("mx_done", 2), sig("exp_done", 2), sig("p_done", 2)
    pt_done, pt_out, o_done, o_out = sig("pt_done", 4), sig("pt_out", 4), sig("o_done", 2), sig("o_out", 2)
    v_step, passed = sem("dve"), sem("passed")
    two = lambda n: [m[f"{n}{e}"] for e in range(2)]
    q_s, k_s, v_s, k_t, s_, p_t, mx, sm = (two(n) for n in ("q_s", "k_s", "v_s", "k_t", "s", "p_t", "mx", "sum"))
    qr_s, kr_s, kr_t = m["qr_s"], m["kr_s2"], m["kr_t"]
    S_AT, S_N = (0, 48, 224), (48, 176, 304)
    KT_, KRT, SL, SH, PL, PH, O = psum[0], psum[1], psum[2], psum[3], psum[4], psum[5], psum[6]
    rows = lambda t: slice(0, TILE_N[t])
    toks = lambda t: slice(TILE_AT[t], TILE_AT[t + 1])
    flat = lambda ap: ap.rearrange("p a t -> p (a t)")
    with nc.Block() as block:
        @block.sync
        def _(sp):
            sp.dma_start(m["att_mask"][:], d["att_mask"]).then_inc(mask_in, 16)
            sp.wait_ge(mask_in, 16)

        @block.gpsimd
        def _(pool):
            for s in (v_staged, q_staged):
                s.open(pool)
            with pool.Fori(0, Q_PAIRS) as i:
                for e in range(2):
                    h = 2 * i + e
                    s_done.wait_last_turn(pool, i, 2 * e + 1)
                    if e == 0:
                        s_done.wait_last_turn(pool, i, 3)
                        nc.gpsimd.tensor_copy(qr_s[:], flat(m["qr"][:, bass.ds(i, 1), :]))
                    nc.gpsimd.tensor_copy(q_s[e][:], flat(m["qn"][:, bass.ds(h, 1), :])).then_inc(q_staged.sem, 1)
                    o_done.wait_last_turn(pool, i, e)
                    nc.gpsimd.tensor_copy(v_s[e][rows(0), 0, :], m["vn"][rows(0), 0, bass.ds(h * P, P)])
                    nc.gpsimd.tensor_copy(v_s[e][:, 1:3, :], m["vn"][:, 1:3, bass.ds(h * P, P)]).then_inc(v_staged.sem, 1)

        @block.tensor
        def _(pe):
            for s in (k_turned, kr_turned, s_done, pt_done, o_done):
                s.open(pe)
            with pe.Fori(0, Q_PAIRS) as i:
                def keys(e):
                    if e == 0:
                        kr_staged.wait(pe, i, 0)
                        krt_out.wait_last_turn(pe, i, 0)
                        for t in TILE_ORDER:
                            last = nc.tensor.transpose(KRT[:, toks(t)], kr_s[rows(t), t, :], m["ident"][rows(t), rows(t)])
                        last.then_inc(kr_turned.sem, 1)
                        kt_out.wait_last_turn(pe, i, 1)
                    else:
                        kt_out.wait(pe, i, 0)
                    k_staged.wait(pe, i, e)
                    for t in TILE_ORDER:
                        last = nc.tensor.transpose(KT_[:, toks(t)], k_s[e][rows(t), t, :], m["ident"][rows(t), rows(t)])
                    last.then_inc(k_turned.sem, 1)

                def scores(e):
                    if e == 0:
                        krt_out.wait(pe, i, 0)
                    kt_out.wait(pe, i, e)
                    q_staged.wait(pe, i, e)
                    half = slice(64 * e, 64 * e + 64)
                    for bank, tiles, at in ((SL, (1, 0), S_AT), (SH, (2,), (0, 0, 0))):
                        n = 2 * e + (bank is SH)
                        if n >= 2:
                            s_out.wait(pe, i, n - 2)
                        else:
                            s_out.wait_last_turn(pe, i, n + 2)
                        for t in tiles:
                            dst = bank[rows(t), at[t]:at[t] + S_N[t]]
                            nc.tensor.matmul(dst, q_s[e][:, toks(t)], k_t[e][:, 0:S_N[t]], start=True, stop=False)
                            last = nc.tensor.matmul(dst, qr_s[half, toks(t)], kr_t[half, 0:S_N[t]], start=False, stop=True)
                        last.then_inc(s_done.sem, 1)

                def turns(e):
                    p_done.wait(pe, i, e)
                    for bank, pairs, n in ((PH, ((1, 1, 0), (1, 2, 128), (2, 2, 256)), 2 * e), (PL, ((0, 1, 48), (0, 2, 176), (0, 0, 0)), 2 * e + 1)):
                        if n >= 2:
                            pt_out.wait(pe, i, n - 2)
                        else:
                            pt_out.wait_last_turn(pe, i, n + 2)
                        pe.sem_inc(passed, 1)
                        for kt, qt, at in pairs:
                            last = nc.tensor.transpose(bank[rows(kt), at:at + TILE_N[qt]],
                                                       s_[e][rows(qt), S_AT[qt] + TILE_AT[kt]:S_AT[qt] + TILE_AT[kt + 1]],
                                                       m["ident"][rows(qt), rows(qt)])
                        last.then_inc(pt_done.sem, 1)
                    v_staged.wait(pe, i, e)
                    pt_out.wait(pe, i, 2 * e)
                    pt_out.wait(pe, i, 2 * e + 1)
                    if e:
                        o_out.wait(pe, i, 0)
                    else:
                        o_out.wait_last_turn(pe, i, 1)
                    pt = p_t[e]
                    nc.tensor.matmul(O[:, 48:TOK], v_s[e][:, 1, :], pt[:, 304:560], start=True, stop=False)
                    nc.tensor.matmul(O[:, 176:TOK], v_s[e][:, 2, :], pt[:, 560:688], start=False, stop=False)
                    nc.tensor.matmul(O[:, 48:TOK], v_s[e][rows(0), 0, :], pt[rows(0), 48:304], start=False, stop=False)
                    nc.tensor.matmul(O[:, 0:48], v_s[e][rows(0), 0, :], pt[rows(0), 0:48], start=False, stop=True).then_inc(o_done.sem, 1)
                keys(0)
                scores(0)
                keys(1)
                scores(1)
                turns(0)
                turns(1)

        @block.scalar
        def _(act):
            for s in (kt_out, krt_out, exp_done, pt_out):
                s.open(act)
            with act.Fori(0, Q_PAIRS) as i:
                def keys(e):
                    if e == 0:
                        kr_turned.wait(act, i, 0)
                        s_done.wait_last_turn(act, i, 3)
                        nc.scalar.activation(kr_t[:], KRT[:, 0:TOK], ACT.Copy).then_inc(krt_out.sem, 1)
                    k_turned.wait(act, i, e)
                    s_done.wait_last_turn(act, i, 2 * e + 1)
                    nc.scalar.activation(k_t[e][:], KT_[:, 0:TOK], ACT.Copy).then_inc(kt_out.sem, 1)

                def exps(e):
                    mx_done.wait(act, i, e)
                    for t in range(3):
                        at = s_[e][rows(t), S_AT[t]:S_AT[t] + S_N[t]]
                        last = nc.scalar.activation(at, at, ACT.Exp, bias=mx[e][rows(t), t:t + 1], accum_out=sm[e][rows(t), t:t + 1])
                    last.then_inc(exp_done.sem, 1)

                def turned(e):
                    o_done.wait_last_turn(act, i, e)
                    pt_done.wait(act, i, 2 * e)
                    nc.scalar.activation(p_t[e][:, 304:688], PH[:, 0:384], ACT.Copy).then_inc(pt_out.sem, 1)
                    pt_done.wait(act, i, 2 * e + 1)
                    nc.scalar.activation(p_t[e][rows(0), 0:304], PL[rows(0), 0:304], ACT.Copy).then_inc(pt_out.sem, 1)
                keys(0)
                keys(1)
                exps(0)
                exps(1)
                turned(0)
                turned(1)

        @block.vector
        def _(dve):
            for s in (kr_staged, k_staged, s_out, mx_done, p_done, o_out):
                s.open(dve)
            v = Chain(dve, v_step)
            dve.wait_ge(mask_in, 16)
            with dve.Fori(0, Q_PAIRS) as i:
                v.turn(i, 4)

                def stage(e):
                    if e == 0:
                        kr_turned.wait_last_turn(dve, i, 0)
                        for t in range(3):
                            for ee in range(2):
                                last = nc.vector.tensor_scalar(kr_s[rows(t), t, 64 * ee:64 * ee + 64], m["rows_n"][rows(t), t, LATENT:ROW],
                                                               m["r_n"][rows(t), t, bass.ds(2 * i + ee, 1)], None, ALU.mult)
                        last.then_inc(kr_staged.sem, 1)
                    k_turned.wait_last_turn(dve, i, e)
                    for t in range(3):
                        last = nc.vector.tensor_scalar(k_s[e][rows(t), t, :], m["kn"][rows(t), t, bass.ds((2 * i + e) * P, P)],
                                                       m["r_n"][rows(t), t, bass.ds(2 * i + e, 1)], None, ALU.mult)
                    last.then_inc(k_staged.sem, 1)

                def masked(e):
                    pt_done.wait_last_turn(dve, i, 2 * e + 1)
                    for n, (bank, tiles, at) in enumerate(((SL, (1, 0), S_AT), (SH, (2,), (0, 0, 0)))):
                        s_done.wait(dve, i, 2 * e + n)
                        for t in tiles:
                            c = slice(S_AT[t], S_AT[t] + S_N[t])
                            last = nc.vector.tensor_tensor(s_[e][rows(t), c], bank[rows(t), at[t]:at[t] + S_N[t]], m["att_mask"][rows(t), c], ALU.add)
                        last.then_inc(s_out.sem, 1)
                    s_out.wait(dve, i, 2 * e + 1)
                    for t in range(3):
                        last = nc.vector.tensor_reduce(mx[e][rows(t), t:t + 1], s_[e][rows(t), S_AT[t]:S_AT[t] + S_N[t]], AX.X, ALU.max, negate=True)
                    last.then_inc(mx_done.sem, 1)

                def normed(e):
                    exp_done.wait(dve, i, e)
                    v(nc.vector.reciprocal(sm[e][rows(0), 0:1], sm[e][rows(0), 0:1]))
                    v(nc.vector.reciprocal(sm[e][:, 1:3], sm[e][:, 1:3]))
                    for t in range(3):
                        at = s_[e][rows(t), S_AT[t]:S_AT[t] + S_N[t]]
                        last = nc.vector.tensor_scalar(at, at, sm[e][rows(t), t:t + 1], None, ALU.mult)
                    last.then_inc(p_done.sem, 1)

                def gated(e):
                    o_done.wait(dve, i, e)
                    o = flat(m["o"][:, bass.ds(2 * i + e, 1), N_SAMPLE:TOK])
                    nc.vector.tensor_tensor(o, o, O[:, N_SAMPLE:TOK], ALU.mult).then_inc(o_out.sem, 1)
                stage(0)
                stage(1)
                masked(0)
                masked(1)
                normed(0)
                normed(1)
                gated(0)
                gated(1)
            v.end(Q_PAIRS)


def sample_attention_stage(nc, ctx, m, psum, d):
    sem = lambda s: ctx.enter_context(nc.semaphore(f"sa_{s}"))
    sig = lambda s, per: Signal(sem(s), per)
    uk_in, (tab_in, uk_hi_done, uk_lo_done) = [sem(f"uk_in{k}") for k in range(2)], [sem(s) for s in ("tab_in", "uk_hi", "uk_lo")]
    seq_in = [sem(f"seq_in{u}") for u in range(2)]
    t_done, t_hi, t_f32, kr_out, t_lo = (sig(s, PAGES) for s in ("t_done", "t_hi", "t_f32", "kr_out", "t_lo"))
    k_done, sq_out, red = (sig(s, 4 * PAGES) for s in ("k_done", "sq_out", "red"))
    s_done, sc_out, ss_done, q_staged = sig("s_done", PAGES), sig("sc_out", 2), sig("ss_done", 1), sig("q_staged", 1)
    r_done, r_turned, r_out, new_done, new_out = sig("r_done", 1), sig("r_turned", 2), sig("r_out", 2), sig("new_done", 1), sig("new_out", 1)
    s_max, s_exp, p_turned, p_out = sig("s_max", 1), sig("s_exp", 1), sig("p_turned", 2), sig("p_out", 2)
    o_done, o_scaled, o_turned, o_out = (sig(s, 1) for s in ("o_done", "o_scaled", "o_turned", "o_out"))
    v_step, a_step, passed = sem("dve"), sem("act"), sem("passed")
    past = m["past"]
    two = lambda n: [m[f"{n}{k}"] for k in range(2)]
    pt_hi, pt_lo, pt, pk, sc, sq = (two(n) for n in ("pt_hi", "pt_lo", "pt", "pk", "sc", "sq"))
    uk_hi, uk_lo = m["uk_hi"], m["uk_lo"]
    PT, PK, KN, SA, SB = psum[0], psum[1], psum[2:6], psum[6], psum[7]
    NEW = PAGES * P
    STEPS = 6
    stage = [past[:, 1].rearrange("p b c -> p (b c)")[:, k * UNIT:(k + 1) * UNIT] for k in range(2)]
    page_cols = lambda half: slice(half * 512, half * 512 + 512)
    LOOPS = DEC_BATCH // 2 - 1

    def sequences(eng, pages, step, chain=None, per=0):
        pages(0, 0, 0, False, True)
        with eng.Fori(0, LOOPS) as i:
            if chain:
                chain.turn(i, per)
            pages(2 * i + 1, 1, i, True, True)
            pages(2 * i + 2, 0, i + 1, True, True)
        if chain:
            chain.end(LOOPS)
        pages(DEC_BATCH - 1, 1, LOOPS, True, False)
        for k in range(STEPS):
            step(DEC_BATCH - 1, 1, k)

    def pages_back(signal, eng, s, k, n):
        if k >= n:
            signal.wait(eng, s, k - n)
        else:
            signal.wait_last_turn(eng, s, PAGES + k - n)
    with nc.Block() as block:
        @block.sync
        def _(sp):
            sp.dma_start(m["table"][:], d["table"]).then_inc(tab_in, 16)
            sp.dma_start(m["new_mask"][:], d["new_mask"]).then_inc(tab_in, 16)

            def load(s, u):
                for k in range(PAGES):
                    page = sp.value_load(m["table"][0:1, bass.ds(s * PAGES + k, 1)], min_val=0, max_val=d["cache"].shape[0] - 1)
                    sp.dma_start(past[:, u, k, :], d["cache"][bass.ds(page, 1)].rearrange("a p n -> (a p) n")).then_inc(seq_in[u], 16)
            for l in range(2):
                sp.dma_start(stage[l], d["kv_units"][l]).then_inc(uk_in[l], 16)
            sp.wait_ge(tab_in, 32)
            load(0, 0)
            for l in range(2, LT):
                sp.wait_ge(uk_lo_done, l - 1)
                sp.dma_start(stage[l % 2], d["kv_units"][l]).then_inc(uk_in[l % 2], 16)
            sp.wait_ge(uk_lo_done, LT)
            load(1, 1)
            with sp.Fori(0, LOOPS) as i:
                for u in range(2):
                    o_done.wait(sp, 2 * i + u, 0)
                    load(2 * i + 2 + u, u)

        @block.gpsimd
        def _(pool):
            t_lo.open(pool)
            with pool.Fori(0, DEC_BATCH) as s:
                for k in range(PAGES):
                    t_hi.wait(pool, s, k)
                    t_f32.wait(pool, s, k)
                    nc.gpsimd.tensor_tensor(pt_lo[k % 2][:], pt[k % 2][:], pt_hi[k % 2][:].bitcast(F32), ALU.subtract).then_inc(t_lo.sem, 1)

        @block.scalar
        def _(act):
            for l in range(LT):
                act.wait_ge(uk_in[l % 2], 16 * (l // 2 + 1))
                nc.scalar.activation(uk_hi[:, l].rearrange("p l n -> p (l n)"), stage[l % 2], ACT.Copy).then_inc(uk_hi_done, 1)
            for s in (t_hi, kr_out, sq_out, r_done, s_exp, p_out):
                s.open(act)
            c = Chain(act, a_step)

            def split(s, k):
                t_done.wait(act, s, k)
                pages_back(s_done, act, s, k, 2)
                nc.scalar.activation(pt_hi[k % 2][:], PT[:, :], ACT.Copy).then_inc(t_hi.sem, 1)
                nc.scalar.activation(pk[k % 2][:], PK[0:ROPE, 0:P], ACT.Copy).then_inc(kr_out.sem, 1)

            def squares(s, k):
                for c4 in range(4):
                    k_done.wait(act, s, 4 * k + c4)
                    if 4 * k + c4 >= 2:
                        red.wait(act, s, 4 * k + c4 - 2)
                    else:
                        red.wait_last_turn(act, s, 4 * PAGES + c4 - 2)
                    nc.scalar.activation(sq[c4 % 2][:], KN[c4][:, :], ACT.Square).then_inc(sq_out.sem, 1)

            def rms(s):
                ss_done.wait(act, s, 0)
                c(nc.scalar.activation(m["ss"][:], m["ss"][:], ACT.Ln, bias=m["eps"][:, 0:1], scale=1.0 / QK))
                r_turned.wait_last_turn(act, s, 1)
                for t in range(DEC_SEQ):
                    last = nc.scalar.activation(m["r4"][:, :, t, :], m["ss"][:], ACT.Exp, scale=-0.5)
                last.then_inc(r_done.sem, 1)

            def step(s, u, k):
                if k == 1:
                    s_max.wait(act, s, 0)
                    nc.scalar.activation(sc[u][:], sc[u][:], ACT.Exp, bias=m["smx"][:, 0:1], accum_out=m["smx"][:, 1:2]).then_inc(s_exp.sem, 1)
                if k == 2:
                    p_turned.wait(act, s, 0)
                    o_done.wait_last_turn(act, s, 0)
                    nc.scalar.activation(m["pst"][:, 0:PAGES, :].rearrange("p k q -> p (k q)"), SB[:, :], ACT.Copy).then_inc(p_out.sem, 1)
                if k == 3:
                    p_turned.wait(act, s, 1)
                    nc.scalar.activation(m["pst"][0:N_SAMPLE, PAGES, :], SB[0:N_SAMPLE, 0:QROWS], ACT.Copy).then_inc(p_out.sem, 1)

            def pages(s, u, nth, before, after):
                for k in range(PAGES):
                    if k + 1 < PAGES:
                        split(s, k + 1)
                    elif after:
                        split(s + 1, 0)
                    squares(s, k)
                    if before and k < STEPS:
                        step(s - 1, 1 - u, k)
                rms(s)
            split(0, 0)
            sequences(act, pages, step, c, 2)

        @block.tensor
        def _(pe):
            for s in (t_done, k_done, s_done, r_turned, new_done, p_turned, o_done, o_turned):
                s.open(pe)

            def turn_page(s, u, nth, k):
                if k == 0:
                    pe.wait_ge(seq_in[u], 16 * PAGES * nth + 16 * PAGES)
                for s_ in (t_f32, t_hi, kr_out):
                    pages_back(s_, pe, s, k, 1)
                for l in range(LT):
                    nc.tensor.transpose(PT[:, l * P:(l + 1) * P], past[:, u, k, l * P:(l + 1) * P], m["ident"][:])
                nc.tensor.transpose(PK[0:ROPE, 0:P], past[:, u, k, LATENT:ROW], m["ident"][:]).then_inc(t_done.sem, 1)

            def keys(s, k):
                t_lo.wait(pe, s, k)
                for c4 in range(4):
                    if k:
                        sq_out.wait(pe, s, 4 * (k - 1) + c4)
                    else:
                        sq_out.wait_last_turn(pe, s, 4 * (PAGES - 1) + c4)
                    for l in range(LT):
                        a = slice(l * P, (l + 1) * P)
                        last = mm3(nc, KN[c4][:, :], (pt_hi[k % 2][:, a], pt_lo[k % 2][:, a]), (uk_hi[:, c4, l, :], uk_lo[:, c4, l, :]), l == 0, l == LT - 1)
                    last.then_inc(k_done.sem, 1)

            def scores(s, k):
                if k == 0:
                    q_staged.wait(pe, s, 0)
                    sc_out.wait_last_turn(pe, s, 1)
                if k == 4:
                    sc_out.wait(pe, s, 0)
                kr_out.wait(pe, s, k)
                dst = SA[0:QROWS, k % 4 * P:(k % 4 + 1) * P]
                for l in range(LT):
                    nc.tensor.matmul(dst, m["q_ls"][:, l, :], pt[k % 2][:, l * P:(l + 1) * P], start=l == 0, stop=False)
                nc.tensor.matmul(dst, m["q_rss"][:], pk[k % 2][:], start=False, stop=True).then_inc(s_done.sem, 1)

            def new_scores(s):
                o_out.wait_last_turn(pe, s, 0)
                dst = SB[0:QROWS, 0:N_SAMPLE]
                for l in range(LT):
                    nc.tensor.matmul(dst, m["q_ls"][:, l, :], m["lat_s"][:, l, :], start=l == 0, stop=False)
                nc.tensor.matmul(dst, m["q_rss"][:], m["kr_s"][:], start=False, stop=True).then_inc(new_done.sem, 1)

            def step(s, u, k):
                if k < 2:
                    if k == 0:
                        r_done.wait(pe, s, 0)
                        new_out.wait(pe, s, 0)
                    else:
                        r_out.wait(pe, s, 0)
                    pe.sem_inc(passed, 1)
                    for n in range(4):
                        last = nc.tensor.transpose(SB[0:QROWS, n * P:(n + 1) * P], m["r4"][:, 4 * k + n].rearrange("p t h -> p (t h)"), m["ident"][:])
                    last.then_inc(r_turned.sem, 1)
                if k == 2:
                    s_exp.wait(pe, s, 0)
                    pe.sem_inc(passed, 1)
                    for n in range(PAGES):
                        last = nc.tensor.transpose(SB[:, n * QROWS:(n + 1) * QROWS], sc[u][:, n * P:(n + 1) * P], m["ident"][0:QROWS, 0:QROWS])
                    last.then_inc(p_turned.sem, 1)
                if k == 3:
                    p_out.wait(pe, s, 0)
                    pe.sem_inc(passed, 1)
                    nc.tensor.transpose(SB[0:N_SAMPLE, 0:QROWS], sc[u][:, NEW:NEW + N_SAMPLE], m["ident"][0:QROWS, 0:QROWS]).then_inc(p_turned.sem, 1)
                if k == 4:
                    p_out.wait(pe, s, 1)
                    for n in range(PAGES):
                        nc.tensor.matmul(SB[0:QROWS, :], m["pst"][:, n, :], past[:, u, n, 0:LATENT], start=n == 0, stop=False)
                    nc.tensor.matmul(SB[0:QROWS, :], m["pst"][0:N_SAMPLE, PAGES, :], m["rows_s"][:], start=False, stop=True).then_inc(o_done.sem, 1)
                if k == 5:
                    o_scaled.wait(pe, s, 0)
                    pe.sem_inc(passed, 1)
                    for l in range(LT):
                        last = nc.tensor.transpose(SB[:, l * QROWS:(l + 1) * QROWS], m["o_s"][:, l * P:(l + 1) * P], m["ident"][0:QROWS, 0:QROWS])
                    last.then_inc(o_turned.sem, 1)

            def pages(s, u, nth, before, after):
                for k in range(PAGES):
                    if k + 1 < PAGES:
                        turn_page(s, u, nth, k + 1)
                    elif after:
                        turn_page(s + 1, 1 - u, nth + u, 0)
                    keys(s, k)
                    scores(s, k)
                    if before and k < STEPS:
                        step(s - 1, 1 - u, k)
                    if k == STEPS:
                        new_scores(s)
            turn_page(0, 0, 0, 0)
            pe.wait_ge(uk_lo_done, LT)
            sequences(pe, pages, step)

        @block.vector
        def _(dve):
            for l in range(LT):
                dve.wait_ge(uk_hi_done, l + 1)
                nc.vector.tensor_tensor(uk_lo[:, l].rearrange("p l n -> p (l n)"), stage[l % 2], uk_hi[:, l].bitcast(F32).rearrange("p l n -> p (l n)"), ALU.subtract).then_inc(uk_lo_done, 1)
            for s in (t_f32, red, q_staged, sc_out, ss_done, r_out, new_out, s_max, o_scaled, o_out):
                s.open(dve)
            v = Chain(dve, v_step)
            dve.wait_ge(tab_in, 32)

            def turned(s, k):
                t_done.wait(dve, s, k)
                t_hi.wait(dve, s, k)
                pages_back(s_done, dve, s, k, 2)
                nc.vector.tensor_copy(pt[k % 2][:], PT[:, :]).then_inc(t_f32.sem, 1)

            def start(s, u, nth):
                s_done.wait_last_turn(dve, s, PAGES - 1)
                nc.vector.tensor_copy(m["q_ls"][:], m["q_lat"][:, :, bass.ds(s, 1), :].rearrange("p l a q -> p l (a q)"))
                nc.vector.tensor_copy(m["q_rss"][:], m["q_rs"][:, bass.ds(s, 1), :].rearrange("p a q -> p (a q)")).then_inc(q_staged.sem, 1)
                dve.wait_ge(seq_in[u], 16 * PAGES * nth + 16 * PAGES)
                ss_done.wait_last_turn(dve, s, 0)
                kr, tmp = past[:, u, :, LATENT:ROW], m["kr_sq"][:]
                v(nc.vector.tensor_tensor(tmp, kr, kr, ALU.mult))
                v(nc.vector.tensor_reduce(m["ssr"][:], tmp, AX.X, ALU.add))

            def reduces(s, k):
                for c4 in range(4):
                    sq_out.wait(dve, s, 4 * k + c4)
                    if k == 0 and c4 == 0:
                        r_done.wait_last_turn(dve, s, 0)
                    nc.vector.tensor_reduce(m["ss"][:, k, 4 * c4:4 * c4 + 4], sq[c4 % 2][:].rearrange("p (h d) -> p h d", h=4), AX.X, ALU.add).then_inc(red.sem, 1)

            def step(s, u, k):
                if k < 2:
                    r_turned.wait(dve, s, k)
                    sc_out.wait(dve, s, k)
                    at = sc[u][:, page_cols(k)]
                    nc.vector.tensor_tensor(at, at, SB[0:QROWS, :], ALU.mult).then_inc(r_out.sem, 1)
                if k == 1:
                    r_out.wait(dve, s, 1)
                    new_out.wait(dve, s, 0)
                    nc.vector.tensor_reduce(m["smx"][:, 0:1], sc[u][:], AX.X, ALU.max, negate=True).then_inc(s_max.sem, 1)
                if k == 4:
                    s_exp.wait(dve, s, 0)
                    v(nc.vector.reciprocal(m["smx"][:, 1:2], m["smx"][:, 1:2]))
                    o_done.wait(dve, s, 0)
                    o_turned.wait_last_turn(dve, s, 0)
                    nc.vector.tensor_scalar(m["o_s"][:], SB[0:QROWS, :], m["smx"][:, 1:2], None, ALU.mult).then_inc(o_scaled.sem, 1)
                if k == 5:
                    o_turned.wait(dve, s, 0)
                    for l in range(LT):
                        dst = m["o_lat"][:, l].rearrange("p h (b t) -> p b t h", t=DEC_SEQ)[:, bass.ds(s, 1)].rearrange("p a t h -> p (a t) h")
                        last = nc.vector.tensor_copy(dst, SB[:, l * QROWS:(l + 1) * QROWS].rearrange("p (t h) -> p t h", h=MLA_HEADS))
                    last.then_inc(o_out.sem, 1)

            def new_scored(s, u):
                new_done.wait(dve, s, 0)
                at = sc[u][:, NEW:NEW + N_SAMPLE]
                v(nc.vector.tensor_tensor(at, SB[0:QROWS, 0:N_SAMPLE], m["r_new"][:], ALU.mult))
                nc.vector.tensor_tensor(at, at, m["new_mask"][:, bass.ds(s, 1), :].rearrange("p a t -> p (a t)"), ALU.add).then_inc(new_out.sem, 1)

            def pages(s, u, nth, before, after):
                for k in range(PAGES):
                    if k + 1 < PAGES:
                        turned(s, k + 1)
                    elif after:
                        turned(s + 1, 0)
                    if k == 0:
                        start(s, u, nth)
                    reduces(s, k)
                    if k in (3, 7):
                        s_done.wait(dve, s, k)
                        nc.vector.tensor_copy(sc[u][:, page_cols(k // 4)], SA[0:QROWS, :]).then_inc(sc_out.sem, 1)
                    if before and k < STEPS:
                        step(s - 1, 1 - u, k)
                    if k == STEPS:
                        new_scored(s, u)
                red.wait(dve, s, 4 * PAGES - 1)
                nc.vector.tensor_tensor(m["ss"][:], m["ss"][:], m["ssr"][:].rearrange("p (k a) -> p k a", a=1).to_broadcast([P, PAGES, MLA_HEADS]), ALU.add).then_inc(ss_done.sem, 1)
            turned(0, 0)
            sequences(dve, pages, step, v, 2 * 4)


def sample_value_stage(nc, shared, m, psum, d):
    raw_in = [shared.plain(f"raw_in{k}", 16 * 2) for k in range(2)]
    v_done, v_out = shared.raised_by("blk_done", 2, 4), shared.raised_by("blk_evac", 2, 4)
    (high, high_base), (low, low_base) = shared.plain("hi_done", 4), shared.plain("lo_done", 4)
    raw = [m["raw0"], m["raw1"]]
    with nc.Block() as block:
        @block.sync
        def _(sp):
            with sp.Fori(0, 2) as i:
                for k in range(2):
                    v_done.wait_last_turn(sp, i, k)
                    sp.dma_start(raw[k][:], d["kv_units"][bass.ds(2 * i + k + 4, 1)].rearrange("a p n -> (a p) n")).then_inc(raw_in[k][0], 16)

        @block.tensor
        def _(pe):
            v_done.open(pe)
            with pe.Fori(0, 2) as i:
                for k in range(2):
                    pe.wait_ge(raw_in[k][0], 16 * i + (raw_in[k][1] + 16))
                    v_out.wait_last_turn(pe, i, k)
                    for hh in range(4):
                        for l in range(LT):
                            last = nc.tensor.matmul(psum[k][:, hh * N_SAMPLE:(hh + 1) * N_SAMPLE], raw[k][:, l * 512 + hh * P:l * 512 + (hh + 1) * P],
                                                    m["o_lat"][:, l, bass.ds(8 * i + 4 * k + hh, 1), :].rearrange("p a t -> p (a t)"), start=l == 0, stop=l == LT - 1)
                    last.then_inc(v_done.sem, 1)

        @block.vector
        def _(dve):
            v_out.open(dve)
            with dve.Fori(0, 2) as i:
                for k in range(2):
                    v_done.wait(dve, i, k)
                    o = m["o"][:, bass.ds(8 * i + 4 * k, 4), 0:N_SAMPLE]
                    nc.vector.tensor_tensor(o, o, psum[k][:, 0:4 * N_SAMPLE].rearrange("p (h t) -> p h t", h=4), ALU.mult).then_inc(v_out.sem, 1)
            for h in range(4):
                c = slice(4 * h, 4 * h + 4)
                dve.wait_ge(high, high_base + h + 1)
                nc.vector.tensor_tensor(m["h_lo"][:, c, :], m["o"][:, c, :], m["h_hi"][:, c, :].bitcast(F32), ALU.subtract).then_inc(low, 1)
            dve.wait_ge(low, low_base + 4)

        @block.scalar
        def _(act):
            v_out.wait(act, 1, 1)
            for h in range(4):
                c = slice(4 * h, 4 * h + 4)
                nc.scalar.activation(m["h_hi"][:, c, :], m["o"][:, c, :], ACT.Copy).then_inc(high, 1)


def store_stage(nc, ctx, m, d):
    stored = ctx.enter_context(nc.semaphore("y_stored"))
    with nc.Block() as block:
        @block.sync
        def _(sp):
            sp.dma_start(d["y_out"], m["x"][:]).then_inc(stored, 16)
            sp.wait_ge(stored, 16)


def load_mla_consts(nc, ctx, m, d):
    loaded = ctx.enter_context(nc.semaphore("mla_loaded"))
    names = ("rot", "half", "cos", "sin", "mla_gain", "qk_gain")
    with nc.Block() as block:
        @block.sync
        def _(sp):
            for name in names:
                sp.dma_start(m[name][:], d[name]).then_inc(loaded, 16)
            sp.wait_ge(loaded, 16 * len(names))


def build(nc, d):
    from contextlib import ExitStack
    with ExitStack() as ctx:
        m = memory(nc)
        psum = [ctx.enter_context(nc.psum_tensor(f"bank{i}", [P, 512], F32)) for i in range(8)]
        norms, latents, dense = (Shared(nc, ctx, kind) for kind in ("norm", "latent", "dense"))
        load_stage(nc, ctx, m, d)
        norm_stage(nc, norms, m, psum, 0)
        dt_stage(nc, ctx, m, psum, d)
        mamba_stage(nc, ctx, m, psum, d)
        memory_mla(nc, m)
        load_mla_consts(nc, ctx, m, d)
        flat = lambda ap: ap.rearrange("p a t -> p (a t)")
        h = lambda j: (m["h_hi"][:, j, :], m["h_lo"][:, j, :])
        norm_stage(nc, norms, m, psum, 1)
        dense_stage(nc, dense, m, psum, d["kva_units"], LT, 1, h,
                    lambda c, bank: nc.vector.tensor_copy(flat(m["lat"][:, bass.ds(c, 1), :]), bank[:, 0:TOK]))
        dense_stage(nc, dense, m, psum, d["kvr_unit"], 1, 1, h,
                    lambda c, bank: nc.vector.tensor_copy(m["kr"][:], bank[:, 0:TOK]))
        latent_norm(nc, latents, m, psum, m["lat"], m["mla_gain"][:, 0, :], m["lat_hi"], m["lat_lo"])
        rows_stage(nc, ctx, m, psum, d)
        norm_stage(nc, norms, m, psum, 2)
        dense_stage(nc, dense, m, psum, d["qa_units"], LT, 1, h,
                    lambda c, bank: nc.vector.tensor_copy(flat(m["qa"][:, bass.ds(c, 1), :]), bank[:, 0:TOK]))
        dense_stage(nc, dense, m, psum, d["gate_units"], MLA_HEADS, 1, h,
                    lambda c, bank: nc.vector.tensor_copy(flat(m["o"][:, bass.ds(c, 1), :]), bank[:, 0:TOK]))
        latent_norm(nc, latents, m, psum, m["qa"], m["mla_gain"][:, 1, :], m["qa_hi"], m["qa_lo"])
        qa = lambda j: (m["qa_hi"][:, j, :], m["qa_lo"][:, j, :])
        dense_stage(nc, dense, m, psum, d["qn_units"], 4, 4, qa,
                    lambda c, bank: nc.vector.tensor_copy(flat(m["qn"][:, bass.ds(c, 1), :]), bank[:, 0:TOK]))
        dense_stage(nc, dense, m, psum, d["qr_units"], 2, 4, qa,
                    lambda c, bank: nc.vector.tensor_copy(flat(m["qr"][:, bass.ds(c, 1), :]), bank[:, 0:TOK]))
        query_stage(nc, ctx, m, psum)
        key_stage(nc, dense, m, psum, d)
        key_rms_stage(nc, ctx, m, psum)
        prompt_attention_stage(nc, ctx, m, psum, d)
        q_lat_stage(nc, dense, m, psum, d)
        sample_attention_stage(nc, ctx, m, psum, d)
        sample_value_stage(nc, dense, m, psum, d)
        dense_stage(nc, dense, m, psum, d["o_units"], KT, 1, h,
                    lambda c, bank: nc.vector.tensor_tensor(flat(m["x"][:, bass.ds(c, 1), :]), flat(m["x"][:, bass.ds(c, 1), :]), bank[:, 0:TOK], ALU.add))
        store_stage(nc, ctx, m, d)


def tables():
    mask = np.zeros((P, PAIR_N), np.float32)
    col = np.arange(TOK)
    for t in range(3):
        j = TILE_AT[t] + np.arange(TILE_N[t])[:, None]
        i = col[None, TILE_AT[t]:]
        sample = (j < N_SAMPLE) & (i < N_SAMPLE) & (i // DEC_SEQ == j // DEC_SEQ) & (j <= i)
        prompt = (j >= N_SAMPLE) & (i >= N_SAMPLE) & (j <= i)
        mask[:TILE_N[t], PAIR_AT[t]:PAIR_AT[t + 1]] = sample | prompt
    diag = (np.arange(N_SAMPLE)[:, None] // DEC_SEQ == np.arange(DEC_BATCH)[None]).astype(np.float32)
    rot = np.zeros((P, P), np.float32)
    for at in (0, ROPE):
        for c in range(ROPE // 2):
            rot[at + ROPE // 2 + c, at + c] = -1.0
            rot[at + c, at + ROPE // 2 + c] = 1.0
    half = np.zeros((P, 2, P), np.float32)
    half[:ROPE, 0] = 1.0
    half[ROPE:, 1] = 1.0
    pos = np.concatenate([np.tile(PAGES * P + np.arange(DEC_SEQ), DEC_BATCH), np.arange(T_PROMPT)]).astype(np.float32)
    inv = (1.0 / (np.float32(10000.0) ** (np.arange(0, ROPE, 2, dtype=np.float32) / ROPE))).astype(np.float32)
    angle = np.tile((pos[:, None] * inv[None, :]).T, (4, 1))
    none = np.float32(-1e30)
    att = np.full((P, 528), none, np.float32)
    for t, at, n in ((0, 0, 48), (1, 48, 176), (2, 224, 304)):
        q, k = TILE_AT[t] + np.arange(TILE_N[t])[:, None], np.arange(n)[None]
        att[:TILE_N[t], at:at + n] = np.where((k >= N_SAMPLE) & (k <= q), np.float32(0), none)
    q, b, k = np.arange(QROWS)[:, None, None] // MLA_HEADS, np.arange(DEC_BATCH)[None, :, None], np.arange(N_SAMPLE)[None, None]
    new = np.where((k // DEC_SEQ == b) & (k % DEC_SEQ <= q), np.float32(0), none).astype(np.float32)
    return {"rot": rot, "half": half, "cos": np.cos(angle).astype(np.float32), "sin": np.sin(angle).astype(np.float32), "att_mask": att, "new_mask": new, "ident": np.eye(P, dtype=np.float32), "ones": np.ones((P, P), np.float32), "eps": np.full((P, 1), EPS, np.float32),
            "mask": mask, "diag": diag}


def lay_out(inp):
    a = {k: np.asarray(v) for k, v in inp.items()}
    blocks = lambda v: v.reshape(-1, P).T
    d = dict(tables())
    x = np.concatenate([a["x_sample"].reshape(N_SAMPLE, D_MODEL), a["meta_tokens"], a["x_prompt"][0]], 0)
    d["x"] = x.T.reshape(KT, P, TOK).transpose(1, 0, 2)
    d["norms"] = np.stack([blocks(a["a_norm"][0]), blocks(a["kv_norm"]), blocks(a["b_norm"][0])], 1)
    w = a["a_w_in"][0]
    d["narrow"] = w[:, D_INNER + 6144:].reshape(KT, P, HD).transpose(1, 0, 2).reshape(P, KT * HD)
    tile = lambda cols: cols.reshape(KT, P, P).transpose(1, 0, 2).reshape(P, UNIT)
    units, outs = [], [np.zeros((P, UNIT), np.float32)] * OUT_UNITS
    for g in range(GROUPS):
        at = [D_INNER + g * GW + p * P for p in range(PAIRS)] + [2 * D_INNER + g * P, 2 * D_INNER + 1024 + g * P] + [g * GW + p * P for p in range(PAIRS)]
        units += [tile(w[:, c:c + P]) for c in at]
        units += outs
        rows = a["a_w_out"][0][g * GW:(g + 1) * GW].reshape(PAIRS, P, OUT_UNITS, 4, P)
        outs = [rows[:, :, k].transpose(1, 2, 0, 3).reshape(P, UNIT) for k in range(OUT_UNITS)]
    units += outs
    d["a_units"] = np.stack(units)

    def conv_order(v):
        v = v.reshape(v.shape[:-1] + (48, P))
        order = [[4 * g + p for p in range(PAIRS)] + [32 + g, 40 + g] for g in range(GROUPS)]
        v = v[..., np.array(order), :]
        return np.moveaxis(np.moveaxis(v, -1, 0), (-2, -1), (1, 2))
    d["conv_w"] = conv_order(a["a_conv_w"][0])
    d["conv_b"] = conv_order(a["a_conv_b"][0])
    d["conv_old"] = conv_order(a["state_conv"][0])
    d["d_skip"] = blocks(np.repeat(a["a_D"][0], HD)).reshape(P, GROUPS, PAIRS)
    d["gate_norm"] = blocks(a["a_gate_norm"][0]).reshape(P, GROUPS, PAIRS)
    d["dt_bias"] = a["a_dt_bias"][0][:, None]
    d["a_log"] = a["a_A_log"][0][:, None]
    two = lambda v: np.concatenate([v, v])
    d["mla_gain"] = np.stack([blocks(a["kv_a_norm"]), blocks(a["b_q_a_norm"][0])], 1)
    qg, kg = a["b_q_norm"][0], a["k_norm"]
    d["qk_gain"] = np.stack([qg[:NOPE], kg[:NOPE], two(qg[NOPE:]), two(kg[NOPE:])], 1)
    kva = a["w_kv_a"]
    d["kva_units"] = np.stack([tile(kva[:, k * P:(k + 1) * P]) for k in range(LT)])
    d["kvr_unit"] = tile(np.concatenate([kva[:, LATENT:]] * 2, 1))[None]
    w = a["b_w_in"][0]
    d["qa_units"] = np.stack([tile(w[:, k * P:(k + 1) * P]) for k in range(LT)])
    d["gate_units"] = np.stack([tile(w[:, LATENT + k * P:LATENT + (k + 1) * P]) for k in range(MLA_HEADS)])
    wq = a["b_w_q"][0].reshape(LT, P, MLA_HEADS, QK)

    def quads(blk):
        return blk.transpose(2, 1, 0, 3).reshape(-1, 4, P, LT * P).transpose(0, 2, 1, 3).reshape(-1, P, UNIT)
    d["qn_units"] = quads(wq[..., :NOPE])
    d["qr_units"] = quads(wq[..., NOPE:].reshape(LT, P, Q_PAIRS, P))
    kv = [a[n].reshape(LT, P, 4, 512).transpose(2, 1, 0, 3).reshape(4, P, UNIT) for n in ("w_uk", "w_uv")]
    d["kv_units"] = np.concatenate(kv)
    d["ukt_units"] = a["w_uk"].transpose(1, 2, 0).reshape(4, 4, P, LATENT).transpose(0, 2, 1, 3).reshape(4, P, UNIT)
    d["o_units"] = np.stack([tile(a["b_w_out"][0][:, k * P:(k + 1) * P]) for k in range(KT)])
    d["cache"] = a["cache_kv"]
    d["table"] = a["page_table"].reshape(1, -1)
    d["state_in"] = a["state_ssm"][0].reshape(DEC_BATCH, D_INNER, STATE)
    return {k: np.ascontiguousarray(v) for k, v in d.items()}


OUTS = {"state_out": (DEC_BATCH, D_INNER, STATE), "sp_out": (GROUPS, P, PAIRS, STATE),
        "conv_out": (P, GROUPS, CONV_BLK, DEC_BATCH + 1, 3), "y_out": (P, KT, TOK), "kv_out": (TOK, 576)}


def kernel(**inputs):
    import concourse.bacc as bacc
    from concourse.bass_utils import run_bass_kernel_spmd as run

    nc = bacc.Bacc("TRN2", target_bir_lowering=False, num_devices=1)
    arrays = {f"in_{k}": v for k, v in lay_out(inputs).items()}
    d = {k[3:]: nc.dram_tensor(k, v.shape, mybir.dt.from_np(v.dtype), kind="ExternalInput").ap() for k, v in arrays.items()}
    for k, shape in OUTS.items():
        d[k] = nc.dram_tensor(f"out_{k}", shape, F32, kind="ExternalOutput").ap()
    build(nc, d)
    r = run(nc, [arrays], core_ids=[0]).results[0]
    got = {k: r[f"out_{k}"] for k in OUTS}
    y = got["y_out"].transpose(1, 0, 2).reshape(D_MODEL, TOK).T
    conv = got["conv_out"]
    back = np.empty((9, 3, 48, P), np.float32)
    for g in range(GROUPS):
        for k, blk in enumerate([4 * g + p for p in range(PAIRS)] + [32 + g, 40 + g]):
            back[:, :, blk] = conv[:, g, k].transpose(1, 2, 0)
    back = back.reshape(9, 3, 6144)
    sp = got["sp_out"].transpose(0, 2, 1, 3).reshape(1, 1, HEADS, HD, STATE)
    kv = got["kv_out"]
    return (y[N_SAMPLE + N_META:][None], y[:N_SAMPLE].reshape(DEC_BATCH, DEC_SEQ, D_MODEL), sp, back[8][None, None],
            kv[N_SAMPLE:][None], got["state_out"].reshape(1, DEC_BATCH, HEADS, HD, STATE), back[:8][None],
            kv[:N_SAMPLE].reshape(DEC_BATCH, DEC_SEQ, 576))
```
